# Optimizing a Trainium2 kernel written in Bass

```python
import jax, jax.numpy as jnp
from jax import lax
import numpy as np
import math
import jax
import jax.numpy as jnp

D_MODEL = 1024
BATCH = 1
SEQ = 512
DEPTH = 2

GRID_W = 64
CTX_LEN = 256
N_MIXERS = 2
D_FF = 4 * D_MODEL
CONV_W = 3
ML_HEADS = 8
ML_DV = D_MODEL // ML_HEADS
ML_DQK = ML_DV // 2
ML_QK_COLS = 2 * ML_HEADS * ML_DQK
ML_QKV_COLS = ML_QK_COLS + ML_HEADS * ML_DV
ML_PROJ_COLS = ML_QKV_COLS + ML_HEADS * ML_DV
ML_CHUNK = 128
EPS = 1e-6
N_CONV_LAYERS = (DEPTH + N_MIXERS - 1) // N_MIXERS
N_MLSTM_LAYERS = DEPTH // N_MIXERS


def _rmsnorm(x, w):
    x32 = x.astype(jnp.float32)
    y = x32 * lax.rsqrt(jnp.mean(x32 * x32, axis=-1, keepdims=True) + EPS)
    return y.astype(x.dtype) * w

def _modulate(h, shift, scale):
    return h * (1 + scale) + shift

def _dwconv_centred(u, w, axis):
    n = u.shape[axis]
    half = CONV_W // 2
    pad = [(0, 0)] * u.ndim
    pad[axis] = (half, CONV_W - 1 - half)
    up = jnp.pad(u, pad)
    out = w[0] * lax.slice_in_dim(up, 0, n, axis=axis)
    for j in range(1, CONV_W):
        out = out + w[j] * lax.slice_in_dim(up, j, j + n, axis=axis)
    return out

def _short_conv_mixer(h, w_in, conv_w, w_out, rows):
    bsz, t_len, d = h.shape
    b_gate, c_gate, u = jnp.split(h @ w_in, 3, axis=-1)
    u = c_gate * u
    if rows is None:
        y = _dwconv_centred(u, conv_w, axis=1)
    else:
        y = _dwconv_centred(u.reshape(bsz, rows, GRID_W, d), conv_w, axis=2).reshape(bsz, t_len, d)
    return (b_gate * y) @ w_out

def _sqrelu_mlp(h, w1, w2):
    return jnp.square(jax.nn.relu(h @ w1)) @ w2

def _mlstm_inputs(h, w_qkvo, w_if, b_if, with_o):
    bsz, t_len, _ = h.shape
    p = h @ (w_qkvo if with_o else w_qkvo[:, :ML_QKV_COLS])
    q = p[..., :ML_HEADS * ML_DQK]
    k = p[..., ML_HEADS * ML_DQK:ML_QK_COLS]
    v = p[..., ML_QK_COLS:ML_QKV_COLS]
    o = p[..., ML_QKV_COLS:] if with_o else None

    def heads(a, dh):
        return a.reshape(bsz, t_len, ML_HEADS, dh).transpose(0, 2, 1, 3).astype(jnp.float32)

    q = heads(q, ML_DQK) * (ML_DQK ** -0.5)
    k = heads(k, ML_DQK)
    v = heads(v, ML_DV)
    g = (jnp.einsum('btd,rdg->rbgt', h, w_if) + b_if[:, None, :, None]).astype(jnp.float32)
    ig = g[:, :, :ML_HEADS]
    lf = jax.nn.log_sigmoid(g[:, :, ML_HEADS:])
    return q, k, v, o, ig, lf

def _mlstm_scan(q, k, v, ig, lf, state, with_output):
    bsz, nh, t_len, _ = q.shape
    dv = v.shape[-1]
    nc = t_len // ML_CHUNK

    def chunks(a):
        a = a.reshape(a.shape[:2] + (nc, ML_CHUNK) + a.shape[3:])
        return jnp.moveaxis(a, 2, 0)

    xs = (chunks(q), chunks(k), chunks(v), chunks(ig), chunks(lf))
    tri = jnp.tril(jnp.ones((ML_CHUNK, ML_CHUNK), dtype=bool))

    def body(carry, inp):
        c_mat, n_vec, m = carry
        qc, kc, vc, ic, fc = inp
        b = jnp.cumsum(fc, axis=-1)
        out = None
        if with_output:
            logd = b[..., :, None] - b[..., None, :] + ic[..., None, :]
            logd = jnp.where(tri, logd, -jnp.inf)
            inter = b + m[..., None]
            m_t = jnp.maximum(inter, jnp.max(logd, axis=-1))
            s = jnp.einsum('bhtd,bhsd->bhts', qc, kc) * jnp.exp(logd - m_t[..., None])
            w_inter = jnp.exp(inter - m_t)
            num = jnp.einsum('bhts,bhsv->bhtv', s, vc) + w_inter[..., None] * jnp.einsum('bhtd,bhdv->bhtv', qc, c_mat)
            den = jnp.sum(s, axis=-1) + w_inter * jnp.einsum('bhtd,bhd->bht', qc, n_vec)
            out = num / jnp.maximum(jnp.abs(den), jnp.exp(-m_t))[..., None]
        b_last = b[..., -1]
        dec = b_last[..., None] - b + ic
        m_new = jnp.maximum(b_last + m, jnp.max(dec, axis=-1))
        wk = jnp.exp(dec - m_new[..., None])
        a = jnp.exp(b_last + m - m_new)
        c_new = a[..., None, None] * c_mat + jnp.einsum('bhsd,bhsv->bhdv', kc * wk[..., None], vc)
        n_new = a[..., None] * n_vec + jnp.einsum('bhs,bhsd->bhd', wk, kc)
        return (c_new, n_new, m_new), out

    state, hs = lax.scan(body, state, xs)
    if with_output:
        hs = jnp.moveaxis(hs, 0, 2).reshape(bsz, nh, t_len, dv)
    return hs, state

def _mlstm_readout(h, o, norm_w, w_out):
    bsz, nh, t_len, dv = h.shape
    h = h.transpose(0, 2, 1, 3)
    h = h * lax.rsqrt(jnp.mean(h * h, axis=-1, keepdims=True) + EPS)
    h = h.reshape(bsz, t_len, nh * dv).astype(o.dtype) * norm_w
    return (jax.nn.sigmoid(o) * h) @ w_out

def _mlstm_mixer(hx, hc, w_qkvo, w_if, b_if, norm_w, w_out, ctx_out):
    qx, kx, vx, ox, igx, lfx = _mlstm_inputs(hx, w_qkvo, w_if, b_if, True)
    qc, kc, vc, oc, igc, lfc = _mlstm_inputs(hc, w_qkvo, w_if, b_if, ctx_out)
    bsz = hx.shape[0]
    zero = (jnp.zeros((bsz, ML_HEADS, ML_DQK, ML_DV), jnp.float32),
            jnp.zeros((bsz, ML_HEADS, ML_DQK), jnp.float32),
            jnp.zeros((bsz, ML_HEADS), jnp.float32))
    hx_sum = 0.0
    hc_sum = 0.0
    for r in range(2):
        if r == 0:
            flip = lambda a: a
        else:
            flip = lambda a: jnp.flip(a, axis=2)
        hc_r, st = _mlstm_scan(flip(qc), flip(kc), flip(vc), flip(igc[r]), flip(lfc[r]), zero, ctx_out)
        hx_r, _ = _mlstm_scan(flip(qx), flip(kx), flip(vx), flip(igx[r]), flip(lfx[r]), st, True)
        hx_sum = hx_sum + flip(hx_r)
        if ctx_out:
            hc_sum = hc_sum + flip(hc_r)
    yx = _mlstm_readout(hx_sum, ox, norm_w, w_out)
    yc = _mlstm_readout(hc_sum, oc, norm_w, w_out) if ctx_out else None
    return yx, yc

def first_inputs(seed: int = 0) -> dict:
    key = jax.random.key(seed)
    ks = jax.random.split(key, 20)
    f32 = jnp.float32

    def nrm(k, shape, fan_in):
        return jax.random.normal(k, shape, f32) * (fan_in ** -0.5)

    x = jax.random.normal(ks[0], (BATCH, SEQ, D_MODEL), f32)
    c = jax.random.normal(ks[1], (BATCH, D_MODEL), f32)
    ctx = jax.random.normal(ks[2], (BATCH, CTX_LEN, D_MODEL), f32)
    c_ctx = jax.random.normal(ks[3], (D_MODEL,), f32)
    norm_w = 1.0 + 0.02 * jax.random.normal(ks[4], (DEPTH, 4, D_MODEL), f32)
    mod_w = nrm(ks[5], (DEPTH, D_MODEL, 6 * D_MODEL), D_MODEL)
    mod_b = 0.01 * jax.random.normal(ks[6], (DEPTH, 6 * D_MODEL), f32)
    mlp_w1 = nrm(ks[7], (DEPTH, D_MODEL, D_FF), D_MODEL)
    mlp_w2 = nrm(ks[8], (DEPTH, D_FF, D_MODEL), D_FF)
    conv_w_in = nrm(ks[9], (N_CONV_LAYERS, D_MODEL, 3 * D_MODEL), D_MODEL)
    conv_w = nrm(ks[10], (N_CONV_LAYERS, CONV_W, D_MODEL), CONV_W)
    conv_w_out = nrm(ks[11], (N_CONV_LAYERS, D_MODEL, D_MODEL), D_MODEL)
    ml_w_qkvo = nrm(ks[12], (N_MLSTM_LAYERS, D_MODEL, ML_PROJ_COLS), D_MODEL)
    ml_w_if = nrm(ks[13], (N_MLSTM_LAYERS, 2, D_MODEL, 2 * ML_HEADS), D_MODEL)
    ig_b = 0.1 * jax.random.normal(ks[14], (N_MLSTM_LAYERS, 2, ML_HEADS), f32)
    fg_b = jnp.linspace(3.0, 6.0, ML_HEADS, dtype=f32) + 0.1 * jax.random.normal(ks[15], (N_MLSTM_LAYERS, 2, ML_HEADS), f32)
    ml_b_if = jnp.concatenate([ig_b, fg_b], axis=-1)
    ml_norm_w = 1.0 + 0.02 * jax.random.normal(ks[16], (N_MLSTM_LAYERS, ML_HEADS * ML_DV), f32)
    ml_w_out = nrm(ks[17], (N_MLSTM_LAYERS, ML_HEADS * ML_DV, D_MODEL), ML_HEADS * ML_DV)
    return {'x': x, 'c': c, 'ctx': ctx, 'c_ctx': c_ctx, 'norm_w': norm_w, 'mod_w': mod_w, 'mod_b': mod_b,
            'mlp_w1': mlp_w1, 'mlp_w2': mlp_w2, 'conv_w_in': conv_w_in, 'conv_w': conv_w,
            'conv_w_out': conv_w_out, 'ml_w_qkvo': ml_w_qkvo, 'ml_w_if': ml_w_if, 'ml_b_if': ml_b_if,
            'ml_norm_w': ml_norm_w, 'ml_w_out': ml_w_out}

def first_block(x, c, ctx, c_ctx, norm_w, mod_w, mod_b, mlp_w1, mlp_w2, conv_w_in, conv_w, conv_w_out,
              ml_w_qkvo, ml_w_if, ml_b_if, ml_norm_w, ml_w_out):
    rows = x.shape[1] // GRID_W
    silu_c = jax.nn.silu(c)[:, None, :]
    silu_cc = jax.nn.silu(c_ctx)
    cx = ctx
    for i in range(DEPTH):
        last = i == DEPTH - 1
        kind = i % N_MIXERS
        j = i // N_MIXERS
        nw = norm_w[i]
        mx = jnp.split(silu_c @ mod_w[i] + mod_b[i], 6, axis=-1)
        hx = _modulate(_rmsnorm(x, nw[0]), mx[0], mx[1])
        need_ctx = (not last) or kind == 1
        if need_ctx:
            mc = jnp.split(silu_cc @ mod_w[i] + mod_b[i], 6, axis=-1)
            hc = _modulate(_rmsnorm(cx, nw[0]), mc[0], mc[1])
        if kind == 0:
            yx = _short_conv_mixer(hx, conv_w_in[j], conv_w[j], conv_w_out[j], rows)
            yc = _short_conv_mixer(hc, conv_w_in[j], conv_w[j], conv_w_out[j], None) if not last else None
        else:
            yx, yc = _mlstm_mixer(hx, hc, ml_w_qkvo[j], ml_w_if[j], ml_b_if[j], ml_norm_w[j], ml_w_out[j],
                                  not last)
        x = x + mx[2] * _rmsnorm(yx, nw[1])
        x = x + mx[5] * _rmsnorm(_sqrelu_mlp(_modulate(_rmsnorm(x, nw[2]), mx[3], mx[4]), mlp_w1[i], mlp_w2[i]), nw[3])
        if not last:
            cx = cx + mc[2] * _rmsnorm(yc, nw[1])
            cx = cx + mc[5] * _rmsnorm(_sqrelu_mlp(_modulate(_rmsnorm(cx, nw[2]), mc[3], mc[4]), mlp_w1[i], mlp_w2[i]), nw[3])
    return x


N_MIXERS_2 = 3
HEAD_DIM = 64
DIFF_HEADS = D_MODEL // (2 * HEAD_DIM)
ATTN_QBLOCK = 128
DIL_HEADS = D_MODEL // HEAD_DIM
DIL_PATTERNS = ((128, 1), (512, 4), (2048, 16))
DIL_QBLOCK = 64
RWKV_HEADS = D_MODEL // HEAD_DIM
DECAY_LORA = 64
AAA_LORA = 64
GATE_LORA = 128
MEM_LEN = 256
XATT_HEADS = 4
D_FF_2 = 2816
CONV_WIDTH = 3
ALPHA = (2 * DEPTH) ** 0.25
BETA = (8 * DEPTH) ** -0.25
LN_EPS = 1e-5
GN_EPS = 64e-5
NEG_INF = -1e30
N_A = len(range(0, DEPTH, N_MIXERS_2))
N_B = len(range(1, DEPTH, N_MIXERS_2))
N_C = len(range(2, DEPTH, N_MIXERS_2))


def layer_norm(x, g, b):
    xf = x.astype(jnp.float32)
    mu = jnp.mean(xf, -1, keepdims=True)
    var = jnp.mean(jnp.square(xf - mu), -1, keepdims=True)
    return ((xf - mu) * lax.rsqrt(var + LN_EPS) * g + b).astype(x.dtype)

def rms_norm(x, g):
    xf = x.astype(jnp.float32)
    return (xf * lax.rsqrt(jnp.mean(jnp.square(xf), -1, keepdims=True) + LN_EPS) * g).astype(x.dtype)

def alibi_slopes(n):
    return jnp.exp2(-8.0 * jnp.arange(1, n + 1, dtype=jnp.float32) / n)

def diff_attention(x, w_qkv, lam, subln, w_o, lambda_init):
    B, S, D = x.shape
    H, E = DIFF_HEADS, HEAD_DIM
    q, k, v = jnp.split(x @ w_qkv, 3, axis=-1)
    q = q.reshape(B, S, H, 2, E)
    k = k.reshape(B, S, H, 2, E)
    v = v.reshape(B, S, H, 2 * E)
    lamf = lam.astype(jnp.float32)
    lam_full = jnp.exp(jnp.sum(lamf[0] * lamf[1])) - jnp.exp(jnp.sum(lamf[2] * lamf[3])) + lambda_init
    slopes = alibi_slopes(H)
    pos = jnp.arange(S)
    nblk = S // ATTN_QBLOCK
    qb = q.reshape(B, nblk, ATTN_QBLOCK, H, 2, E).transpose(1, 0, 2, 3, 4, 5)
    starts = jnp.arange(nblk) * ATTN_QBLOCK

    def block(args):
        q_blk, start = args
        s = jnp.einsum('bqhce,bkhce->bhcqk', q_blk, k,
                       preferred_element_type=jnp.float32) * (E ** -0.5)
        dist = jnp.abs((start + jnp.arange(ATTN_QBLOCK))[:, None] - pos[None, :]).astype(jnp.float32)
        s = s - slopes[None, :, None, None, None] * dist[None, None, None]
        p = jax.nn.softmax(s, axis=-1)
        attn = p[:, :, 0] - lam_full * p[:, :, 1]
        return jnp.einsum('bhqk,bkhe->bqhe', attn.astype(v.dtype), v)

    o = lax.map(block, (qb, starts))
    o = o.transpose(1, 0, 2, 3, 4).reshape(B, S, H, 2 * E)
    o = rms_norm(o, subln) * (1.0 - lambda_init)
    return o.reshape(B, S, D) @ w_o

def dilated_group(q, k, v, window, dilation, slopes):
    B, S, H, E = q.shape
    half = window // (2 * dilation)
    L = S // dilation
    nblk = -(-L // DIL_QBLOCK)
    Lp = nblk * DIL_QBLOCK
    KB = DIL_QBLOCK + 2 * half

    def to_res(a):
        return a.reshape(B, L, dilation, H, E).transpose(0, 2, 1, 3, 4)

    qr = jnp.pad(to_res(q), ((0, 0), (0, 0), (0, Lp - L), (0, 0), (0, 0)))
    pad_k = ((0, 0), (0, 0), (half, Lp - L + half), (0, 0), (0, 0))
    kr = jnp.pad(to_res(k), pad_k)
    vr = jnp.pad(to_res(v), pad_k)
    starts = jnp.arange(nblk) * DIL_QBLOCK
    idx = starts[:, None] + jnp.arange(KB)[None, :]
    kb = kr[:, :, idx]
    vb = vr[:, :, idx]
    qb = qr.reshape(B, dilation, nblk, DIL_QBLOCK, H, E)
    s = jnp.einsum('brnqhe,brnkhe->brnhqk', qb, kb,
                   preferred_element_type=jnp.float32) * (E ** -0.5)
    u_q = starts[:, None] + jnp.arange(DIL_QBLOCK)[None, :]
    u_k = idx - half
    rel = u_k[:, None, :] - u_q[:, :, None]
    valid = (jnp.abs(rel) <= half) & (u_k[:, None, :] >= 0) & (u_k[:, None, :] < L)
    dist = (dilation * jnp.abs(rel)).astype(jnp.float32)
    bias = -slopes[None, :, None, None] * dist[:, None]
    s = jnp.where(valid[:, None], s + bias, NEG_INF)
    lse = jax.nn.logsumexp(s, axis=-1)
    p = jnp.exp(s - lse[..., None])
    o = jnp.einsum('brnhqk,brnkhe->brnqhe', p.astype(v.dtype), vb)
    o = o.reshape(B, dilation, Lp, H, E)[:, :, :L].transpose(0, 2, 1, 3, 4).reshape(B, S, H, E)
    lse = lse.transpose(0, 1, 2, 4, 3).reshape(B, dilation, Lp, H)[:, :, :L]
    lse = lse.transpose(0, 2, 1, 3).reshape(B, S, H)
    return o, lse

def dilated_attention(x, w_qkv, w_o):
    B, S, D = x.shape
    H, E, G = DIL_HEADS, HEAD_DIM, len(DIL_PATTERNS)
    qkv = (x @ w_qkv).reshape(B, S, G, 3, H, E)
    slopes = alibi_slopes(H)
    outs, lses = [], []
    for g, (window, dilation) in enumerate(DIL_PATTERNS):
        o, l = dilated_group(qkv[:, :, g, 0], qkv[:, :, g, 1], qkv[:, :, g, 2], window, dilation, slopes)
        outs.append(o)
        lses.append(l)
    wts = jax.nn.softmax(jnp.stack(lses), axis=0)
    o = jnp.sum(wts[..., None] * jnp.stack(outs).astype(jnp.float32), axis=0)
    return o.astype(x.dtype).reshape(B, S, D) @ w_o

def token_shift(x, reverse):
    if reverse:
        return jnp.pad(x[:, 1:], ((0, 0), (0, 1), (0, 0)))
    return jnp.pad(x[:, :-1], ((0, 0), (1, 0), (0, 0)))

def wkv7_scan(r, w, k, v, kk, a, reverse):
    B, S, H, N = r.shape
    seq = tuple(t.transpose(1, 0, 2, 3) for t in (r, w, k, v, kk, a))

    def step(state, inp):
        r_t, w_t, k_t, v_t, kk_t, a_t = inp
        sa = jnp.einsum('bhij,bhj->bhi', state, -kk_t)
        state = (state * w_t[:, :, None, :] + sa[..., None] * (kk_t * a_t)[:, :, None, :]
                 + v_t[..., None] * k_t[:, :, None, :])
        return state, jnp.einsum('bhij,bhj->bhi', state, r_t)

    _, y = lax.scan(step, jnp.zeros((B, H, N, N), jnp.float32), seq, reverse=reverse)
    return y.transpose(1, 0, 2, 3)

def head_group_norm(y, g, b):
    H, N = y.shape[-2], y.shape[-1]
    mu = jnp.mean(y, -1, keepdims=True)
    var = jnp.mean(jnp.square(y - mu), -1, keepdims=True)
    return (y - mu) * lax.rsqrt(var + GN_EPS) * g.reshape(H, N) + b.reshape(H, N)

def rwkv7_direction(x, mu, w_r, w_k, w_v, w0, w1, w2, a0, a1, a2, g1, g2, k_k, k_a, r_k,
                    gn_g, gn_b, reverse):
    B, S, D = x.shape
    H, N = RWKV_HEADS, HEAD_DIM
    xx = token_shift(x, reverse) - x
    xr, xw, xk, xv, xa, xg = (x + xx * mu[j] for j in range(6))
    r = xr @ w_r
    k = xk @ w_k
    v = xv @ w_v
    w_log = -jax.nn.softplus(-(w0 + jnp.tanh(xw @ w1) @ w2).astype(jnp.float32)) - 0.5
    w = jnp.exp(-jnp.exp(w_log))
    a = jax.nn.sigmoid((a0 + (xa @ a1) @ a2).astype(jnp.float32))
    g = jax.nn.sigmoid(xg @ g1) @ g2

    def heads(t):
        return t.astype(jnp.float32).reshape(B, S, H, N)

    r, k, v, w, a = heads(r), heads(k), heads(v), heads(w), heads(a)
    kk = k * k_k.astype(jnp.float32).reshape(H, N)
    kk = kk / jnp.maximum(jnp.linalg.norm(kk, axis=-1, keepdims=True), 1e-12)
    k = k * (1.0 + (a - 1.0) * k_a.astype(jnp.float32).reshape(H, N))
    y = wkv7_scan(r, w, k, v, kk, a, reverse)
    y = head_group_norm(y, gn_g, gn_b) + jnp.sum(r * k * r_k.astype(jnp.float32), -1, keepdims=True) * v
    return (y.reshape(B, S, D) * g).astype(x.dtype)

def rwkv7_time_mix(x, mu, w_rkv, w0, w1, w2, a0, a1, a2, g1, g2, k_k, k_a, r_k, gn_g, gn_b, w_o):
    fwd = rwkv7_direction(x, mu[0], w_rkv[0], w_rkv[1], w_rkv[2], w0[0], w1[0], w2[0], a0[0], a1[0], a2[0],
                          g1[0], g2[0], k_k[0], k_a[0], r_k, gn_g, gn_b, False)
    bwd = rwkv7_direction(x, mu[1], w_rkv[0], w_rkv[1], w_rkv[2], w0[1], w1[1], w2[1], a0[1], a1[1], a2[1],
                          g1[1], g2[1], k_k[1], k_a[1], r_k, gn_g, gn_b, True)
    return (fwd + bwd) @ w_o

def memory_cross_attention(x, mem, w_q, w_kv, w_o):
    B, S, D = x.shape
    M = mem.shape[1]
    H = XATT_HEADS
    E = D // H
    q = (x @ w_q).reshape(B, S, H, E)
    kv = (mem @ w_kv).reshape(B, M, 2, H, E)
    s = jnp.einsum('bshe,bmhe->bhsm', q, kv[:, :, 0], preferred_element_type=jnp.float32) * (E ** -0.5)
    p = jax.nn.softmax(s, axis=-1).astype(x.dtype)
    o = jnp.einsum('bhsm,bmhe->bshe', p, kv[:, :, 1])
    return o.reshape(B, S, D) @ w_o

def conv_glu(x, w_in, conv_w, conv_b, w_out):
    gate, val = jnp.split(x @ w_in, 2, axis=-1)
    gate = lax.conv_general_dilated(gate, conv_w[:, None, :], window_strides=(1,),
                                    padding=((CONV_WIDTH // 2, CONV_WIDTH // 2),),
                                    dimension_numbers=('NWC', 'WIO', 'NWC'),
                                    feature_group_count=gate.shape[-1]) + conv_b
    return (jax.nn.gelu(gate, approximate=False) * val) @ w_out

def second_inputs(seed: int = 0) -> dict:
    key = jax.random.key(seed)
    keys = iter(jax.random.split(key, 48))
    D, F, H, N = D_MODEL, D_FF_2, RWKV_HEADS, HEAD_DIM
    G = len(DIL_PATTERNS)
    inv = D ** -0.5

    def normal(shape, scale):
        return jax.random.normal(next(keys), shape, jnp.float32) * scale

    def uniform(shape, lo, hi):
        return jax.random.uniform(next(keys), shape, jnp.float32, lo, hi)

    return {
        "x": normal((BATCH, SEQ, D), 1.0),
        "mem": normal((BATCH, MEM_LEN, D), 1.0),
        "diff_w_qkv": normal((N_A, D, 3 * D), inv),
        "diff_lambda": normal((N_A, 4, HEAD_DIM), 0.1),
        "diff_subln": 1.0 + normal((N_A, 2 * HEAD_DIM), 0.02),
        "diff_w_o": normal((N_A, D, D), inv * BETA),
        "dil_w_qkv": normal((N_B, D, G * 3 * D), inv),
        "dil_w_o": normal((N_B, D, D), inv * BETA),
        "rwkv_mu": uniform((N_C, 2, 6, D), 0.0, 1.0),
        "rwkv_w_rkv": normal((N_C, 3, D, D), inv),
        "rwkv_w0": uniform((N_C, 2, D), -5.0, 0.0),
        "rwkv_w1": normal((N_C, 2, D, DECAY_LORA), inv),
        "rwkv_w2": normal((N_C, 2, DECAY_LORA, D), 0.1 * DECAY_LORA ** -0.5),
        "rwkv_a0": normal((N_C, 2, D), 0.1),
        "rwkv_a1": normal((N_C, 2, D, AAA_LORA), inv),
        "rwkv_a2": normal((N_C, 2, AAA_LORA, D), 0.1 * AAA_LORA ** -0.5),
        "rwkv_g1": normal((N_C, 2, D, GATE_LORA), inv),
        "rwkv_g2": normal((N_C, 2, GATE_LORA, D), GATE_LORA ** -0.5),
        "rwkv_k_k": 0.85 + normal((N_C, 2, D), 0.02),
        "rwkv_k_a": 1.0 + normal((N_C, 2, D), 0.02),
        "rwkv_r_k": normal((N_C, H, N), 0.1),
        "rwkv_gn_g": 1.0 + normal((N_C, D), 0.02),
        "rwkv_gn_b": normal((N_C, D), 0.02),
        "rwkv_w_o": normal((N_C, D, D), inv * BETA),
        "xatt_w_q": normal((DEPTH, D, D), inv),
        "xatt_w_kv": normal((DEPTH, D, 2 * D), inv),
        "xatt_w_o": normal((DEPTH, D, D), inv * BETA),
        "ffn_w_in": normal((DEPTH, D, 2 * F), inv),
        "ffn_conv_w": normal((DEPTH, CONV_WIDTH, F), CONV_WIDTH ** -0.5),
        "ffn_conv_b": normal((DEPTH, F), 0.02),
        "ffn_w_out": normal((DEPTH, F, D), F ** -0.5 * BETA),
        "ln_g": 1.0 + normal((DEPTH, 3, D), 0.02),
        "ln_b": normal((DEPTH, 3, D), 0.02),
    }

def second_block(x, mem, diff_w_qkv, diff_lambda, diff_subln, diff_w_o, dil_w_qkv, dil_w_o,
              rwkv_mu, rwkv_w_rkv, rwkv_w0, rwkv_w1, rwkv_w2, rwkv_a0, rwkv_a1, rwkv_a2,
              rwkv_g1, rwkv_g2, rwkv_k_k, rwkv_k_a, rwkv_r_k, rwkv_gn_g, rwkv_gn_b, rwkv_w_o,
              xatt_w_q, xatt_w_kv, xatt_w_o, ffn_w_in, ffn_conv_w, ffn_conv_b, ffn_w_out,
              ln_g, ln_b):
    for i in range(DEPTH):
        m, j = i % N_MIXERS_2, i // N_MIXERS_2
        if m == 0:
            lambda_init = 0.8 - 0.6 * math.exp(-0.3 * i)
            h = diff_attention(x, diff_w_qkv[j], diff_lambda[j], diff_subln[j], diff_w_o[j], lambda_init)
        elif m == 1:
            h = dilated_attention(x, dil_w_qkv[j], dil_w_o[j])
        else:
            h = rwkv7_time_mix(x, rwkv_mu[j], rwkv_w_rkv[j], rwkv_w0[j], rwkv_w1[j], rwkv_w2[j],
                               rwkv_a0[j], rwkv_a1[j], rwkv_a2[j], rwkv_g1[j], rwkv_g2[j],
                               rwkv_k_k[j], rwkv_k_a[j], rwkv_r_k[j], rwkv_gn_g[j], rwkv_gn_b[j],
                               rwkv_w_o[j])
        x = layer_norm(ALPHA * x + h, ln_g[i, 0], ln_b[i, 0])
        x = layer_norm(ALPHA * x + memory_cross_attention(x, mem, xatt_w_q[i], xatt_w_kv[i], xatt_w_o[i]),
                       ln_g[i, 1], ln_b[i, 1])
        x = layer_norm(ALPHA * x + conv_glu(x, ffn_w_in[i], ffn_conv_w[i], ffn_conv_b[i], ffn_w_out[i]),
                       ln_g[i, 2], ln_b[i, 2])
    return x


def setup_inputs(seed=0):
    out = dict(first_inputs(seed))
    for name, value in second_inputs(seed + 1).items():
        if name != "x":
            out[name + "_2"] = value
    return out


def reference(
    x, c, ctx, c_ctx, norm_w, mod_w, mod_b, mlp_w1, mlp_w2, conv_w_in, conv_w, conv_w_out,
    ml_w_qkvo, ml_w_if, ml_b_if, ml_norm_w, ml_w_out, mem_2, diff_w_qkv_2, diff_lambda_2,
    diff_subln_2, diff_w_o_2, dil_w_qkv_2, dil_w_o_2, rwkv_mu_2, rwkv_w_rkv_2, rwkv_w0_2,
    rwkv_w1_2, rwkv_w2_2, rwkv_a0_2, rwkv_a1_2, rwkv_a2_2, rwkv_g1_2, rwkv_g2_2, rwkv_k_k_2,
    rwkv_k_a_2, rwkv_r_k_2, rwkv_gn_g_2, rwkv_gn_b_2, rwkv_w_o_2, xatt_w_q_2, xatt_w_kv_2,
    xatt_w_o_2, ffn_w_in_2, ffn_conv_w_2, ffn_conv_b_2, ffn_w_out_2, ln_g_2, ln_b_2,
):
    x = first_block(
        x, c, ctx, c_ctx, norm_w, mod_w, mod_b, mlp_w1, mlp_w2, conv_w_in, conv_w, conv_w_out,
        ml_w_qkvo, ml_w_if, ml_b_if, ml_norm_w, ml_w_out,
    )
    return second_block(
        x, mem_2, diff_w_qkv_2, diff_lambda_2, diff_subln_2, diff_w_o_2, dil_w_qkv_2, dil_w_o_2,
        rwkv_mu_2, rwkv_w_rkv_2, rwkv_w0_2, rwkv_w1_2, rwkv_w2_2, rwkv_a0_2, rwkv_a1_2,
        rwkv_a2_2, rwkv_g1_2, rwkv_g2_2, rwkv_k_k_2, rwkv_k_a_2, rwkv_r_k_2, rwkv_gn_g_2,
        rwkv_gn_b_2, rwkv_w_o_2, xatt_w_q_2, xatt_w_kv_2, xatt_w_o_2, ffn_w_in_2, ffn_conv_w_2,
        ffn_conv_b_2, ffn_w_out_2, ln_g_2, ln_b_2,
    )


_drawn_inputs = setup_inputs


def setup_inputs(seed=0):
    import zlib

    import numpy as np

    out = dict(_drawn_inputs(seed))
    spreads = {}
    factors = {'ml_norm_w': 6.171, 'diff_subln_2': 8.0, 'ffn_conv_b_2': 8.0}
    for name, (base, spread) in spreads.items():
        noise = np.random.default_rng([zlib.crc32(name.encode()), seed]).standard_normal(out[name].shape)
        drawn = base * np.exp(spread * noise) if base else spread * noise
        out[name] = jnp.asarray(drawn.astype(out[name].dtype))
    for name, factor in factors.items():
        out[name] = (out[name] * factor).astype(out[name].dtype)
    return out
```

```python
from contextlib import ExitStack

import concourse.bass as bass
from concourse import mybir

F32 = mybir.dt.float32
F32R = mybir.dt.float32r
ACT = mybir.ActivationFunctionType
ALU = mybir.AluOpType
AXX = mybir.AxisListType.X

P = 128
D = 1024
KT = D // P
TX = 512
TC = 256
TA = TX + TC
TM = 256
GRID_W = 64
HEADS = 8
FF = 4 * D
FF2 = 2816
FT2 = FF2 // P
XH = 4
EPS = 1e-6
LN_EPS = 1e-5
ALPHA = 4 ** 0.25
LAMBDA_INIT = 0.2
BIG = 1e30
RING = 4


class Stage:

    def __init__(self, name, n, body, groups, kt=KT):
        self.name, self.n, self.body, self.groups, self.kt = name, n, body, groups, kt
        self.B = len(body)
        assert self.B % RING == 0
        self.inc = {}
        for b, u in enumerate(body):
            if u is not None:
                skip = 0
                while b + 1 + skip < self.B and body[b + 1 + skip] is None:
                    skip += 1
                self.inc[b] = 1 + skip
        self.next = None


class Plan:

    def __init__(self, stages):
        self.stages = stages
        h, m = RING, RING
        loads = [0] * RING
        last = None
        for st in stages:
            st.loads = list(loads)
            st.per = [sum(1 for b in st.inc if b % RING == s) for s in range(RING)]
            loads = [a + st.n * p for a, p in zip(loads, st.per)]
            st.h0, st.m0 = h, m
            if st.raw:
                m += st.n * st.B
                last = None
            else:
                h += st.n * st.B
                if last is not None:
                    last.next = st
                last = st
            st.h1, st.m1 = h, m

    def loaded(self, st, i, b):
        before = sum(1 for c in st.inc if c < b and c % RING == b % RING)
        return 16 * (st.loads[b % RING] + before + 1) + i * (16 * st.per[b % RING])


def build(nc, a, out):
    GX = [(0, 0, TX)]
    GXC = [(0, 0, TX), (1, TX, TC)]
    GC = [(1, TX, TC)]
    GM = [(0, 0, TM)]

    def cols(w, c, k0=0, kt=KT):
        return w.rearrange("(k p) n -> p k n", p=P)[:, k0:k0 + kt, bass.ds(c, P)]

    def unit(w, step, c):
        return lambda i: cols(w, i * step + c)

    def mod_stage(l):
        st = Stage(f"mod{l}", 12, [(lambda i, b=b: cols(a["mod_w"][l], i * (4 * P) + b * P)) for b in range(4)], None)
        st.raw = True
        return st

    def dense(name, w, groups, tiles=KT, c0=0, k0=0, kt=KT):
        st = Stage(name, tiles // 4, [(lambda i, b=b: cols(w, i * (4 * P) + (c0 + b) * P, k0, kt)) for b in range(4)],
                   groups, kt)
        st.raw = False
        return st

    def custom(name, n, body, groups):
        st = Stage(name, n, body, groups)
        st.raw = False
        return st

    S = {}
    order = []

    def add(st):
        S[st.name] = st
        order.append(st)

    w_in, w_out = a["conv_w_in"][0], a["conv_w_out"][0]
    add(mod_stage(0))
    add(custom("conv", KT, [unit(w_in, P, j * D) for j in range(3)] + [None], GXC))
    add(dense("conv_out", w_out, GXC))
    for c in range(4):
        add(dense(f"mlp0_up{c}", a["mlp_w1"][0], GXC, c0=c * KT))
        add(dense(f"mlp0_down{c}", a["mlp_w2"][0], GXC, k0=c * KT))
    add(mod_stage(1))
    qkvo = a["ml_w_qkvo"][0]
    ml_at = [0, KT // 2, KT, KT + 1, 2 * KT, 2 * KT + 1]
    ml_step = [1, 1, 2, 2, 2, 2]
    add(custom("mlstm", HEADS // 2,
               [unit(qkvo, s * P, c * P) for c, s in zip(ml_at, ml_step)] + [None, None],
               None))
    add(dense("mlstm_out", a["ml_w_out"][0], GX))
    for c in range(4):
        add(dense(f"mlp1_up{c}", a["mlp_w1"][1], GX, c0=c * KT))
        add(dense(f"mlp1_down{c}", a["mlp_w2"][1], GX, k0=c * KT))
    dq = a["diff_w_qkv_2"][0]
    add(custom("diff", HEADS, [unit(dq, P, j * D) for j in range(3)] + [None], GX))
    add(dense("diff_out", a["diff_w_o_2"][0], GX))
    lq = a["dil_w_qkv_2"][0]
    for l in range(2):
        if l == 1:
            body = []
            for g in range(3):
                body += [unit(lq, P, (g * 3 + j) * D) for j in range(3)] + [None]
            add(custom("dil", HEADS, body, GX))
            add(dense("dil_out", a["dil_w_o_2"][0], GX))
        kv, wq = a["xatt_w_kv_2"][l], a["xatt_w_q_2"][l]
        body = [unit(kv, 2 * P, c) for c in (0, P, D, D + P)] + [unit(wq, 2 * P, c) for c in (0, P)] + [None, None]
        add(custom(f"xatt{l}", XH, body, None))
        add(dense(f"xatt{l}_out", a["xatt_w_o_2"][l], GX))
        for c in range(3):
            nt = min(8, FT2 - 8 * c)
            body = [unit(a["ffn_w_in_2"][l], 2 * P, (8 * c + t) * P + o) for t in range(2) for o in (0, FF2)]
            add(custom(f"ffn{l}_in{c}", nt // 2, body, GX))
            add(dense(f"ffn{l}_out{c}", a["ffn_w_out_2"][l], GX, k0=8 * c, kt=nt))
    plan = Plan(order)

    with ExitStack() as ctx:
        def sem(name):
            return ctx.enter_context(nc.semaphore(name))

        base = 16512
        top = [base]

        def place(name, shape, dt=F32, at=None):
            size = 4
            for s in shape[1:]:
                size *= s
            if at is None:
                at = top[0]
                top[0] += (size + 31) // 32 * 32
            return nc.alloc_sbuf_tensor_at(name, shape, dt, offset=at)

        WR = place("w_raw", [P, RING, KT, P])
        WS = place("w_split", [P, 2, RING, KT, P], F32R)
        X = place("x_state", [P, KT, TA])
        h_at = top[0]
        HA = place("h_a", [P, 2, KT, TA], F32R)
        g_at = top[0]
        GA = place("g_a", [P, 2, KT, TA], F32R)
        y_at = top[0]
        Y = place("y", [P, KT, TA])
        wk_at = top[0]
        WK = place("wk", [P, 3, TA])
        ident = place("ident", [P, P])
        ones = place("ones", [P, P])
        VT = place("vt", [P, 5, P])
        MOD = place("mod", [P, 2, 48])
        COEF = place("coef", [P, 2, 4, KT])
        SV = place("sv", [P, KT, 2])
        MASK = place("mask", [P, 2, P])
        SLOPE = place("slope", [P, HEADS])
        SM = place("small", [P, 32])
        LSL = place("dl_slope", [P, 2 * HEADS])
        assert top[0] <= 229344, top[0]
        XTOK = place("x_tok", [P, 6, D], at=y_at)
        VR = place("vr", [P, 5, P], at=wk_at)
        half = 4 * 2 * KT * TX
        G1 = place("g_1", [P, 2, KT, TX], F32R, at=g_at)
        tail = g_at + half
        WIF = place("wif", [P, KT, P], at=tail)
        MROW = place("mrow", [8, 2, TX], at=tail)
        IG = place("ig_rows", [8, 2, TA], at=tail + 4096)
        BR = place("b_rows", [8, 2, TA], at=tail + 4096 + 6144)
        GCOL = place("g_cols", [P, 2, 6, 8], at=wk_at + 8704)
        LF = place("lf_rows", [8, 6, TA], at=y_at)
        MQ = place("ml_q", [P, TX], at=y_at)
        MK = place("ml_k", [P, TA], at=y_at + 2048)
        MV = place("ml_v", [P, TA], at=y_at + 5120)
        MO = place("ml_o", [P, 2, TX], at=y_at + 8192)
        ME = place("ml_e", [P, 2, TX], at=y_at + 12288)
        MM = place("ml_mneg", [P, 2, TX], at=y_at + 16384)
        RH = place("ml_rows", [8, 2, TX], at=y_at + 20480)
        HS = place("ml_h", [P, TX], at=wk_at)
        RD = place("ml_rd", [P, TX], at=wk_at + 2048)
        MT = place("ml_t", [P, TX], at=wk_at + 4096)
        HB = place("h_b", [P, 2, KT, TX], F32R, at=h_at)
        MEMH = place("mem_h", [P, 2, KT, TM], F32R, at=h_at + half)
        GB = place("g_b", [P, 2, KT, TX], F32R, at=g_at)
        MEMT = place("mem_tok", [P, 2, D], at=tail)
        wb = tail
        WB = place("wk_b", [P, 6, TX], at=wb)
        at_b = wb + 12288
        AQ = place("at_q", [P, 2, TX], at=at_b)
        AK = place("at_k", [P, 2, TX], at=at_b + 4096)
        AV = place("at_v", [P, TX], at=at_b + 8192)
        MEMF = place("mem_f", [P, KT, TM], at=at_b + 19456)
        VTK = place("v_tok", [P, 4, P], at=at_b + 10240)
        DIST = place("dist", [P, 896], at=at_b + 12288)
        DISTI = place("dist_i", [P, 896], mybir.dt.int32, at=at_b + 12288 + 3584)
        SB = place("bias_h", [P, 896], at=at_b + 12288 + 3584)
        DS = place("scores", [P, 2, 2, TX], at=at_b + 19456)
        AT = place("attn_t", [P, 4, TX], at=at_b + 27648)
        DST = place("diff_stat", [P, 4, 4, 2], at=at_b + 35840)
        assert at_b + 35840 + 128 <= wk_at + 9216
        OG = place("og", [P, HEADS, 2, TX], at=g_at)
        OG2 = place("og2", [P, HEADS, TX], at=at_b)
        dl = at_b + 16384
        LQ = place("dl_qkv", [P, 3, TX], at=dl)
        LB = place("dl_dist", [P, 640], at=dl + 6144)
        LSB = place("dl_bias", [P, 640], at=dl + 8704)
        LBI = place("dl_dist_i", [P, 640], mybir.dt.int32, at=dl + 8704)
        LP = place("dl_p", [P, 1024], at=dl + 11264)
        LPT = place("dl_pt", [P, 8, P], at=dl + 15360)
        LMS = place("dl_stat", [P, 2, 3, 4, 16], at=dl + 19456)
        LROW = place("dl_rows", [16, 6, TX], at=wb)
        LSEL = place("dl_sel", [16, HEADS, P], at=dl)
        LR2 = place("dl_rows2", [16, TX], at=dl + 4096)
        assert dl + 19456 + 1536 <= wk_at + 9216
        OTOK = place("out_tok", [P, 4, D], at=wb)

        psl = ctx.enter_context(nc.psum_tensor("ps_lin", [P, 2, 2, 512], F32))
        psa = ctx.enter_context(nc.psum_tensor("ps_att", [P, 4, 512], F32))

        loaded = [sem(f"w_loaded{s}") for s in range(RING)]
        hi_ready = sem("w_hi_ready")
        lo_ready = sem("w_lo_ready")
        unit_done = sem("unit_done")
        mod_used = sem("mod_used")
        evac_done = sem("evac_done")
        split_ready = sem("split_ready")
        split_hi = sem("split_hi")
        split_done = sem("split_done")
        small_in = sem("small_in")
        x_in = sem("x_in")
        wif_in = sem("wif_in")
        lam_in = sem("lam_in")
        mem_in = sem("mem_in")
        out_sem = sem("out_stored")
        const_step = sem("const_step")
        const_ready = sem("const_ready")
        x_tr = sem("out_transposed")
        x_tr_k = sem("x_transposed")
        x_ready = sem("x_ready")
        v_tr = sem("vectors_transposed")
        v_ready = sem("vectors_ready")
        sv_exp = sem("silu_exp")
        sv_ready = sem("silu_ready")
        sq_ready = sem("sq_ready")
        ysq_ready = sem("ysq_ready")
        acc_ready = sem("acc_ready")
        stat_ready = sem("stat_ready")
        mean_ready = sem("mean_ready")
        var_ready = sem("var_ready")
        rstd_ready = sem("rstd_ready")
        wif_zero = sem("wif_zero")

        def tile_at(ap3, m):
            return ap3[:, bass.ds(m, 1), :].rearrange("p a n -> p (a n)")

        def col(ap2, m):
            return ap2[:, bass.ds(m, 1)]

        def h_of(st, i, b):
            return i * st.B + (st.h0 + b)

        def groups_of(st, b):
            if st.groups is not None:
                return st.groups
            if st.name == "mlstm":
                return GX if b in (0, 4, 5) else GXC
            return GM if b < 4 else GX

        def pe_unit(pe, st, i, b, rhs, kwait=None):
            pe.wait_ge(lo_ready, h_of(st, i, b) + 1)
            pe.wait_ge(evac_done, h_of(st, i, b) - 1)
            groups = groups_of(st, b)
            for k in range(st.kt):
                if kwait is not None:
                    pe.wait_ge(split_done, kwait + k + 1)
                for n, (wp, xp) in enumerate(((0, 0), (0, 1), (1, 0))):
                    for gi, c0, nn in groups:
                        mm = pe.matmul(psl[:, b % 2, gi, 0:nn], WS[:, wp, b % RING, k, :], rhs[:, xp, k, c0:c0 + nn],
                                       start=(k == 0 and n == 0), stop=(k == st.kt - 1 and n == 2))
            mm.then_inc(unit_done, st.inc[b])

        def pe_dense(pe, st, rhs, kwait):
            with pe.Fori(0, st.n) as i:
                for b in sorted(st.inc):
                    pe_unit(pe, st, i, b, rhs, kwait if b == 0 else None)

        def act_hi(act, st, i, b):
            t = b + 3
            if t >= st.B:
                t -= st.B
                if isinstance(i, int) and i == st.n - 1:
                    st, i = st.next, 0
                    if st is None:
                        return
                else:
                    i = i + 1
            if t not in st.inc:
                return
            act.wait_ge(loaded[t % RING], plan.loaded(st, i, t))
            act.wait_ge(unit_done, h_of(st, i, t) - 3)
            act.activation(WS[:, 0, t % RING, 0:st.kt, :], WR[:, t % RING, 0:st.kt, :], ACT.Copy)\
               .then_inc(hi_ready, st.inc[t])

        def act_first(act, st):
            for t in range(3):
                act.wait_ge(loaded[t], plan.loaded(st, 0, t))
                act.activation(WS[:, 0, t, :, :], WR[:, t, :, :], ACT.Copy).then_inc(hi_ready, st.inc[t])

        def act_rounds(act, st, body):
            if st.n > 1:
                with act.Fori(0, st.n - 1) as i:
                    body(i)
            body(st.n - 1)

        def evac_wait(dve, st, i, b):
            dve.wait_ge(unit_done, h_of(st, i, b) + 1)

        def act_split(act, idx, src, dst):
            act.wait_ge(split_ready, idx + 1)
            act.activation(dst, src, ACT.Copy).then_inc(split_hi, 1)

        def dve_split(dve, idx, src, hi, lo):
            dve.wait_ge(split_hi, idx + 1)
            dve.tensor_tensor(lo, src, hi.bitcast(F32), ALU.subtract).then_inc(split_done, 1)

        cnt = {"split": 0, "stat": 0, "sq": 0, "x": 0, "ysq": 0, "mean": 0}

        def take(kind, n):
            v = cnt[kind]
            cnt[kind] = v + n
            return v

        N = {}
        N["x0"] = take("x", 8)
        for nm in ("n0",):
            N[nm] = (take("sq", 8), take("stat", 1), take("split", 8))
        N["conv"] = take("split", 8)

        def number_residual(nm):
            N[nm] = (take("ysq", 8), take("stat", 1), take("x", 8))

        number_residual("r0")
        N["n1"] = (take("sq", 8), take("stat", 1), take("split", 8))
        for c in range(4):
            N[f"mlp0_{c}"] = take("split", 8)
        number_residual("r1")
        N["n2"] = (take("sq", 8), take("stat", 1), take("split", 8))
        N["mlstm"] = take("split", 8)
        number_residual("r2")
        N["n3"] = (take("sq", 8), take("stat", 1), take("split", 8))
        for c in range(4):
            N[f"mlp1_{c}"] = take("split", 8)
        N["r3"] = (take("ysq", 8), take("stat", 1), None)
        N["xb"] = take("split", 8)
        N["mem"] = take("split", 8)

        def number_ln(nm, split):
            N[nm] = (take("ysq", 8), take("stat", 1), take("mean", 1), take("split", 8) if split else None)

        for l in range(2):
            N[f"mix{l}"] = take("split", 8)
            number_ln(f"ln{l}0", True)
            N[f"xatt{l}"] = take("split", 8)
            number_ln(f"ln{l}1", True)
            for c in range(3):
                N[f"ffn{l}_{c}"] = take("split", min(8, FT2 - 8 * c))
            number_ln(f"ln{l}2", l == 0)
        N["x_end"] = take("x", 8)

        def X_(k, n):
            return X[:, k, 0:n]

        TMP, RB, ACC = WK[:, 0, :], WK[:, 1, :], WK[:, 2, :]

        def act_stat(act, s, groups, eps, scale=1.0 / D):
            act.wait_ge(stat_ready, s + 1)
            for gi, c0, n in groups:
                act.activation(RB[:, c0:c0 + n], psa[:, gi, 0:n], ACT.Ln, bias=eps, scale=scale)
            act.drain()
            n = sum(g[2] for g in groups)
            act.activation(RB[:, 0:n], RB[:, 0:n], ACT.Exp, scale=-0.5).then_inc(rstd_ready, 1)

        def act_prenorm(act, num, groups, xbase, whole):
            sq, s, sp = num
            n = sum(g[2] for g in groups)
            for k in range(KT):
                act.wait_ge(x_ready, xbase + (KT if whole else k + 1))
                act.activation(Y[:, k, 0:n], X_(k, n), ACT.Square).then_inc(sq_ready, 1)
            act_stat(act, s, groups, EPS)
            for k in range(KT):
                act_split(act, sp + k, Y[:, k, 0:n], HA[:, 0, k, 0:n])

        def dve_prenorm(dve, num, groups, which, between=None):
            sq, s, sp = num
            n = sum(g[2] for g in groups)
            for k in range(KT):
                dve.drain()
                dve.wait_ge(sq_ready, sq + k + 1)
                if k == 0:
                    dve.tensor_copy(ACC[:, 0:n], Y[:, 0, 0:n]).then_inc(acc_ready, 1)
                else:
                    dve.tensor_tensor(ACC[:, 0:n], ACC[:, 0:n], Y[:, k, 0:n], ALU.add).then_inc(acc_ready, 1)
            if between is not None:
                between()
            dve.wait_ge(rstd_ready, s + 1)
            for k in range(KT + 1):
                if k < KT:
                    dve.tensor_tensor(Y[:, k, 0:n], X_(k, n), RB[:, 0:n], ALU.mult)
                    dve.drain()
                    for v, (gi, c0, nn) in enumerate(groups):
                        op = dve.tensor_scalar(Y[:, k, c0:c0 + nn], Y[:, k, c0:c0 + nn],
                                               COEF[:, v, 2 * which, k:k + 1], MOD[:, v, 24 * which + k:24 * which + k + 1],
                                               ALU.mult, ALU.add)
                    op.then_inc(split_ready, 1)
                if k > 0:
                    dve_split(dve, sp + k - 1, Y[:, k - 1, 0:n], HA[:, 0, k - 1, 0:n], HA[:, 1, k - 1, 0:n])

        def pe_stat(pe, s, groups, src):
            pe.wait_ge(acc_ready, 8 * (s + 1))
            for gi, c0, n in groups:
                mm = pe.matmul(psa[:, gi, 0:n], ones[:], src[:, c0:c0 + n], start=True, stop=True)
            mm.then_inc(stat_ready, 1)

        def act_ysq(act, st, num, last, n):
            ysq, s, xb = num

            def body(i):
                for b in range(4):
                    if last:
                        act.wait_ge(evac_done, h_of(st, i, b) + 1)
                        act.wait_ge(acc_ready, 8 * s + i * 4 + b)
                        act.activation(TMP[:, 0:n], tile_at(Y[:, :, 0:n], i * 4 + b), ACT.Square)\
                           .then_inc(ysq_ready, 1)
                    act_hi(act, st, i, b)
            act_rounds(act, st, body)

        def dve_y(dve, st, num, first, last, n):
            ysq, s, xb = num
            with dve.Fori(0, st.n) as i:
                for b in range(4):
                    dve.drain()
                    evac_wait(dve, st, i, b)
                    y = Y[:, bass.ds(i * 4 + b, 1), :].rearrange("p a n -> p (a n)")
                    for gi, c0, nn in st.groups:
                        if first:
                            op = dve.tensor_copy(y[:, c0:c0 + nn], psl[:, b % 2, gi, 0:nn])
                        else:
                            op = dve.tensor_tensor(y[:, c0:c0 + nn], psl[:, b % 2, gi, 0:nn], y[:, c0:c0 + nn], ALU.add)
                    op.then_inc(evac_done, 1)
                    if last:
                        dve.wait_ge(ysq_ready, i * 4 + (ysq + b + 1))
                        dve.tensor_tensor(ACC[:, 0:n], ACC[:, 0:n], TMP[:, 0:n], ALU.add).then_inc(acc_ready, 1)

        def dve_zero_acc(dve, n):
            dve.drain()
            dve.memset(ACC[:, 0:n], 0.0)

        def dve_residual(dve, num, groups, which, out_sem_=x_ready):
            ysq, s, xb = num
            n = sum(g[2] for g in groups)
            dve.wait_ge(rstd_ready, s + 1)
            for k in range(KT):
                dve.tensor_tensor(Y[:, k, 0:n], Y[:, k, 0:n], RB[:, 0:n], ALU.mult)
                dve.drain()
                for v, (gi, c0, nn) in enumerate(groups):
                    op = dve.scalar_tensor_tensor(out=X[:, k, c0:c0 + nn], in0=Y[:, k, c0:c0 + nn],
                                                  scalar=COEF[:, v, 2 * which + 1, k:k + 1], in1=X[:, k, c0:c0 + nn],
                                                  op0=ALU.mult, op1=ALU.add)
                op.then_inc(out_sem_, 1)

        def act_up(act, st, sp, G, n):
            def body(i):
                for b in range(4):
                    act_split(act, i * 4 + (sp + b), WK[:, b % 2, 0:n], tile_at(G[:, 0, :, 0:n], i * 4 + b))
                    act_hi(act, st, i, b)
            act_rounds(act, st, body)

        def dve_up(dve, st, sp, G, n):
            with dve.Fori(0, st.n) as i:
                for b in range(4):
                    dve.drain()
                    evac_wait(dve, st, i, b)
                    z = WK[:, b % 2, 0:n]
                    for gi, c0, nn in st.groups:
                        op = dve.tensor_scalar(z[:, c0:c0 + nn], psl[:, b % 2, gi, 0:nn], 0.0, None, ALU.max)
                    op.then_inc(evac_done, 1)
                    dve.drain()
                    dve.tensor_tensor(z, z, z, ALU.mult).then_inc(split_ready, 1)
                    dve_split(dve, i * 4 + (sp + b), z, tile_at(G[:, 0, :, 0:n], i * 4 + b),
                              tile_at(G[:, 1, :, 0:n], i * 4 + b))

        def mlp(l, G, groups, num):
            n = sum(g[2] for g in groups)

            def pe_part(pe):
                for c in range(4):
                    pe_dense(pe, S[f"mlp{l}_up{c}"], HA, N["n1" if l == 0 else "n3"][2])
                    pe_dense(pe, S[f"mlp{l}_down{c}"], G, N[f"mlp{l}_{c}"])

            def act_part(act):
                for c in range(4):
                    act_up(act, S[f"mlp{l}_up{c}"], N[f"mlp{l}_{c}"], G, n)
                    act_ysq(act, S[f"mlp{l}_down{c}"], num, c == 3, n)

            def dve_part(dve):
                for c in range(4):
                    dve_up(dve, S[f"mlp{l}_up{c}"], N[f"mlp{l}_{c}"], G, n)
                    if c == 3:
                        dve_zero_acc(dve, n)
                    dve_y(dve, S[f"mlp{l}_down{c}"], num, c == 0, c == 3, n)
            return pe_part, act_part, dve_part

        pe_mlp0, act_mlp0, dve_mlp0 = mlp(0, GA, GXC, N["r1"])
        pe_mlp1, act_mlp1, dve_mlp1 = mlp(1, G1, GX, N["r3"])

        def pe_mod(pe, st):
            with pe.Fori(0, st.n) as i:
                for b in range(4):
                    pe.wait_ge(loaded[b], plan.loaded(st, i, b))
                    for k in range(KT):
                        mm = pe.matmul(psa[:, 0, bass.ds(i * 8 + 2 * b, 2)], WR[:, b, k, :], SV[:, k, :],
                                       start=(k == 0), stop=(k == KT - 1))
                    mm.then_inc(mod_used, 1)

        def dve_mod(dve, l, st):
            dve.drain()
            dve.wait_ge(mod_used, st.m1)
            for v in range(2):
                dve.tensor_tensor(MOD[:, v, :], psa[:, 0, v:96:2], VT[:, 1, 48 * l:48 * l + 48], ALU.add)
            dve.drain()
            nw = 32 * l
            for v in range(2):
                for w in range(2):
                    dve.scalar_tensor_tensor(out=COEF[:, v, 2 * w, :], in0=MOD[:, v, 24 * w + 8:24 * w + 16], scalar=1.0,
                                             in1=VT[:, 0, nw + 16 * w:nw + 16 * w + 8], op0=ALU.add, op1=ALU.mult)
                    dve.tensor_tensor(COEF[:, v, 2 * w + 1, :], MOD[:, v, 24 * w + 16:24 * w + 24],
                                      VT[:, 0, nw + 16 * w + 8:nw + 16 * w + 16], ALU.mult)
            dve.drain()

        TB, RBB, ACS, ACR, MNB, ZB = (WB[:, j, :] for j in range(6))

        def act_lnsq(act, st, num, last):
            ysq, s, mn, sp = num

            def body(i):
                for b in range(4):
                    if last:
                        act.wait_ge(evac_done, h_of(st, i, b) + 1)
                        act.wait_ge(acc_ready, 8 * s + i * 4 + b)
                        act.activation(TB, tile_at(X[:, :, 0:TX], i * 4 + b), ACT.Square).then_inc(ysq_ready, 1)
                    act_hi(act, st, i, b)
            act_rounds(act, st, body)

        def dve_lnx(dve, st, num, first, last):
            ysq, s, mn, sp = num
            if last:
                dve.drain()
                dve.memset(ACS, 0.0)
                dve.memset(ACR, 0.0)
            with dve.Fori(0, st.n) as i:
                for b in range(4):
                    dve.drain()
                    evac_wait(dve, st, i, b)
                    x = X[:, bass.ds(i * 4 + b, 1), 0:TX].rearrange("p a n -> p (a n)")
                    if first:
                        dve.scalar_tensor_tensor(out=x, in0=x, scalar=ALPHA, in1=psl[:, b % 2, 0, :],
                                                 op0=ALU.mult, op1=ALU.add).then_inc(evac_done, 1)
                    else:
                        dve.tensor_tensor(x, psl[:, b % 2, 0, :], x, ALU.add).then_inc(evac_done, 1)
                    if last:
                        dve.drain()
                        dve.tensor_tensor(ACR, ACR, x, ALU.add)
                        dve.wait_ge(ysq_ready, i * 4 + (ysq + b + 1))
                        dve.tensor_tensor(ACS, ACS, TB, ALU.add).then_inc(acc_ready, 1)

        def pe_ln(pe, num):
            pe.wait_ge(acc_ready, 8 * (num[1] + 1))
            pe.matmul(psa[:, 0, :], ones[:], ACR, start=True, stop=True)
            pe.matmul(psa[:, 1, :], ones[:], ACS, start=True, stop=True).then_inc(stat_ready, 1)

        def act_ln(act, num):
            ysq, s, mn, sp = num
            act.wait_ge(stat_ready, s + 1)
            act.activation(MNB, psa[:, 0, :], ACT.Copy, scale=1.0 / D)
            act.activation(TB, psa[:, 0, :], ACT.Square, scale=1.0 / D).then_inc(mean_ready, 1)
            act.wait_ge(var_ready, mn + 1)
            act.activation(RBB, RBB, ACT.Ln, bias=LN_EPS)
            act.drain()
            act.activation(RBB, RBB, ACT.Exp, scale=-0.5).then_inc(rstd_ready, 1)
            if sp is not None:
                for k in range(KT):
                    act_split(act, sp + k, X_(k, TX), HB[:, 0, k, :])

        def dve_ln(dve, num, l, j):
            ysq, s, mn, sp = num
            dve.wait_ge(mean_ready, mn + 1)
            dve.scalar_tensor_tensor(out=RBB, in0=psa[:, 1, :], scalar=1.0 / D, in1=TB, op0=ALU.mult, op1=ALU.subtract)\
               .then_inc(var_ready, 1)
            dve.wait_ge(rstd_ready, s + 1)
            for k in range(KT + 1):
                if k < KT:
                    x = X_(k, TX)
                    dve.tensor_tensor(x, x, MNB, ALU.subtract)
                    dve.drain()
                    dve.tensor_tensor(x, x, RBB, ALU.mult)
                    dve.drain()
                    g0 = l * 24 + j * 8 + k
                    op = dve.tensor_scalar(x, x, VT[:, 2, g0:g0 + 1], VT[:, 2, 48 + g0:49 + g0], ALU.mult, ALU.add)
                    op.then_inc(split_ready if sp is not None else x_ready, 1)
                if k > 0 and sp is not None:
                    dve_split(dve, sp + k - 1, X_(k - 1, TX), HB[:, 0, k - 1, :], HB[:, 1, k - 1, :])

        def ffn_parts(l):
            g_ready = sem(f"gate_conv{l}")
            gelu_ready = sem(f"gelu{l}")
            num = N[f"ln{l}2"]

            def pe_part(pe):
                for c in range(3):
                    pe_dense(pe, S[f"ffn{l}_in{c}"], HB, N[f"ln{l}1"][3])
                    pe_dense(pe, S[f"ffn{l}_out{c}"], GB, N[f"ffn{l}_{c}"])

            def act_part(act):
                for c in range(3):
                    st = S[f"ffn{l}_in{c}"]

                    def body(i):
                        for t in range(2):
                            tile = i * 2 + t
                            act.wait_ge(g_ready, i * 2 + (8 * c + t + 1))
                            act.activation(WB[:, 1 + t, :], WB[:, 1 + t, :], ACT.Gelu).then_inc(gelu_ready, 1)
                            act_hi(act, st, i, 2 * t)
                            act_split(act, i * 2 + (N[f"ffn{l}_{c}"] + t), WB[:, 3 + t, :], tile_at(GB[:, 0, :, :], tile))
                            act_hi(act, st, i, 2 * t + 1)
                    act_rounds(act, st, body)
                    act_lnsq(act, S[f"ffn{l}_out{c}"], num, c == 2)

            def dve_part(dve):
                for c in range(3):
                    st = S[f"ffn{l}_in{c}"]
                    with dve.Fori(0, st.n) as i:
                        for t in range(2):
                            def wcol(j):
                                return col(VT[:, 3 + l, :], i * 2 + (j * FT2 + 8 * c + t))
                            g, y, z = WB[:, 0, :], WB[:, 1 + t, :], WB[:, 3 + t, :]
                            dve.drain()
                            evac_wait(dve, st, i, 2 * t)
                            dve.tensor_copy(g, psl[:, 0, 0, :]).then_inc(evac_done, 1)
                            dve.drain()
                            dve.tensor_scalar(y, g, wcol(1), wcol(3), ALU.mult, ALU.add)
                            dve.drain()
                            dve.scalar_tensor_tensor(out=y[:, 1:TX], in0=g[:, 0:TX - 1], scalar=wcol(0), in1=y[:, 1:TX],
                                                     op0=ALU.mult, op1=ALU.add)
                            dve.drain()
                            dve.scalar_tensor_tensor(out=y[:, 0:TX - 1], in0=g[:, 1:TX], scalar=wcol(2),
                                                     in1=y[:, 0:TX - 1], op0=ALU.mult, op1=ALU.add).then_inc(g_ready, 1)
                            evac_wait(dve, st, i, 2 * t + 1)
                            dve.wait_ge(gelu_ready, i * 2 + (8 * c + t + 1))
                            dve.tensor_tensor(z, psl[:, 1, 0, :], y, ALU.mult).then_inc(evac_done, 1)
                            dve.drain().then_inc(split_ready, 1)
                            dve_split(dve, i * 2 + (N[f"ffn{l}_{c}"] + t), z, tile_at(GB[:, 0, :, :], i * 2 + t),
                                      tile_at(GB[:, 1, :, :], i * 2 + t))
                    dve_lnx(dve, S[f"ffn{l}_out{c}"], num, c == 0, c == 2)
            return pe_part, act_part, dve_part

        ffn = [ffn_parts(0), ffn_parts(1)]

        def act_conv(act):
            st, sp = S["conv"], N["conv"]

            def body(i):
                act_hi(act, st, i, 0)
                act_hi(act, st, i, 1)
                act_hi(act, st, i, 2)
                act_hi(act, st, i, 3)
                act_split(act, i + sp, Y[:, 3, :], tile_at(GA[:, 0, :, :], i))
            act_rounds(act, st, body)

        def dve_conv(dve):
            st, sp = S["conv"], N["conv"]
            Bt, Ct, U, Z = (Y[:, j, :] for j in range(4))
            with dve.Fori(0, st.n) as i:
                def wcol(j):
                    return col(VT[:, 0, :], i + (64 + 8 * j))
                for b, dst in ((0, Bt), (1, Ct)):
                    dve.drain()
                    evac_wait(dve, st, i, b)
                    for gi, c0, nn in GXC:
                        op = dve.tensor_copy(dst[:, c0:c0 + nn], psl[:, b % 2, gi, 0:nn])
                    op.then_inc(evac_done, 1)
                dve.drain()
                evac_wait(dve, st, i, 2)
                for gi, c0, nn in GXC:
                    op = dve.tensor_tensor(U[:, c0:c0 + nn], psl[:, 0, gi, 0:nn], Ct[:, c0:c0 + nn], ALU.mult)
                op.then_inc(evac_done, 2)
                dve.drain()
                dve.tensor_scalar(Z, U, wcol(1), None, ALU.mult)
                dve.drain()
                Zr = Z[:, 0:TX].rearrange("p (r w) -> p r w", w=GRID_W)
                Ur = U[:, 0:TX].rearrange("p (r w) -> p r w", w=GRID_W)
                for (dz, du, j) in ((slice(1, GRID_W), slice(0, GRID_W - 1), 0), (slice(0, GRID_W - 1), slice(1, GRID_W), 2)):
                    dve.scalar_tensor_tensor(out=Zr[:, :, dz], in0=Ur[:, :, du], scalar=wcol(j), in1=Zr[:, :, dz],
                                             op0=ALU.mult, op1=ALU.add)
                    dve.drain()
                for (dz, du, j) in ((slice(TX + 1, TA), slice(TX, TA - 1), 0), (slice(TX, TA - 1), slice(TX + 1, TA), 2)):
                    dve.scalar_tensor_tensor(out=Z[:, dz], in0=U[:, du], scalar=wcol(j), in1=Z[:, dz],
                                             op0=ALU.mult, op1=ALU.add)
                    dve.drain()
                dve.tensor_tensor(Z, Z, Bt, ALU.mult).then_inc(split_ready, 1)
                dve_split(dve, i + sp, Z, tile_at(GA[:, 0, :, :], i), tile_at(GA[:, 1, :, :], i))

        gate_mm = sem("gate_mm")
        gate_f = sem("gate_f")
        gate_ln = sem("gate_ln")
        gate_m = sem("gate_m")
        gate_e = sem("gate_e")
        gate_t = sem("gate_t")
        gate_c = sem("gate_c")

        def pe_gates(pe):
            pe.wait_ge(wif_in, 64)
            pe.wait_ge(split_ready, N["n2"][2] + KT)
            for gi, c0, n in GXC:
                for k in range(KT):
                    mm = pe.matmul(psa[:, 2 + gi, 0:n], WIF[:, k, :], Y[:, k, c0:c0 + n], start=(k == 0), stop=(k == KT - 1))
            mm.then_inc(gate_mm, 1)
            pe.wait_ge(gate_f, 2)
            for r in range(2):
                for st in range(6):
                    tr = pe.transpose(psa[:, 0, (r * 6 + st) * 8:(r * 6 + st) * 8 + 8], IG[:, r, st * P:st * P + P],
                                      ident[0:8, 0:8])
            tr.then_inc(gate_t, 1)

        def act_gates(act):
            act.wait_ge(gate_f, 1)
            for fn, sc, bi in ((ACT.Abs, 1.0, 0.0), (ACT.Exp, -1.0, 0.0), (ACT.Ln, 1.0, 1.0)):
                for r in range(2):
                    op = act.activation(LF[:, 2 + r, :], LF[:, (0 if fn == ACT.Abs else 2) + r, :], fn, bias=bi, scale=sc)
                if fn != ACT.Ln:
                    act.drain()
            op.then_inc(gate_ln, 1)
            act.wait_ge(gate_m, 1)
            for r in range(2):
                op = act.activation(BR[:, r, 0:TX], LF[:, 2 + r, 0:TX], ACT.Exp, scale=-1.0)
            op.then_inc(gate_e, 1)

        def dve_gates(dve):
            dve.drain()
            dve.wait_ge(gate_mm, 1)
            rows = [IG[:, 0, :], IG[:, 1, :], LF[:, 0, :], LF[:, 1, :]]
            for q in range(4):
                dve.tensor_copy(rows[q][:, 0:TX], psa[32 * q:32 * q + 8, 2, :])
                dve.tensor_copy(rows[q][:, TX:TA], psa[32 * q:32 * q + 8, 3, 0:TC])
            dve.memset(LF[:, 4, :], 0.0)
            dve.drain()
            for q in (0, 1, 2, 3):
                op = dve.tensor_scalar(rows[q], rows[q], SM[0:8, q:q + 1], None, ALU.add)
            op.then_inc(gate_f, 1)
            dve.wait_ge(gate_ln, 1)
            zero = LF[:, 4, :]
            for r in range(2):
                dve.scalar_tensor_tensor(out=LF[:, r, :], in0=LF[:, r, :], scalar=0.0, in1=LF[:, 2 + r, :],
                                         op0=ALU.min, op1=ALU.subtract)
            dve.drain()

            def view(t, r, lo, hi):
                return t[:, lo:hi] if r == 0 else t[:, lo:hi][:, ::-1]

            def last(t, r):
                return t[:, TA - 1:TA] if r == 0 else t[:, TX:TX + 1]

            for r in range(2):
                b = BR[:, r, :]
                dve.tensor_tensor_scan(view(b, r, TX, TA), zero[:, 0:TC], view(LF[:, r, :], r, TX, TA), 0.0, ALU.add, ALU.add)
                dve.drain()
                dve.tensor_tensor_scan(view(b, r, 0, TX), zero[:, 0:TX], view(LF[:, r, :], r, 0, TX), last(b, r),
                                       ALU.add, ALU.add)
            dve.drain()
            op = dve.tensor_tensor(IG[:, :, :], IG[:, :, :], BR[:, :, :], ALU.subtract)
            op.then_inc(gate_f, 1)
            dve.drain()
            for r in range(2):
                g, t = IG[:, r, :], LF[:, 5, :]
                dve.tensor_tensor_scan(view(t, r, TX, TA), zero[:, 0:TC], view(g, r, TX, TA), 0.0, ALU.add, ALU.max)
                dve.drain()
                dve.tensor_tensor_scan(view(MROW[:, r, :], r, 0, TX), zero[:, 0:TX], view(g, r, 0, TX), last(t, r),
                                       ALU.add, ALU.max)
                dve.drain()
                op = dve.tensor_tensor(LF[:, 2 + r, 0:TX], BR[:, r, 0:TX], MROW[:, r, :], ALU.add)
                dve.drain()
            dve.drain().then_inc(gate_m, 1)
            dve.wait_ge(gate_t, 1)
            dve.tensor_copy(GCOL[:, :, :, :].rearrange("p r s h -> p (r s h)"), psa[:, 0, 0:96]).then_inc(gate_c, 1)
            dve.wait_ge(gate_e, 1)

        ml_vt = sem("ml_v_transposed")
        ml_vk = sem("ml_v_ready")
        ml_sig = sem("ml_gate_exp")
        ml_rows = sem("ml_rows")
        ml_mb = sem("ml_rows_spread")
        ml_me = sem("ml_mneg_ready")
        ml_s = sem("ml_scores")
        ml_e = sem("ml_weights")
        ml_p = sem("ml_weighted")
        ml_pv = sem("ml_summed")
        ml_h = sem("ml_h_ready")
        ml_hq = sem("ml_h_squared")
        ml_hs = sem("ml_h_ssq")
        ml_hr = sem("ml_h_rstd")
        SEQ = [4, 5, 0, 1, 2, 3]

        def span(st, r):
            if st >= 4:
                return 0, TX
            return (P * st, TX) if r == 0 else (0, P * (st + 1))

        def vtok(a_, st):
            c = a_ * 6 + st
            return X[:, c // 2, TX + (c % 2) * P:TX + (c % 2) * P + P]

        def pe_mlstm(pe):
            st_, sp = S["mlstm"], N["mlstm"]
            numden = [(psa[:, 2, :], psa[:, 3, :]), (psl[:, 1, 0, :], psl[:, 1, 1, :])]
            pe.wait_ge(gate_c, 1)
            with pe.Fori(0, st_.n) as i:
                pe.wait_ge(split_done, i * 2 + sp)
                for b in range(6):
                    pe_unit(pe, st_, i, b, HA, N["n2"][2] if b == 0 else None)
                    if b in (3, 4):
                        pe.wait_ge(evac_done, h_of(st_, i, b - 1) + 1)
                        for st in range(6):
                            tr = pe.transpose(psa[:, st // 4, (st % 4) * P:(st % 4) * P + P], MV[:, st * P:st * P + P], ident[:])
                        tr.then_inc(ml_vt, 1)
                pe.wait_ge(evac_done, i * 8 + (st_.h0 + 8))
                pe.wait_ge(ml_vk, i * 2 + 2)
                for a_ in range(2):
                    lo = 64 * a_
                    pe.wait_ge(split_done, i * 2 + (sp + a_))
                    pe.wait_ge(ml_rows, i * 4 + (2 * a_ + 1))
                    for r in range(2):
                        mm = pe.matmul(psl[:, 0, r, :], ones[0:8, :], RH[:, r, :], start=True, stop=True)
                    mm.then_inc(ml_mb, 1)

                    def scores(n):
                        if n >= 2:
                            pe.wait_ge(ml_p, i * 24 + (12 * a_ + 2 * (n - 1)))
                        pe.matmul(psa[:, n % 2, :], MK[lo:lo + 64, SEQ[n] * P:SEQ[n] * P + P], MQ[lo:lo + 64, :],
                                  start=True, stop=True).then_inc(ml_s, 1)

                    scores(0)
                    for n in range(6):
                        if n < 5:
                            scores(n + 1)
                        for r in range(2):
                            t0, t1 = span(SEQ[n], r)
                            pe.wait_ge(ml_p, i * 24 + (12 * a_ + 2 * n + r + 1))
                            pe.matmul(numden[r][0][:, t0:t1], vtok(a_, SEQ[n]), ME[:, r, t0:t1], start=(n == 0),
                                      stop=(n == 5), skip_group_check=True)
                            mm = pe.matmul(numden[r][1][:, t0:t1], ones[:], ME[:, r, t0:t1], start=(n == 0),
                                           stop=(n == 5), skip_group_check=True)
                        mm.then_inc(ml_pv, 1)
                    pe.wait_ge(ml_rows, i * 4 + (2 * a_ + 2))
                    for r in range(2):
                        mm = pe.matmul(psl[:, 0, r, :], ones[0:8, :], RH[:, r, :], start=True, stop=True)
                    mm.then_inc(ml_mb, 1)
                    pe.wait_ge(ml_hq, i * 2 + (a_ + 1))
                    pe.matmul(psa[:, 0, :], ones[:], ME[:, 0, :], start=True, stop=True).then_inc(ml_hs, 1)

        def act_mlstm(act):
            st_, sp = S["mlstm"], N["mlstm"]

            def body(i):
                for b in range(8):
                    act_hi(act, st_, i, b)
                act.wait_ge(evac_done, i * 8 + (st_.h0 + 8))
                act.activation(MO[:, :, :], MO[:, :, :], ACT.Exp, scale=-1.0).then_inc(ml_sig, 1)
                for a_ in range(2):
                    act.wait_ge(ml_me, i * 2 + (a_ + 1))
                    for n in range(6):
                        st = SEQ[n]
                        act.wait_ge(ml_pv, i * 12 + (6 * a_ + n + 1))
                        for r in range(2):
                            g = GCOL[:, r, st, bass.ds(i * 2 + a_, 1)]
                            if st >= 4:
                                op = act.activation(ME[:, r, :], psl[:, 0, r, :], ACT.Exp, bias=g, scale=-1.0)
                            else:
                                d0 = st * P
                                t0, t1 = (d0 + P, TX) if r == 0 else (0, d0)
                                if t1 > t0:
                                    act.activation(ME[:, r, t0:t1], psl[:, 0, r, t0:t1], ACT.Exp, bias=g, scale=-1.0)
                                op = act.activation(ME[:, r, d0:d0 + P], MM[:, r, d0:d0 + P], ACT.Exp, bias=g)
                            op.then_inc(ml_e, 1)
                    act.wait_ge(ml_h, i * 2 + (a_ + 1))
                    act.activation(ME[:, 0, :], HS[:, :], ACT.Square).then_inc(ml_hq, 1)
                    act.wait_ge(ml_hs, i * 2 + (a_ + 1))
                    act.activation(MM[:, 0, :], psa[:, 0, :], ACT.Ln, bias=EPS, scale=1.0 / P)
                    act.drain()
                    act.activation(MM[:, 0, :], MM[:, 0, :], ACT.Exp, scale=-0.5).then_inc(ml_hr, 1)
                    act_split(act, i * 2 + (sp + a_), MT[:, :], tile_at(G1[:, 0, :, :], i * 2 + a_))
            act_rounds(act, st_, body)

        def dve_mlstm(dve):
            st_, sp = S["mlstm"], N["mlstm"]
            numden = [(psa[:, 2, :], psa[:, 3, :]), (psl[:, 1, 0, :], psl[:, 1, 1, :])]
            with dve.Fori(0, st_.n) as i:
                dve.drain()
                evac_wait(dve, st_, i, 0)
                dve.tensor_scalar(MQ[:, :], psl[:, 0, 0, :], 64 ** -0.5, None, ALU.mult).then_inc(evac_done, 1)
                for b, dst in ((1, MK), (2, MV), (3, MV)):
                    if b == 3:
                        take_values(dve, i, 0)
                    evac_wait(dve, st_, i, b)
                    dve.tensor_copy(dst[:, 0:TX], psl[:, b % 2, 0, :])
                    dve.tensor_copy(dst[:, TX:TA], psl[:, b % 2, 1, 0:TC]).then_inc(evac_done, 1)
                for b in (4, 5):
                    evac_wait(dve, st_, i, b)
                    dve.tensor_copy(MO[:, b - 4, :], psl[:, b % 2, 0, :]).then_inc(evac_done, st_.inc[b])
                take_values(dve, i, 1)
                dve.wait_ge(ml_sig, i + 1)
                dve.tensor_scalar(MO[:, :, :], MO[:, :, :], 1.0, None, ALU.add)
                dve.drain()
                dve.reciprocal(MO[:, :, :], MO[:, :, :])
                for a_ in range(2):
                    onehot = ident[0:8, bass.ds(i * 2 + a_, 1)]
                    dve.tensor_scalar(RH[:, :, :], MROW[:, :, :], onehot, None, ALU.mult).then_inc(ml_rows, 1)
                    dve.wait_ge(ml_mb, i * 4 + (2 * a_ + 1))
                    for r in range(2):
                        op = dve.scalar_tensor_tensor(
                            out=MM[:, r, :].rearrange("p (a n) -> p a n", a=4),
                            in0=psl[:, 0, r, :].rearrange("p (a n) -> p a n", a=4), scalar=-1.0,
                            in1=MASK[:, r:r + 1, :].to_broadcast([P, 4, P]), op0=ALU.mult, op1=ALU.add)
                    op.then_inc(ml_me, 1)
                    for n in range(6):
                        dve.wait_ge(ml_s, i * 12 + (6 * a_ + n + 1))
                        for r in range(2):
                            t0, t1 = span(SEQ[n], r)
                            dve.wait_ge(ml_e, i * 24 + (12 * a_ + 2 * n + r + 1))
                            dve.tensor_tensor(ME[:, r, t0:t1], psa[:, n % 2, t0:t1], ME[:, r, t0:t1], ALU.mult)\
                               .then_inc(ml_p, 1)
                    dve.tensor_scalar(RH[:, :, :], BR[:, :, 0:TX], onehot, None, ALU.mult).then_inc(ml_rows, 1)
                    dve.wait_ge(ml_mb, i * 4 + (2 * a_ + 2))
                    dve.wait_ge(ml_pv, i * 12 + (6 * a_ + 7))
                    for r in range(2):
                        num, den = numden[r]
                        if r == 1:
                            dve.drain()
                        dve.tensor_copy(RD[:, :], den)
                        dve.drain()
                        dve.scalar_tensor_tensor(out=RD[:, :], in0=RD[:, :], scalar=-1.0, in1=RD[:, :], op0=ALU.mult,
                                                 op1=ALU.max)
                        dve.drain()
                        dve.tensor_tensor(RD[:, :], RD[:, :], psl[:, 0, r, :], ALU.max)
                        dve.drain()
                        dve.reciprocal(RD[:, :], RD[:, :])
                        dve.drain()
                        if r == 0:
                            dve.tensor_tensor(HS[:, :], num, RD[:, :], ALU.mult)
                        else:
                            dve.tensor_tensor(MT[:, :], num, RD[:, :], ALU.mult)
                            dve.drain()
                            dve.tensor_tensor(HS[:, :], HS[:, :], MT[:, :], ALU.add).then_inc(ml_h, 1)
                    dve.drain()
                    dve.wait_ge(ml_hr, i * 2 + (a_ + 1))
                    dve.tensor_tensor(MT[:, :], HS[:, :], MM[:, 0, :], ALU.mult)
                    dve.drain()
                    dve.scalar_tensor_tensor(out=MT[:, :], in0=MT[:, :], scalar=col(VT[:, 0, :], i * 2 + (88 + a_)),
                                             in1=MO[:, a_, :], op0=ALU.mult, op1=ALU.mult).then_inc(split_ready, 1)
                    dve_split(dve, i * 2 + (sp + a_), MT[:, :], tile_at(G1[:, 0, :, :], i * 2 + a_),
                              tile_at(G1[:, 1, :, :], i * 2 + a_))

        def take_values(dve, i, a_):
            dve.drain()
            dve.wait_ge(ml_vt, i * 2 + (a_ + 1))
            dve.tensor_copy(X[:, 3 * a_:3 * a_ + 3, TX:TA],
                            psa[:, 0:2, :].rearrange("p a n -> p (a n)")[:, 0:768].rearrange("p (a n) -> p a n", n=2 * P))\
               .then_inc(ml_vk, 1)

        mem_tr = sem("mem_transposed")
        mem_f = sem("mem_f_ready")

        def pe_mem(pe):
            pe.wait_ge(mem_in, 16)
            for k in range(KT):
                for t in range(2):
                    o = (k * 2 + t) * P
                    tr = pe.transpose(psa[:, o // 512, o % 512:o % 512 + P], MEMT[:, t, k * P:k * P + P], ident[:])
            tr.then_inc(mem_tr, 1)

        def dve_mem(dve):
            dve.drain()
            dve.wait_ge(mem_tr, 1)
            dve.tensor_copy(MEMF[:, :, :].rearrange("p k n -> p (k n)"), psa[:, :, :].rearrange("p a n -> p (a n)"))
            dve.drain()
            for k in range(KT):
                dve.drain().then_inc(split_ready, 1)
                dve_split(dve, N["mem"] + k, MEMF[:, k, :], MEMH[:, 0, k, :], MEMH[:, 1, k, :])

        def act_mem(act):
            for k in range(KT):
                act_split(act, N["mem"] + k, MEMF[:, k, :], MEMH[:, 0, k, :])

        lam_b = sem("lam_spread")
        lam_s = sem("lam_sums")
        lam_e = sem("lam_exp")
        dist_i = sem("dist_iota")
        df_vt = sem("df_v_transposed")
        df_vk = sem("df_v_ready")
        df_s = sem("df_scores")
        df_u = sem("df_scores_used")
        df_m = sem("df_max")
        df_e = sem("df_exp")
        df_a = sem("df_attn")
        df_t = sem("df_attn_transposed")
        df_c = sem("df_attn_copied")
        df_p = sem("df_out")
        df_q = sem("df_squared")
        df_z = sem("df_ssq")
        df_r = sem("df_rstd")

        def pe_lam(pe):
            pe.wait_ge(lam_in, 16)
            pe.matmul(psl[:, 0, 1, 0:256], ones[0:1, :], AT[0:1, 0, 0:256], start=True, stop=True).then_inc(lam_b, 1)

        def act_lam(act):
            act.wait_ge(lam_s, 1)
            act.activation(SM[:, 8:10], SM[:, 6:8], ACT.Exp).then_inc(lam_e, 1)

        def dve_lam(dve):
            dve.wait_ge(lam_b, 1)
            dve.tensor_copy(AT[:, 1, 0:256], psl[:, 0, 1, 0:256])
            dve.drain()
            for j in range(2):
                dve.tensor_tensor(AT[:, 2, j * 64:j * 64 + 64], AT[:, 1, j * 128:j * 128 + 64],
                                  AT[:, 1, j * 128 + 64:j * 128 + 128], ALU.mult)
            dve.drain()
            dve.tensor_reduce(SM[:, 6:8], AT[:, 2, 0:128].rearrange("p (a n) -> p a n", a=2), AXX, ALU.add)\
               .then_inc(lam_s, 1)
            dve.wait_ge(lam_e, 1)
            dve.tensor_tensor(SM[:, 10:11], SM[:, 9:10], SM[:, 8:9], ALU.subtract)
            dve.drain()
            dve.tensor_scalar(SM[:, 10:11], SM[:, 10:11], -LAMBDA_INIT, None, ALU.add)
            dve.tensor_scalar(SM[:, 11:12], VT[:, 0, 112:113], 1.0 - LAMBDA_INIT, None, ALU.mult)
            dve.wait_ge(dist_i, 1)
            dve.tensor_copy(DIST[:, :], DISTI[:, :])
            dve.drain()
            dve.scalar_tensor_tensor(out=DIST[:, :], in0=DIST[:, :], scalar=-1.0, in1=DIST[:, :], op0=ALU.mult, op1=ALU.max)
            dve.drain()

        def pe_diff(pe):
            st_, sp = S["diff"], N["mix0"]
            with pe.Fori(0, st_.n) as i:
                for b in range(3):
                    pe_unit(pe, st_, i, b, HB, N["xb"] if b == 0 else None)
                pe.wait_ge(split_done, i + sp)
                pe.wait_ge(evac_done, i * 4 + (st_.h0 + 4))
                for t in range(4):
                    tr = pe.transpose(psl[:, 0, 1, t * P:t * P + P], AV[:, t * P:t * P + P], ident[:])
                tr.then_inc(df_vt, 1)

                def scores(t):
                    if t >= 2:
                        pe.wait_ge(df_u, i * 8 + 2 * (t - 1))
                    for c in range(2):
                        pe.matmul(psa[:, 2 * (t % 2) + c, :], AQ[64 * c:64 * c + 64, 0, t * P:t * P + P],
                                  AK[64 * c:64 * c + 64, 0, :], start=True, stop=True).then_inc(df_s, 1)

                scores(0)
                scores(1)
                for t in range(4):
                    pe.wait_ge(df_a, i * 4 + (t + 1))
                    if t >= 1:
                        pe.wait_ge(df_c, i * 4 + t)
                    for kt in range(4):
                        tr = pe.transpose(psl[:, 1, 1, kt * P:kt * P + P], DS[:, t % 2, 0, kt * P:kt * P + P], ident[:])
                    tr.then_inc(df_t, 1)
                    if t + 2 < 4:
                        scores(t + 2)
                pe.wait_ge(df_vk, i + 1)
                pe.wait_ge(df_c, i * 4 + 4)
                for kt in range(4):
                    mm = pe.matmul(psl[:, 0, 1, :], VTK[:, kt, :], AT[:, kt, :], start=(kt == 0), stop=(kt == 3))
                mm.then_inc(df_p, 1)
                pe.wait_ge(df_q, i + 1)
                pe.matmul(psa[:, 0, :], ones[:], TB, start=True, stop=True).then_inc(df_z, 1)

        def act_diff(act):
            st_, sp = S["diff"], N["mix0"]

            def body(i):
                for b in range(4):
                    act_hi(act, st_, i, b)
                act.wait_ge(df_vt, i + 1)
                act.activation(VTK[:, :, :].rearrange("p a n -> p (a n)"), psl[:, 0, 1, :], ACT.Copy).then_inc(df_vk, 1)

                def expo(t):
                    for c in range(2):
                        act.wait_ge(df_m, i * 4 + (t + 1))
                        act.activation(DS[:, t % 2, c, :], DS[:, t % 2, c, :], ACT.Exp, bias=DST[:, t, 1, c:c + 1],
                                       accum_out=DST[:, t, 2, c:c + 1]).then_inc(df_e, 1)

                def copy(t):
                    act.wait_ge(df_t, i * 4 + (t + 1))
                    act.activation(AT[:, :, t * P:t * P + P], psl[:, 1, 1, :].rearrange("p (a n) -> p a n", a=4), ACT.Copy)\
                       .then_inc(df_c, 1)

                expo(0)
                expo(1)
                copy(0)
                expo(2)
                copy(1)
                expo(3)
                copy(2)
                copy(3)
                act.wait_ge(df_p, i + 1)
                act.activation(TB, psl[:, 0, 1, :], ACT.Square).then_inc(df_q, 1)
                act.wait_ge(df_z, i + 1)
                act.activation(RBB, psa[:, 0, :], ACT.Ln, bias=LN_EPS, scale=1.0 / P)
                act.drain()
                act.activation(RBB, RBB, ACT.Exp, scale=-0.5).then_inc(df_r, 1)
                act_split(act, i + sp, ZB, tile_at(GB[:, 0, :, :], i))
            act_rounds(act, st_, body)

        def dve_diff(dve):
            st_, sp = S["diff"], N["mix0"]
            with dve.Fori(0, st_.n) as i:
                dve.drain()
                evac_wait(dve, st_, i, 0)
                dve.tensor_scalar(AQ[:, 0, :], psl[:, 0, 0, :], 64 ** -0.5, None, ALU.mult).then_inc(evac_done, 1)
                evac_wait(dve, st_, i, 1)
                dve.tensor_copy(AK[:, 0, :], psl[:, 1, 0, :]).then_inc(evac_done, 1)
                evac_wait(dve, st_, i, 2)
                dve.tensor_copy(AV[:, :], psl[:, 0, 0, :]).then_inc(evac_done, 2)
                dve.tensor_scalar(SB[:, :], DIST[:, :], col(SLOPE[:, :], i), None, ALU.mult)

                def bias_max(t):
                    if t >= 2:
                        dve.wait_ge(df_t, i * 4 + (t - 1))
                    off = 384 - t * P
                    dve.wait_ge(df_s, i * 8 + (2 * t + 2))
                    dve.tensor_copy(DST[:, t, 3, :], SM[:, 12:14])
                    dve.drain()
                    for c in range(2):
                        dve.tensor_tensor_reduce(DS[:, t % 2, c, :], psa[:, 2 * (t % 2) + c, :], SB[:, off:off + TX], 1.0,
                                                 -3e38, ALU.add, ALU.max, DST[:, t, 0, c:c + 1]).then_inc(df_u, 1)
                    dve.drain()
                    dve.tensor_scalar(DST[:, t, 1, :], DST[:, t, 0, :], -1.0, None, ALU.mult).then_inc(df_m, 1)

                def combine(t):
                    dve.wait_ge(df_e, i * 8 + (2 * t + 2))
                    dve.reciprocal(DST[:, t, 3, :], DST[:, t, 2, :])
                    dve.drain()
                    dve.tensor_scalar(DST[:, t, 3, 1:2], DST[:, t, 3, 1:2], SM[:, 10:11], None, ALU.mult)
                    dve.tensor_scalar(DS[:, t % 2, 0, :], DS[:, t % 2, 0, :], DST[:, t, 3, 0:1], None, ALU.mult)
                    dve.drain()
                    dve.scalar_tensor_tensor(out=DS[:, t % 2, 0, :], in0=DS[:, t % 2, 1, :], scalar=DST[:, t, 3, 1:2],
                                             in1=DS[:, t % 2, 0, :], op0=ALU.mult, op1=ALU.add).then_inc(df_a, 1)

                bias_max(0)
                for t in range(4):
                    if t == 0:
                        bias_max(1)
                    combine(t)
                    if t + 2 < 4:
                        bias_max(t + 2)
                dve.wait_ge(df_r, i + 1)
                dve.tensor_tensor(ZB, psl[:, 0, 1, :], RBB, ALU.mult)
                dve.drain()
                dve.tensor_scalar(ZB, ZB, SM[:, 11:12], None, ALU.mult).then_inc(split_ready, 1)
                dve_split(dve, i + sp, ZB, tile_at(GB[:, 0, :, :], i), tile_at(GB[:, 1, :, :], i))

        def xatt_parts(l):
            vt, vk, xs, xm, xe, xa, xt, xc, xp, xz = (sem(f"xa{l}_{n}") for n in
                ("v_transposed", "v_ready", "scores", "max", "exp", "probs", "probs_transposed", "probs_copied",
                 "out", "out_taken"))
            st_, sp = S[f"xatt{l}"], N[f"xatt{l}"]
            XS = DS[:, 0, :, :].rearrange("p a n -> p (a n)").rearrange("p (t m) -> p t m", t=4)
            STT = DST[:, :, :, :].rearrange("p a b c -> p (a b c)")
            V2 = AV[:, :].rearrange("p (e m) -> p e m", e=2)
            VK = VTK[:, :, :].rearrange("p a n -> p (a n)").rearrange("p (m n) -> p m n", m=2)

            def pe_part(pe):
                with pe.Fori(0, st_.n) as i:
                    for b in range(6):
                        if b < 4:
                            pe_unit(pe, st_, i, b, MEMH, N["mem"] if b == 0 else None)
                        else:
                            pe_unit(pe, st_, i, b, HB, N[f"ln{l}0"][3] if b == 4 else None)
                    pe.wait_ge(split_done, i * 2 + sp)
                    pe.wait_ge(evac_done, i * 8 + (st_.h0 + 8))
                    for m in range(2):
                        for e in range(2):
                            tr = pe.transpose(psl[:, 0, 1, (m * 2 + e) * P:(m * 2 + e) * P + P],
                                              AV[:, e * TM + m * P:e * TM + m * P + P], ident[:])
                    tr.then_inc(vt, 1)
                    for t in range(4):
                        for e in range(2):
                            mm = pe.matmul(psa[:, t, 0:TM], AQ[:, e, t * P:t * P + P], AK[:, e, 0:TM], start=(e == 0),
                                           stop=(e == 1))
                        mm.then_inc(xs, 1)
                    pe.wait_ge(vk, i + 1)
                    for t in range(4):
                        pe.wait_ge(xa, i * 4 + (t + 1))
                        if t >= 2:
                            pe.wait_ge(xc, i * 4 + (t - 1))
                        for m in range(2):
                            tr = pe.transpose(psl[:, t % 2, 1, m * P:m * P + P], XS[:, t, m * P:m * P + P], ident[:])
                        tr.then_inc(xt, 1)
                    pe.wait_ge(xc, i * 4 + 4)
                    for e in range(2):
                        for m in range(2):
                            mm = pe.matmul(psa[:, e, :], VK[:, m, e * P:e * P + P], AT[:, m, :], start=(m == 0), stop=(m == 1))
                        mm.then_inc(xp, 1)

            def act_part(act):
                def body(i):
                    for b in range(8):
                        act_hi(act, st_, i, b)
                    act.wait_ge(vt, i + 1)
                    act.activation(VTK[:, :, :].rearrange("p a n -> p (a n)"), psl[:, 0, 1, :], ACT.Copy).then_inc(vk, 1)
                    for t in range(4):
                        act.wait_ge(xm, i * 4 + (t + 1))
                        act.activation(XS[:, t, :], psa[:, t, 0:TM], ACT.Exp, bias=STT[:, 4 + t:5 + t],
                                       accum_out=STT[:, 8 + t:9 + t]).then_inc(xe, 1)
                    for t in range(4):
                        act.wait_ge(xt, i * 4 + (t + 1))
                        act.activation(AT[:, 0:2, t * P:t * P + P],
                                       psl[:, t % 2, 1, 0:2 * P]
                                       .rearrange("p (a n) -> p a n", a=2), ACT.Copy).then_inc(xc, 1)
                    for e in range(2):
                        act_split(act, i * 2 + (sp + e), WB[:, e, :], tile_at(GB[:, 0, :, :], i * 2 + e))
                act_rounds(act, st_, body)

            def dve_part(dve):
                with dve.Fori(0, st_.n) as i:
                    for b in range(6):
                        if b == 0:
                            dve.drain()
                        evac_wait(dve, st_, i, b)
                        if b < 2:
                            op = dve.tensor_copy(AK[:, b, 0:TM], psl[:, b % 2, 0, 0:TM])
                        elif b < 4:
                            op = dve.tensor_copy(V2[:, b - 2, :], psl[:, b % 2, 0, 0:TM])
                        else:
                            op = dve.tensor_scalar(AQ[:, b - 4, :], psl[:, b % 2, 0, :], 256 ** -0.5, None, ALU.mult)
                        op.then_inc(evac_done, st_.inc[b])
                    for t in range(4):
                        dve.wait_ge(xs, i * 4 + (t + 1))
                        dve.tensor_reduce(STT[:, t:t + 1], psa[:, t, 0:TM], AXX, ALU.max)
                        dve.drain()
                        dve.tensor_scalar(STT[:, 4 + t:5 + t], STT[:, t:t + 1], -1.0, None, ALU.mult).then_inc(xm, 1)
                    for t in range(4):
                        dve.wait_ge(xe, i * 4 + (t + 1))
                        dve.reciprocal(STT[:, 12 + t:13 + t], STT[:, 8 + t:9 + t])
                        dve.drain()
                        dve.tensor_scalar(XS[:, t, :], XS[:, t, :], STT[:, 12 + t:13 + t], None, ALU.mult).then_inc(xa, 1)
                    for e in range(2):
                        dve.wait_ge(xp, i * 2 + (e + 1))
                        dve.tensor_copy(WB[:, e, :], psa[:, e, :]).then_inc(split_ready, 1)
                    for e in range(2):
                        dve_split(dve, i * 2 + (sp + e), WB[:, e, :], tile_at(GB[:, 0, :, :], i * 2 + e),
                                  tile_at(GB[:, 1, :, :], i * 2 + e))
            return pe_part, act_part, dve_part

        xatt = [xatt_parts(0), xatt_parts(1)]

        dl_i = sem("dl_iota")
        dl_mf = sem("dl_mask_float")
        dl_mk = sem("dl_mask")
        dl_vt = sem("dl_v_transposed")
        dl_vk = sem("dl_v_ready")
        dl_s = sem("dl_scores")
        dl_m = sem("dl_max")
        dl_e = sem("dl_exp")
        dl_t = sem("dl_p_transposed")
        dl_c = sem("dl_p_copied")
        dl_o = sem("dl_out")
        dl_q = sem("dl_out_taken")
        dl_x = sem("dl_rows_transposed")
        dl_y = sem("dl_rows_taken")
        dl_w1 = sem("dl_row_diff")
        dl_w2 = sem("dl_row_exp")
        dl_rw = sem("dl_rows_ready")
        dl_b = sem("dl_rows_spread")
        DIL = [1, 4, 16]
        LW = [2 * P, P, P]
        LOFF = [0, 384, 512]
        WIN = [0, 64, 192, 256]

        def perm(ap, g):
            if g == 0:
                return ap
            return ap.rearrange("p (u r) -> p r u", r=DIL[g])

        def ordered(ap, g):
            if g == 0:
                return ap
            return ap.rearrange("p (r u) -> p r u", r=DIL[g])

        def vkeys(g, t, ch):
            c = 2 * t + ch if g == 0 else t
            return X[:, c // 2, TX + (c % 2) * P:TX + (c % 2) * P + P]

        def table(g, t):
            if g == 0:
                delta = t * P - WIN[t]
                return LSB[:, P - delta:P - delta + 2 * P]
            return LSB[:, LOFF[g]:LOFF[g] + P]

        def pe_dil(pe):
            st_ = S["dil"]
            with pe.Fori(0, st_.n) as i:
                for g in range(3):
                    for j in range(3):
                        pe_unit(pe, st_, i, 4 * g + j, HB, N["ln02"][3] if g == 0 and j == 0 else None)
                    nch = 8 if g == 0 else 4
                    pe.wait_ge(evac_done, i * 12 + (st_.h0 + 4 * g + 4))
                    pe.wait_ge(dl_q, i * 3 + (g + 1))
                    for c in range(nch):
                        t0 = WIN[c // 2] + (c % 2) * P if g == 0 else c * P
                        tr = pe.transpose(psl[:, c // 4, 1, (c % 4) * P:(c % 4) * P + P], LQ[:, 2, t0:t0 + P], ident[:])
                    tr.then_inc(dl_vt, 1)
                    pe.wait_ge(dl_vk, i * 3 + (g + 1))
                    w = LW[g]
                    nt = 8 if g == 0 else 4
                    for a_ in range(2):
                        lo = 64 * a_
                        n6 = 2 * g + a_
                        pe.wait_ge(dl_c, i * 6 + (n6 + 1))
                        for t in range(4):
                            k0 = WIN[t] if g == 0 else t * P
                            mm = pe.matmul(psa[:, (t * w) // 512, (t * w) % 512:(t * w) % 512 + w],
                                           LQ[lo:lo + 64, 0, t * P:t * P + P], LQ[lo:lo + 64, 1, k0:k0 + w],
                                           start=True, stop=True)
                        mm.then_inc(dl_s, 1)
                        pe.wait_ge(dl_e, i * 6 + (n6 + 1))
                        for c in range(nt):
                            tr = pe.transpose(psa[:, 2 + c // 4, (c % 4) * P:(c % 4) * P + P], LP[:, c * P:c * P + P], ident[:])
                        tr.then_inc(dl_t, 1)
                        pe.wait_ge(dl_c, i * 6 + (n6 + 2))
                        for t in range(4):
                            for ch in range(2 if g == 0 else 1):
                                c = 2 * t + ch if g == 0 else t
                                mm = pe.matmul(psl[lo:lo + 64, 0, 1, t * P:t * P + P], vkeys(g, t, ch)[:, lo:lo + 64],
                                               LPT[:, c, :], start=(ch == 0), stop=(ch == (1 if g == 0 else 0)),
                                               skip_group_check=True)
                        mm.then_inc(dl_o, 1)
            pe.wait_ge(dl_q, 3 * HEADS + 1)
            for q in range(2):
                for g in range(3):
                    if q == 1:
                        pe.wait_ge(dl_y, 1)
                    for t in range(4):
                        tr = pe.transpose(psa[0:16, g, t * P:t * P + P], LMS[:, q, g, t, :], ident[:])
                tr.then_inc(dl_x, 1)
            pe.wait_ge(dl_mk, 2)
            for i in range(HEADS):
                if i == 0:
                    pe.wait_ge(dl_rw, 1)
                else:
                    pe.wait_ge(split_ready, N["mix1"] + i)
                for g in range(3):
                    mm = pe.matmul(psa[:, g, :], LSEL[:, i, :], LROW[:, g, :], start=True, stop=True)
                mm.then_inc(dl_b, 1)

        def act_dil(act):
            st_ = S["dil"]

            def body(i):
                for g in range(3):
                    for b in range(4):
                        act_hi(act, st_, i, 4 * g + b)
                    nch = 8 if g == 0 else 4
                    act.wait_ge(dl_vt, i * 3 + (g + 1))
                    for h in range(nch // 4):
                        op = act.activation(X[:, 2 * h:2 * h + 2, TX:TA],
                                            psl[:, h, 1, :].rearrange("p (a n) -> p a n", a=2), ACT.Copy)
                    op.then_inc(dl_vk, 1)
                    w = LW[g]
                    for a_ in range(2):
                        n6 = 2 * g + a_
                        act.wait_ge(dl_m, i * 6 + (n6 + 1))
                        for t in range(4):
                            hcol = bass.ds(i * 2 + a_, 1)
                            op = act.activation(LP[:, t * w:t * w + w], LP[:, t * w:t * w + w], ACT.Exp,
                                                bias=SM[:, 16 + t:17 + t], accum_out=LMS[:, 1, g, t, hcol])
                        op.then_inc(dl_e, 1)
                        act.wait_ge(dl_t, i * 6 + (n6 + 1))
                        nt = 8 if g == 0 else 4
                        act.activation(LPT[:, 0:nt, :].rearrange("p a n -> p (a n)"),
                                       psa[:, 2:2 + nt // 4, :].rearrange("p a n -> p (a n)"), ACT.Copy).then_inc(dl_c, 1)
            act_rounds(act, st_, body)
            act.wait_ge(dl_w1, 1)
            act.activation(LROW[:, 0:3, :], LROW[:, 0:3, :], ACT.Exp).then_inc(dl_w2, 1)
            for i in range(KT):
                act_split(act, N["mix1"] + i, LP[:, 0:TX], HB[:, 0, i, :])

        def dve_dil(dve):
            st_ = S["dil"]
            dve.wait_ge(dl_i, 1)
            dve.tensor_copy(LB[:, :], LBI[:, :])
            dve.drain()
            dve.scalar_tensor_tensor(out=LB[:, :], in0=LB[:, :], scalar=-1.0, in1=LB[:, :], op0=ALU.mult, op1=ALU.max)
            dve.drain()
            dve.drain().then_inc(dl_mf, 1)
            dve.wait_ge(dl_mk, 1)
            with dve.Fori(0, st_.n) as i:
                for g in range(3):
                    for j in range(3):
                        dve.drain()
                        evac_wait(dve, st_, i, 4 * g + j)
                        src, dst = perm(psl[:, j % 2, 0, :], g), ordered(LQ[:, j, :], g)
                        if j == 0:
                            op = dve.tensor_scalar(dst, src, 64 ** -0.5, None, ALU.mult)
                        else:
                            op = dve.tensor_copy(dst, src)
                        op.then_inc(evac_done, st_.inc[4 * g + j])
                    w = LW[g]
                    for a_ in range(2):
                        n6 = 2 * g + a_
                        dve.drain()
                        if g == 0:
                            dve.tensor_scalar(LSB[:, 0:384], LB[:, 0:384],
                                              LSL[:, bass.ds(i * 2 + a_, 1)], None, ALU.mult)
                        else:
                            dve.tensor_scalar(LSB[:, LOFF[g]:LOFF[g] + P], LB[:, LOFF[g]:LOFF[g] + P],
                                              LSL[:, bass.ds(i * 2 + a_, 1)], None, ALU.mult)
                        dve.drain()
                        dve.wait_ge(dl_s, i * 6 + (n6 + 1))
                        for t in range(4):
                            dve.tensor_tensor(LP[:, t * w:t * w + w], psa[:, (t * w) // 512, (t * w) % 512:(t * w) % 512 + w],
                                              table(g, t), ALU.add)
                        dve.drain()
                        dve.tensor_reduce(SM[:, 20:24], LP[:, 0:4 * w].rearrange("p (t w) -> p t w", t=4), AXX, ALU.max)
                        dve.drain()
                        dve.tensor_copy(LMS[:, 0, g, :, bass.ds(i * 2 + a_, 1)].rearrange("p t a -> p (t a)"), SM[:, 20:24])
                        dve.tensor_scalar(SM[:, 16:20], SM[:, 20:24], -1.0, None, ALU.mult).then_inc(dl_m, 1)
                    dve.wait_ge(dl_o, i * 6 + (2 * g + 2))
                    og = tile_at(OG[:, :, g, :], i) if g < 2 else tile_at(OG2[:, :, :], i)
                    dve.tensor_copy(perm(og, g) if g else og, ordered(psl[:, 0, 1, :], g) if g else psl[:, 0, 1, :])\
                       .then_inc(dl_q, 1)
            for q in range(2):
                dve.drain()
                dve.wait_ge(dl_x, q + 1)
                for g in range(3):
                    dst, src = LROW[:, 3 * q + g, :], psa[0:16, g, :]
                    op = dve.tensor_copy(perm(dst, g) if g else dst, ordered(src, g) if g else src)
                op.then_inc(dl_y, 1)
            dve.drain()
            dve.tensor_tensor(LR2[:, :], LROW[:, 0, :], LROW[:, 1, :], ALU.max)
            dve.drain()
            dve.tensor_tensor(LR2[:, :], LR2[:, :], LROW[:, 2, :], ALU.max)
            dve.drain()
            for g in range(3):
                dve.tensor_tensor(LROW[:, g, :], LROW[:, g, :], LR2[:, :], ALU.subtract)
            dve.drain().then_inc(dl_w1, 1)
            dve.wait_ge(dl_w2, 1)
            for g in range(3):
                dve.tensor_tensor(LROW[:, 3 + g, :], LROW[:, 3 + g, :], LROW[:, g, :], ALU.mult)
            dve.drain()
            dve.tensor_tensor(LR2[:, :], LROW[:, 3, :], LROW[:, 4, :], ALU.add)
            dve.drain()
            dve.tensor_tensor(LR2[:, :], LR2[:, :], LROW[:, 5, :], ALU.add)
            dve.drain()
            dve.reciprocal(LR2[:, :], LR2[:, :])
            dve.drain()
            for g in range(3):
                dve.tensor_tensor(LROW[:, g, :], LROW[:, g, :], LR2[:, :], ALU.mult)
            dve.drain().then_inc(dl_rw, 1)
            A, Bt = LP[:, 0:TX], LP[:, TX:2 * TX]
            for i in range(HEADS):
                dve.wait_ge(dl_b, i + 1)
                if i > 0:
                    dve.drain()
                dve.tensor_tensor(A, OG[:, i, 0, :], psa[:, 0, :], ALU.mult)
                dve.tensor_tensor(Bt, OG[:, i, 1, :], psa[:, 1, :], ALU.mult)
                dve.drain()
                dve.tensor_tensor(A, A, Bt, ALU.add)
                dve.drain()
                dve.tensor_tensor(Bt, OG2[:, i, :], psa[:, 2, :], ALU.mult)
                dve.drain()
                dve.tensor_tensor(A, A, Bt, ALU.add).then_inc(split_ready, 1)
                dve_split(dve, N["mix1"] + i, A, HB[:, 0, i, :], HB[:, 1, i, :])

        block = ctx.enter_context(nc.Block())

        @block.sync
        def _(sp):
            sp.dma_start(XTOK[:, 0:4, :], a["x"][0].rearrange("(t p) d -> p t d", p=P)).then_inc(x_in, 16)
            sp.dma_start(XTOK[:, 4:6, :], a["ctx"][0].rearrange("(t p) d -> p t d", p=P)).then_inc(x_in, 16)
            before = None
            for st in plan.stages:
                if before is not None and st.raw:
                    sp.wait_ge(lo_ready, st.h0)
                if before is not None and before.raw:
                    sp.wait_ge(mod_used, before.m1)
                if st.name == "diff":
                    sp.wait_ge(split_done, N["mlstm"] + 8)
                    sp.dma_start(MEMT[:, :, :], a["mem_2"][0].rearrange("(t p) d -> p t d", p=P)).then_inc(mem_in, 16)
                with sp.Fori(0, st.n) as i:
                    for b, u in enumerate(st.body):
                        if u is None:
                            continue
                        if st.raw:
                            sp.wait_ge(mod_used, i * 4 + (st.m0 + b - 3))
                        else:
                            sp.wait_ge(lo_ready, i * st.B + (st.h0 + b - 3))
                        sp.dma_start(WR[:, b % RING, 0:st.kt, :], u(i)).then_inc(loaded[b % RING], 16)
                before = st
            sp.wait_ge(x_tr, 2)
            sp.dma_start(out[0].rearrange("(t p) d -> p t d", p=P), OTOK[:, :, :]).then_inc(out_sem, 16)
            sp.wait_ge(out_sem, 16)

        @block.gpsimd
        def _(pool):
            pool.sem_inc(lo_ready, RING)
            pool.memset(ident[:], 0.0)
            pool.memset(MASK[:, :, :], 0.0)
            pool.memset(ones[:], 1.0).then_inc(const_step, 1)
            pool.wait_ge(const_step, 1)
            pool.affine_select(out=ident[:], in_=ident[:], compare_op=ALU.not_equal, fill=1.0, base=0,
                               pattern=[[-1, P]], channel_multiplier=1).then_inc(const_step, 1)
            pool.affine_select(out=MASK[:, 0, :], in_=MASK[:, 0, :], compare_op=ALU.is_ge, fill=-BIG, base=0,
                               pattern=[[1, P]], channel_multiplier=-1).then_inc(const_step, 1)
            pool.affine_select(out=MASK[:, 1, :], in_=MASK[:, 1, :], compare_op=ALU.is_ge, fill=-BIG, base=0,
                               pattern=[[-1, P]], channel_multiplier=1).then_inc(const_step, 1)
            for h in range(HEADS):
                pool.memset(SLOPE[:, h:h + 1], -2.0 ** -(h + 1))
            for h in range(2 * HEADS):
                pool.memset(LSL[:, h:h + 1], -2.0 ** (-(h + 1) / 2))
            pool.memset(SM[:, 12:16], 0.0).then_inc(const_step, 1)
            pool.wait_ge(const_step, 5)
            pool.sem_inc(const_ready, 1)
            before = None
            for st in plan.stages:
                if st.raw:
                    before = st
                    continue
                if before is not None and before.raw:
                    pool.wait_ge(mod_used, before.m1)
                if st.name == "diff":
                    pool.wait_ge(split_done, N["mlstm"] + 8)
                    pool.wait_ge(split_ready, N["xb"] + 8)
                    pool.iota(DISTI[:, :], [[-1, 896]], base=384, channel_multiplier=1).then_inc(dist_i, 1)
                if st.name == "dil":
                    pool.wait_ge(split_done, N["ln02"][3] + 8)
                    pool.iota(LBI[:, 0:384], [[-1, 384]], base=P, channel_multiplier=1)
                    pool.iota(LBI[:, 384:512], [[-4, P]], base=0, channel_multiplier=4)
                    pool.iota(LBI[:, 512:640], [[-16, P]], base=0, channel_multiplier=16).then_inc(dl_i, 1)
                    pool.wait_ge(dl_mf, 1)
                    sel = dict(compare_op=ALU.is_ge, fill=BIG)
                    for k_, (o, n_, b0) in enumerate(((0, 384, P), (384, P, 0))):
                        t_ = LB[:, o:o + n_]
                        pool.affine_select(out=t_, in_=t_, base=64 + b0, pattern=[[-1, n_]], channel_multiplier=1, **sel)\
                            .then_inc(dl_i, 1)
                        pool.wait_ge(dl_i, 2 + 2 * k_)
                        pool.affine_select(out=t_, in_=t_, base=64 - b0, pattern=[[1, n_]], channel_multiplier=-1, **sel)\
                            .then_inc(dl_i, 1)
                        pool.wait_ge(dl_i, 3 + 2 * k_)
                    t_ = LB[:, 512:640].rearrange("p (b u) -> p b u", b=4)
                    pool.affine_select(out=t_, in_=t_, base=0, pattern=[[-32, 4], [0, 32]], channel_multiplier=1, **sel)\
                        .then_inc(dl_i, 1)
                    pool.wait_ge(dl_i, 6)
                    pool.affine_select(out=t_, in_=t_, base=31, pattern=[[32, 4], [0, 32]], channel_multiplier=-1, **sel)\
                        .then_inc(dl_mk, 1)
                if st.name == "dil_out":
                    pool.wait_ge(dl_q, 3 * HEADS + 1)
                    pool.memset(LSEL[:, :, :], 0.0).then_inc(dl_i, 1)
                    pool.wait_ge(dl_i, 7)
                    pool.affine_select(out=LSEL[:, :, :].rearrange("p i (a n) -> p i a n", a=2),
                                       in_=LSEL[:, :, :].rearrange("p i (a n) -> p i a n", a=2),
                                       compare_op=ALU.not_equal, fill=1.0, base=0,
                                       pattern=[[-2, HEADS], [-1, 2], [0, 64]], channel_multiplier=1).then_inc(dl_mk, 1)
                with pool.Fori(0, st.n) as i:
                    for b in sorted(st.inc):
                        pool.wait_ge(hi_ready, h_of(st, i, b) + 1)
                        pool.wait_ge(unit_done, h_of(st, i, b) - 3)
                        pool.tensor_tensor(WS[:, 1, b % RING, 0:st.kt, :], WR[:, b % RING, 0:st.kt, :],
                                           WS[:, 0, b % RING, 0:st.kt, :].bitcast(F32), ALU.subtract)\
                            .then_inc(lo_ready, st.inc[b])
                before = st

        @block.scalar
        def _(act):
            act.sem_inc(hi_ready, RING)
            act.sem_inc(dl_c, 1)
            rows = [(0, 0, a["norm_w"].rearrange("l n (k p) -> (l n k) p", p=P)),
                    (0, 64, a["conv_w"].rearrange("l j (k p) -> (l j k) p", p=P)),
                    (0, 88, a["ml_norm_w"].rearrange("l (k p) -> (l k) p", p=P)),
                    (0, 96, a["c"].rearrange("l (k p) -> (l k) p", p=P)),
                    (0, 104, a["c_ctx"].rearrange("(k p) -> k p", p=P)),
                    (0, 112, a["diff_subln_2"]),
                    (1, 0, a["mod_b"].rearrange("l (k p) -> (l k) p", p=P)),
                    (2, 0, a["ln_g_2"].rearrange("l n (k p) -> (l n k) p", p=P)),
                    (2, 48, a["ln_b_2"].rearrange("l n (k p) -> (l n k) p", p=P))]
            for l in range(2):
                rows.append((3 + l, 0, a["ffn_conv_w_2"][l].rearrange("j (k p) -> (j k) p", p=P)))
                rows.append((3 + l, 66, a["ffn_conv_b_2"][l].rearrange("(k p) -> k p", p=P)))
            for blk, r0, src in rows:
                act.dma_start(VR[r0:r0 + src.shape[0], blk, :], src).then_inc(small_in, 16)
            for kind in range(2):
                for r in range(2):
                    act.dma_start(SM[0:8, 2 * kind + r:2 * kind + r + 1],
                                  a["ml_b_if"][0][r:r + 1, 8 * kind:8 * kind + 8].rearrange("r h -> h r"))\
                       .then_inc(small_in, 16)
            act.wait_ge(v_ready, 1)
            act.activation(SV[:, :, :], VT[:, 0, 96:112].rearrange("p (v k) -> p k v", v=2), ACT.Exp, scale=-1.0)\
               .then_inc(sv_exp, 1)
            act_prenorm(act, N["n0"], GXC, N["x0"], True)
            act_first(act, S["conv"])
            act_conv(act)
            act_ysq(act, S["conv_out"], N["r0"], True, TA)
            act_stat(act, N["r0"][1], GXC, EPS)
            act_prenorm(act, N["n1"], GXC, N["r0"][2], False)
            act_mlp0(act)
            act_stat(act, N["r1"][1], GXC, EPS)
            act.wait_ge(wif_zero, 1)
            for r in range(2):
                for kind in range(2):
                    q = 2 * kind + r
                    act.dma_start(WIF[:, :, 32 * q:32 * q + 8],
                                  a["ml_w_if"][0, r].rearrange("(k p) g -> p k g", p=P)[:, :, 8 * kind:8 * kind + 8])\
                       .then_inc(wif_in, 16)
            act_prenorm(act, N["n2"], GXC, N["r1"][2], False)
            act_first(act, S["mlstm"])
            act_gates(act)
            act_mlstm(act)
            act_ysq(act, S["mlstm_out"], N["r2"], True, TX)
            act_stat(act, N["r2"][1], GX, EPS)
            act_prenorm(act, N["n3"], GX, N["r2"][2], False)
            act_mlp1(act)
            act_stat(act, N["r3"][1], GX, EPS)
            for k in range(KT):
                act_split(act, N["xb"] + k, X_(k, TX), HB[:, 0, k, :])
            act_mem(act)
            act.dma_start(AT[0:1, 0, 0:256], a["diff_lambda_2"].rearrange("l j e -> l (j e)")).then_inc(lam_in, 16)
            act_lam(act)
            act_diff(act)
            for l in range(2):
                if l == 1:
                    act_dil(act)
                act_lnsq(act, S["diff_out" if l == 0 else "dil_out"], N[f"ln{l}0"], True)
                act_ln(act, N[f"ln{l}0"])
                xatt[l][1](act)
                act_lnsq(act, S[f"xatt{l}_out"], N[f"ln{l}1"], True)
                act_ln(act, N[f"ln{l}1"])
                ffn[l][1](act)
                act_ln(act, N[f"ln{l}2"])
            act.wait_ge(x_tr, 1)
            for t in range(2):
                act.activation(OTOK[:, t, :], psa[:, 2 * t:2 * t + 2, :].rearrange("p a n -> p (a n)"), ACT.Copy)
            for t in range(2):
                op = act.activation(OTOK[:, 2 + t, :], psl[:, t, :, :].rearrange("p a n -> p (a n)"), ACT.Copy)
            act.drain().then_inc(x_tr, 1)

        @block.tensor
        def _(pe):
            pe.sem_inc(unit_done, RING)
            pe.sem_inc(mod_used, RING)
            pe.sem_inc(ml_pv, 1)
            pe.wait_ge(const_ready, 1)
            pe.wait_ge(small_in, 16 * 17)
            for blk, n in enumerate((113, 96, 96, 88, 88)):
                tr = pe.transpose(psl[:, blk // 4, 0, (blk % 4) * P:(blk % 4) * P + n], VR[0:n, blk, :], ident[0:n, 0:n])
            tr.then_inc(v_tr, 1)
            pe.wait_ge(x_in, 32)
            for k in range(KT):
                if k >= 2:
                    pe.wait_ge(x_ready, k - 1)
                for t in range(6):
                    tr = pe.transpose(psa[:, 2 * (k % 2) + t // 4, (t % 4) * P:(t % 4) * P + P], XTOK[:, t, k * P:k * P + P],
                                      ident[:])
                tr.then_inc(x_tr_k, 1)
            pe_stat(pe, N["n0"][1], GXC, ACC)
            pe.wait_ge(sv_ready, 1)
            pe.wait_ge(rstd_ready, 1)
            pe_mod(pe, S["mod0"])
            pe_dense(pe, S["conv"], HA, N["n0"][2])
            pe_dense(pe, S["conv_out"], GA, N["conv"])
            pe_stat(pe, N["r0"][1], GXC, ACC)
            pe_stat(pe, N["n1"][1], GXC, ACC)
            pe_mlp0(pe)
            pe_stat(pe, N["r1"][1], GXC, ACC)
            pe.wait_ge(rstd_ready, N["r1"][1] + 1)
            pe_mod(pe, S["mod1"])
            pe_stat(pe, N["n2"][1], GXC, ACC)
            pe_gates(pe)
            pe_mlstm(pe)
            pe_dense(pe, S["mlstm_out"], G1, N["mlstm"])
            pe_stat(pe, N["r2"][1], GX, ACC)
            pe_stat(pe, N["n3"][1], GX, ACC)
            pe_mlp1(pe)
            pe_stat(pe, N["r3"][1], GX, ACC)
            pe.wait_ge(split_ready, N["xb"] + 8)
            pe_mem(pe)
            pe_lam(pe)
            pe.wait_ge(lam_s, 1)
            pe_diff(pe)
            for l in range(2):
                if l == 1:
                    pe_dil(pe)
                pe_dense(pe, S["diff_out" if l == 0 else "dil_out"], GB if l == 0 else HB, N[f"mix{l}"])
                pe_ln(pe, N[f"ln{l}0"])
                xatt[l][0](pe)
                pe_dense(pe, S[f"xatt{l}_out"], GB, N[f"xatt{l}"])
                pe_ln(pe, N[f"ln{l}1"])
                ffn[l][0](pe)
                pe_ln(pe, N[f"ln{l}2"])
            pe.wait_ge(x_ready, N["x_end"] + 8)
            for t in range(4):
                for k in range(KT):
                    dst = psa[:, 2 * t + k // 4, :] if t < 2 else psl[:, t - 2, k // 4, :]
                    tr = pe.transpose(dst[:, (k % 4) * P:(k % 4) * P + P], X[:, k, t * P:t * P + P], ident[:])
            tr.then_inc(x_tr, 1)

        @block.vector
        def _(dve):
            dve.sem_inc(evac_done, RING)
            dve.sem_inc(dl_q, 1)
            dve.wait_ge(v_tr, 1)
            for blk, n in enumerate((113, 96, 96, 88, 88)):
                op = dve.tensor_copy(VT[:, blk, 0:n], psl[:, blk // 4, 0, (blk % 4) * P:(blk % 4) * P + n])
            op.then_inc(v_ready, 1)
            for k in range(KT):
                dve.wait_ge(x_tr_k, k + 1)
                dve.tensor_copy(X[:, k, 0:TX], psa[:, 2 * (k % 2), :])
                dve.tensor_copy(X[:, k, TX:TA], psa[:, 2 * (k % 2) + 1, 0:TC]).then_inc(x_ready, 1)
            dve.wait_ge(sv_exp, 1)
            dve.tensor_scalar(SV[:, :, :], SV[:, :, :], 1.0, None, ALU.add)
            dve.drain()
            dve.reciprocal(SV[:, :, :], SV[:, :, :])
            dve.drain()
            dve.tensor_tensor(SV[:, :, :], SV[:, :, :], VT[:, 0, 96:112].rearrange("p (v k) -> p k v", v=2), ALU.mult)\
               .then_inc(sv_ready, 1)
            dve_prenorm(dve, N["n0"], GXC, 0, lambda: dve_mod(dve, 0, S["mod0"]))
            dve_conv(dve)
            dve_zero_acc(dve, TA)
            dve_y(dve, S["conv_out"], N["r0"], True, True, TA)
            dve_residual(dve, N["r0"], GXC, 0)
            dve_prenorm(dve, N["n1"], GXC, 1)
            dve_mlp0(dve)
            dve_residual(dve, N["r1"], GXC, 1)
            dve.memset(WIF[:, :, :], 0.0).then_inc(wif_zero, 1)
            dve_mod(dve, 1, S["mod1"])
            dve_prenorm(dve, N["n2"], GXC, 0)
            dve_gates(dve)
            dve_mlstm(dve)
            dve_zero_acc(dve, TX)
            dve_y(dve, S["mlstm_out"], N["r2"], True, True, TX)
            dve_residual(dve, N["r2"], GX, 0)
            dve_prenorm(dve, N["n3"], GX, 1)
            dve_mlp1(dve)
            dve_residual(dve, N["r3"], GX, 1, split_ready)
            for k in range(KT):
                dve_split(dve, N["xb"] + k, X_(k, TX), HB[:, 0, k, :], HB[:, 1, k, :])
            dve_mem(dve)
            dve_lam(dve)
            dve_diff(dve)
            for l in range(2):
                if l == 1:
                    dve_dil(dve)
                dve_lnx(dve, S["diff_out" if l == 0 else "dil_out"], N[f"ln{l}0"], True, True)
                dve_ln(dve, N[f"ln{l}0"], l, 0)
                xatt[l][2](dve)
                dve_lnx(dve, S[f"xatt{l}_out"], N[f"ln{l}1"], True, True)
                dve_ln(dve, N[f"ln{l}1"], l, 1)
                ffn[l][2](dve)
                dve_ln(dve, N[f"ln{l}2"], l, 2)


_INS = ["x", "c", "ctx", "c_ctx", "norm_w", "mod_w", "mod_b", "mlp_w1", "mlp_w2", "conv_w_in", "conv_w", "conv_w_out",
        "ml_w_qkvo", "ml_w_if", "ml_b_if", "ml_norm_w", "ml_w_out", "mem_2", "diff_w_qkv_2", "diff_lambda_2",
        "diff_subln_2", "diff_w_o_2", "dil_w_qkv_2", "dil_w_o_2", "xatt_w_q_2", "xatt_w_kv_2", "xatt_w_o_2",
        "ffn_w_in_2", "ffn_conv_w_2", "ffn_conv_b_2", "ffn_w_out_2", "ln_g_2", "ln_b_2"]


def kernel(**inputs):
    import numpy as _np
    import concourse.bacc as _bacc
    from concourse import mybir as _mybir
    from concourse.bass_utils import run_bass_kernel_spmd as _run

    nc = _bacc.Bacc("TRN2", target_bir_lowering=False, num_devices=1)
    arrays, aps = {}, {}
    for name in _INS:
        arr = _np.ascontiguousarray(inputs[name])
        arrays[f"in_{name}_dram"] = arr
        aps[name] = nc.dram_tensor(f"in_{name}_dram", arr.shape, _mybir.dt.from_np(arr.dtype), kind="ExternalInput").ap()
    out = nc.dram_tensor("out_0_dram", (1, TX, D), F32, kind="ExternalOutput").ap()
    build(nc, aps, out)
    r = _run(nc, [arrays], core_ids=[0])
    return r.results[0]["out_0_dram"]
```

```python
from contextlib import ExitStack

import concourse.bass as bass
from concourse import mybir

F32 = mybir.dt.float32
F32R = mybir.dt.float32r
ACT = mybir.ActivationFunctionType
ALU = mybir.AluOpType
AXX = mybir.AxisListType.X

P = 128
D = 1024
KT = D // P
TX = 512
TC = 256
TA = TX + TC
TM = 256
GRID_W = 64
HEADS = 8
FF2 = 2816
FT2 = FF2 // P
XH = 4
EPS = 1e-6
LN_EPS = 1e-5
ALPHA = 4 ** 0.25
LAMBDA_INIT = 0.2
BIG = 1e30
RING = 4


class Stage:

    def __init__(self, name, n, body, groups, kt=KT):
        self.name, self.n, self.body, self.groups, self.kt = name, n, body, groups, kt
        self.B = len(body)
        assert self.B % RING == 0
        self.inc = {}
        for b, u in enumerate(body):
            if u is not None:
                skip = 0
                while b + 1 + skip < self.B and body[b + 1 + skip] is None:
                    skip += 1
                self.inc[b] = 1 + skip
        self.next = None


class Plan:

    def __init__(self, stages):
        self.stages = stages
        h, m = RING, RING
        loads = [0] * RING
        last = None
        for st in stages:
            st.loads = list(loads)
            st.per = [sum(1 for b in st.inc if b % RING == s) for s in range(RING)]
            loads = [a + st.n * p for a, p in zip(loads, st.per)]
            st.h0, st.m0 = h, m
            if st.raw:
                m += st.n * st.B
                last = None
            else:
                h += st.n * st.B
                if last is not None:
                    last.next = st
                last = st
            st.h1, st.m1 = h, m

    def loaded(self, st, i, b):
        before = sum(1 for c in st.inc if c < b and c % RING == b % RING)
        return 16 * (st.loads[b % RING] + before + 1) + i * (16 * st.per[b % RING])


def build(nc, a, out):
    GX = [(0, 0, TX)]
    GXC = [(0, 0, TX), (1, TX, TC)]
    GM = [(0, 0, TM)]

    def cols(w, c, k0=0, kt=KT):
        return w.rearrange("(k p) n -> p k n", p=P)[:, k0:k0 + kt, bass.ds(c, P)]

    def unit(w, step, c):
        return lambda i: cols(w, i * step + c)

    def mod_stage(l):
        st = Stage(f"mod{l}", 12, [(lambda i, b=b: cols(a["mod_w"][l], i * (4 * P) + b * P)) for b in range(4)], None)
        st.raw = True
        return st

    def dense(name, w, groups, tiles=KT, c0=0, k0=0, kt=KT):
        st = Stage(name, tiles // 4, [(lambda i, b=b: cols(w, i * (4 * P) + (c0 + b) * P, k0, kt)) for b in range(4)],
                   groups, kt)
        st.raw = False
        return st

    def custom(name, n, body, groups):
        st = Stage(name, n, body, groups)
        st.raw = False
        return st

    S = {}
    order = []

    def add(st):
        S[st.name] = st
        order.append(st)

    w_in, w_out = a["conv_w_in"][0], a["conv_w_out"][0]
    add(mod_stage(0))
    add(custom("conv", KT, [unit(w_in, P, j * D) for j in range(3)] + [None], GXC))
    add(dense("conv_out", w_out, GXC))
    for c in range(4):
        add(dense(f"mlp0_up{c}", a["mlp_w1"][0], GXC, c0=c * KT))
        add(dense(f"mlp0_down{c}", a["mlp_w2"][0], GXC, k0=c * KT))
    add(mod_stage(1))
    qkvo = a["ml_w_qkvo"][0]
    ml_at = [KT, KT + 1, 2 * KT, 0, KT // 2, 2 * KT + 1]
    ml_step = [2, 2, 2, 1, 1, 2]
    add(custom("mlstm", HEADS // 2,
               [unit(qkvo, s * P, c * P) for c, s in zip(ml_at, ml_step)] + [None, None],
               None))
    add(dense("mlstm_out", a["ml_w_out"][0], GX))
    for c in range(4):
        add(dense(f"mlp1_up{c}", a["mlp_w1"][1], GX, c0=c * KT))
        add(dense(f"mlp1_down{c}", a["mlp_w2"][1], GX, k0=c * KT))
    dq = a["diff_w_qkv_2"][0]
    body = []
    for head in range(2):
        body += [unit(dq, 2 * P, j * D + head * P) for j in range(3)] + [None]
    add(custom("diff", HEADS // 2, body, GX))
    add(dense("diff_out", a["diff_w_o_2"][0], GX))
    lq = a["dil_w_qkv_2"][0]
    for l in range(2):
        if l == 1:
            body = []
            for g in range(3):
                body += [unit(lq, P, (g * 3 + j) * D) for j in range(3)] + [None]
            add(custom("dil", HEADS, body, GX))
            add(dense("dil_out", a["dil_w_o_2"][0], GX))
        kv, wq = a["xatt_w_kv_2"][l], a["xatt_w_q_2"][l]
        body = [unit(kv, 2 * P, c) for c in (0, P, D, D + P)] + [unit(wq, 2 * P, c) for c in (0, P)] + [None, None]
        add(custom(f"xatt{l}", XH, body, None))
        add(dense(f"xatt{l}_out", a["xatt_w_o_2"][l], GX))
        for c in range(3):
            nt = min(8, FT2 - 8 * c)
            body = [unit(a["ffn_w_in_2"][l], 2 * P, (8 * c + t) * P + o) for t in range(2) for o in (0, FF2)]
            add(custom(f"ffn{l}_in{c}", nt // 2, body, GX))
            add(dense(f"ffn{l}_out{c}", a["ffn_w_out_2"][l], GX, k0=8 * c, kt=nt))
    plan = Plan(order)

    with ExitStack() as ctx:
        def sem(name):
            return ctx.enter_context(nc.semaphore(name))

        base = 16512
        top = [base]

        def place(name, shape, dt=F32, at=None):
            size = 4
            for s in shape[1:]:
                size *= s
            if at is None:
                at = top[0]
                top[0] += (size + 31) // 32 * 32
            return nc.alloc_sbuf_tensor_at(name, shape, dt, offset=at)

        WR = place("w_raw", [P, RING, KT, P])
        WS = place("w_split", [P, 2, RING, KT, P], F32R)
        x_at = top[0]
        X = place("x_state", [P, KT, TA])
        h_at = top[0]
        HA = place("h_a", [P, 2, KT, TA], F32R)
        g_at = top[0]
        GA = place("g_a", [P, 2, KT, TA], F32R)
        y_at = top[0]
        Y = place("y", [P, KT, TA])
        wk_at = top[0]
        WK = place("wk", [P, 3, TA])
        ident = place("ident", [P, P])
        ones = place("ones", [P, P])
        VT = place("vt", [P, 5, P])
        MOD = place("mod", [P, 2, 48])
        COEF = place("coef", [P, 2, 4, KT])
        SV = place("sv", [P, KT, 2])
        MASK = place("mask", [P, 2, P])
        SLOPE = place("slope", [P, HEADS])
        SM = place("small", [P, 32])
        LSL = place("dl_slope", [P, 2 * HEADS])
        assert top[0] <= 229344, top[0]
        XTOK = place("x_tok", [P, 6, D], at=y_at)
        VR = place("vr", [P, 6, P], at=wk_at)
        half = 4 * 2 * KT * TX
        G1 = place("g_1", [P, 2, KT, TX], F32R, at=g_at)
        tail = g_at + half
        MR = place("mod_rows", [2, 2, TX], at=g_at)
        WIF = place("wif", [P, KT, P], at=tail)
        MROW = place("mrow", [8, 2, TX], at=tail)
        IG = place("ig_rows", [8, 2, TA], at=tail + 4096)
        BR = place("b_rows", [8, 2, TA], at=tail + 4096 + 6144)
        GCOL = X[:, 6, TX:TX + 96].rearrange("p (r s h) -> p r s h", r=2, s=6)
        MN = place("ml_neg", [P, 2, TX], at=tail + 4096)
        LF = place("lf_rows", [8, 6, TA], at=g_at)
        MQ = place("ml_q", [P, TX], at=y_at)
        MK = place("ml_k", [P, TA], at=y_at + 2048)
        MV = place("ml_v", [P, TA], at=wk_at)
        MO = place("ml_o", [P, 2, TX], at=y_at + 8192)
        ME = place("ml_e", [P, 2, TX], at=y_at + 12288)
        ME2 = [place(f"ml_e2_{r}", [P, TX], at=at) for r, at in enumerate((wk_at + 7168, tail + 8192))]
        MM = place("ml_mneg", [P, 2, TX], at=y_at + 16384)
        RH = place("ml_rows", [8, 2, TX], at=y_at + 20480)
        HS = place("ml_h", [P, TX], at=y_at + 5120)
        RD = place("ml_rd", [P, TX], at=wk_at + 3072)
        MT = place("ml_t", [P, TX], at=wk_at + 5120)
        HB = place("h_b", [P, 2, KT, TX], F32R, at=h_at)
        MEMH = place("mem_h", [P, 2, KT, TM], F32R, at=h_at + half)
        GB = place("g_b", [P, 2, KT, TX], F32R, at=g_at)
        MEMT = place("mem_tok", [P, 2, D], at=tail)
        wb = tail
        WB = place("wk_b", [P, 6, TX], at=wb)
        at_b = wb + 12288
        AQ = place("at_q", [P, 2, TX], at=at_b)
        AK = place("at_k", [P, 2, TX], at=at_b + 4096)
        AV = place("at_v", [P, TX], at=at_b + 8192)
        MEMF = place("mem_f", [P, KT, TM], at=at_b + 19456)
        VTK = place("v_tok", [P, 4, P], at=at_b + 10240)
        DIST = place("dist", [P, 896], at=at_b + 12288)
        DISTI = place("dist_i", [P, KT, TA], mybir.dt.int32, at=x_at)[:, 0:4, TX:TX + 224]
        SB = place("bias_h", [P, 896], at=at_b + 12288 + 3584)
        DS = place("scores", [P, 2, 2, TX], at=at_b + 19456)
        AT = place("attn_t", [P, 4, TX], at=at_b + 27648)
        DST = place("diff_stat", [P, 4, 4, 2], at=at_b + 35840)
        assert at_b + 35840 + 128 <= wk_at + 9216
        OG = place("og", [P, HEADS, 2, TX], at=g_at)
        OG2 = place("og2", [P, HEADS, TX], at=at_b)
        dl = at_b + 16384
        LV = place("dl_v", [P, TX], at=dl + 4096)
        LQK = [place(f"dl_qk{g}", [P, 2, TX], at=at) for g, at in enumerate((dl, wb, wb + 4096))]
        LB = place("dl_dist", [P, 640], at=dl + 6144)
        LSB = place("dl_bias", [P, 640], at=dl + 8704)
        LBI = place("dl_dist_i", [P, 640], mybir.dt.int32, at=dl + 8704)
        LP = place("dl_p", [P, 1024], at=dl + 11264)
        LPT = place("dl_pt", [P, 8, P], at=dl + 15360)
        LMS = place("dl_stat", [P, 2, 3, 4, 16], at=dl + 19456)
        LROW = place("dl_rows", [16, 6, TX], at=wb)
        LSEL = place("dl_sel", [16, HEADS, P], at=dl)
        LR2 = place("dl_rows2", [16, TX], at=dl + 4096)
        assert dl + 19456 + 1536 <= wk_at + 9216
        OTOK = place("out_tok", [P, 4, D], at=wb)

        psl = ctx.enter_context(nc.psum_tensor("ps_lin", [P, 2, 2, 512], F32))
        psa = ctx.enter_context(nc.psum_tensor("ps_att", [P, 4, 512], F32))

        loaded = [sem(f"w_loaded{s}") for s in range(RING)]
        hi_ready = sem("w_hi_ready")
        lo_ready = sem("w_lo_ready")
        unit_done = sem("unit_done")
        mod_used = sem("mod_used")
        mod_taken = sem("mod_rows_taken")
        mod_turned = sem("mod_rows_transposed")
        evac_done = sem("evac_done")
        split_ready = sem("split_ready")
        split_hi = sem("split_hi")
        split_done = sem("split_done")
        small_in = sem("small_in")
        x_in = sem("x_in")
        wif_in = sem("wif_in")
        mem_in = sem("mem_in")
        out_sem = sem("out_stored")
        const_step = sem("const_step")
        const_ready = sem("const_ready")
        x_tr = sem("out_transposed")
        x_tr_k = sem("x_transposed")
        x_ready = sem("x_ready")
        v_tr = sem("vectors_transposed")
        v_ready = sem("vectors_ready")
        sv_exp = sem("silu_exp")
        sv_ready = sem("silu_ready")
        sq_ready = sem("sq_ready")
        ysq_ready = sem("ysq_ready")
        acc_ready = sem("acc_ready")
        stat_ready = sem("stat_ready")
        mean_ready = sem("mean_ready")
        var_ready = sem("var_ready")
        rstd_ready = sem("rstd_ready")
        wif_zero = sem("wif_zero")
        end_norm = sem("end_normalised")

        def tile_at(ap3, m):
            return ap3[:, bass.ds(m, 1), :].rearrange("p a n -> p (a n)")

        def col(ap2, m):
            return ap2[:, bass.ds(m, 1)]

        def h_of(st, i, b):
            return i * st.B + (st.h0 + b)

        def groups_of(st, b):
            if st.groups is not None:
                return st.groups
            if st.name == "mlstm":
                return GX if b in (2, 3, 5) else GXC
            return GM if b < 4 else GX

        def pe_unit(pe, st, i, b, rhs, kwait=None, slots=2):
            pe.wait_ge(lo_ready, h_of(st, i, b) + 1)
            pe.wait_ge(evac_done, h_of(st, i, b) + 1 - slots)
            groups = groups_of(st, b)
            for k in range(st.kt):
                if kwait is not None:
                    pe.wait_ge(split_done, kwait + k + 1)
                for n, (wp, xp) in enumerate(((0, 0), (0, 1), (1, 0))):
                    for gi, c0, nn in groups:
                        mm = pe.matmul(psl[:, b % slots, gi, 0:nn], WS[:, wp, b % RING, k, :], rhs[:, xp, k, c0:c0 + nn],
                                       start=(k == 0 and n == 0), stop=(k == st.kt - 1 and n == 2))
            mm.then_inc(unit_done, st.inc[b])

        def pe_dense(pe, st, rhs, kwait):
            with pe.Fori(0, st.n) as i:
                for b in sorted(st.inc):
                    pe_unit(pe, st, i, b, rhs, kwait if b == 0 else None)

        def act_hi(act, st, i, b):
            t = b + 3
            if t >= st.B:
                t -= st.B
                if isinstance(i, int) and i == st.n - 1:
                    st, i = st.next, 0
                    if st is None:
                        return
                else:
                    i = i + 1
            if t not in st.inc:
                return
            act.wait_ge(loaded[t % RING], plan.loaded(st, i, t))
            act.wait_ge(unit_done, h_of(st, i, t) - 3)
            act.activation(WS[:, 0, t % RING, 0:st.kt, :], WR[:, t % RING, 0:st.kt, :], ACT.Copy)\
               .then_inc(hi_ready, st.inc[t])

        def act_first(act, st):
            for t in range(3):
                act.wait_ge(loaded[t], plan.loaded(st, 0, t))
                act.activation(WS[:, 0, t, :, :], WR[:, t, :, :], ACT.Copy).then_inc(hi_ready, st.inc[t])

        def act_rounds(act, st, body):
            if st.n > 1:
                with act.Fori(0, st.n - 1) as i:
                    body(i)
            body(st.n - 1)

        def evac_wait(dve, st, i, b):
            dve.wait_ge(unit_done, h_of(st, i, b) + 1)

        def act_split(act, idx, src, dst):
            act.wait_ge(split_ready, idx + 1)
            act.activation(dst, src, ACT.Copy).then_inc(split_hi, 1)

        def dve_split(dve, idx, src, hi, lo):
            dve.wait_ge(split_hi, idx + 1)
            dve.tensor_tensor(lo, src, hi.bitcast(F32), ALU.subtract).then_inc(split_done, 1)

        cnt = {"split": 0, "stat": 0, "sq": 0, "x": 0, "ysq": 0, "mean": 0}

        def take(kind, n):
            v = cnt[kind]
            cnt[kind] = v + n
            return v

        N = {}
        N["x0"] = take("x", 8)
        for nm in ("n0",):
            N[nm] = (take("sq", 8), take("stat", 1), take("split", 8))
        N["conv"] = take("split", 8)

        def number_residual(nm):
            N[nm] = (take("ysq", 8), take("stat", 1), take("x", 8))

        number_residual("r0")
        N["n1"] = (take("sq", 8), take("stat", 1), take("split", 8))
        for c in range(4):
            N[f"mlp0_{c}"] = take("split", 8)
        number_residual("r1")
        N["n2"] = (take("sq", 8), take("stat", 1), take("split", 8))
        N["mlstm"] = take("split", 8)
        number_residual("r2")
        N["n3"] = (take("sq", 8), take("stat", 1), take("split", 8))
        for c in range(4):
            N[f"mlp1_{c}"] = take("split", 8)
        N["r3"] = (take("ysq", 8), take("stat", 1), None)
        N["xb"] = take("split", 8)
        N["mem"] = take("split", 8)

        def number_ln(nm, split):
            N[nm] = (take("ysq", 8), take("stat", 1), take("mean", 1), take("split", 8) if split else None)

        for l in range(2):
            N[f"mix{l}"] = take("split", 8)
            number_ln(f"ln{l}0", True)
            N[f"xatt{l}"] = take("split", 8)
            number_ln(f"ln{l}1", True)
            for c in range(3):
                N[f"ffn{l}_{c}"] = take("split", min(8, FT2 - 8 * c))
            number_ln(f"ln{l}2", l == 0)
        N["x_end"] = take("x", 8)

        def X_(k, n):
            return X[:, k, 0:n]

        TMP, RB, ACC = WK[:, 0, :], WK[:, 1, :], WK[:, 2, :]

        def act_stat(act, s, groups, eps, scale=1.0 / D):
            act.wait_ge(stat_ready, s + 1)
            for gi, c0, n in groups:
                act.activation(RB[:, c0:c0 + n], psa[:, gi, 0:n], ACT.Ln, bias=eps, scale=scale)
            act.drain()
            n = sum(g[2] for g in groups)
            act.activation(RB[:, 0:n], RB[:, 0:n], ACT.Exp, scale=-0.5).then_inc(rstd_ready, 1)

        def act_prenorm(act, num, groups, xbase, whole, which, between=None):
            sq, s, sp = num
            n = sum(g[2] for g in groups)
            for k in range(KT):
                act.wait_ge(x_ready, xbase + (KT if whole else k + 1))
                act.activation(Y[:, k, 0:n], X_(k, n), ACT.Square).then_inc(sq_ready, 1)
            act_stat(act, s, groups, EPS)
            if between is not None:
                between()
            for k in range(KT):
                if which is None:
                    act_split(act, sp + k, Y[:, k, 0:n], HA[:, 0, k, 0:n])
                    continue
                act.wait_ge(split_ready, sp + k + 1)
                for v, (gi, c0, nn) in enumerate(groups):
                    op = act.activation(HA[:, 0, k, c0:c0 + nn], Y[:, k, c0:c0 + nn], ACT.Identity,
                                        bias=MOD[:, v, 24 * which + k:24 * which + k + 1])
                op.then_inc(split_hi, 1)

        def dve_prenorm(dve, num, groups, which, between=None, whole=False):
            sq, s, sp = num
            n = sum(g[2] for g in groups)
            dve.sem_inc(acc_ready, KT)
            if between is not None:
                between()
            dve.wait_ge(rstd_ready, s + 1)
            for k in range(KT + 1):
                if k < KT and not whole:
                    for v, (gi, c0, nn) in enumerate(groups):
                        op = dve.scalar_tensor_tensor(out=Y[:, k, c0:c0 + nn], in0=X[:, k, c0:c0 + nn],
                                                      scalar=COEF[:, v, 2 * which, k:k + 1], in1=RB[:, c0:c0 + nn],
                                                      op0=ALU.mult, op1=ALU.mult)
                    op.then_inc(split_ready, 1)
                elif k < KT:
                    dve.tensor_tensor(Y[:, k, 0:n], X_(k, n), RB[:, 0:n], ALU.mult)
                    dve.drain()
                    for v, (gi, c0, nn) in enumerate(groups):
                        op = dve.tensor_scalar(Y[:, k, c0:c0 + nn], Y[:, k, c0:c0 + nn],
                                               COEF[:, v, 2 * which, k:k + 1], MOD[:, v, 24 * which + k:24 * which + k + 1],
                                               ALU.mult, ALU.add)
                    op.then_inc(split_ready, 1)
                if k > 0 and whole:
                    dve_split(dve, sp + k - 1, Y[:, k - 1, 0:n], HA[:, 0, k - 1, 0:n], HA[:, 1, k - 1, 0:n])
                elif k > 0:
                    dve.wait_ge(split_hi, sp + k)
                    for v, (gi, c0, nn) in enumerate(groups):
                        op = dve.scalar_tensor_tensor(out=HA[:, 1, k - 1, c0:c0 + nn], in0=Y[:, k - 1, c0:c0 + nn],
                                                      scalar=MOD[:, v, 24 * which + k - 1:24 * which + k],
                                                      in1=HA[:, 0, k - 1, c0:c0 + nn].bitcast(F32),
                                                      op0=ALU.add, op1=ALU.subtract)
                    op.then_inc(split_done, 1)

        def pe_stat(pe, s, groups, src):
            pe.wait_ge(acc_ready, 8 * (s + 1))
            for gi, c0, n in groups:
                mm = pe.matmul(psa[:, gi, 0:n], ones[:], src[:, c0:c0 + n], start=True, stop=True)
            mm.then_inc(stat_ready, 1)

        def pe_stat_squares(pe, num, groups):
            sq, s, sp = num
            for k in range(KT):
                pe.wait_ge(sq_ready, sq + k + 1)
                for gi, c0, n in groups:
                    mm = pe.matmul(psa[:, gi, 0:n], ones[:], Y[:, k, c0:c0 + n], start=(k == 0), stop=(k == KT - 1))
            mm.then_inc(stat_ready, 1)

        def act_ysq(act, st, num, last, n):
            ysq, s, xb = num

            def body(i):
                for b in range(4):
                    if last:
                        act.wait_ge(evac_done, h_of(st, i, b) + 1)
                        act.wait_ge(acc_ready, 8 * s + i * 4 + b)
                        act.activation(TMP[:, 0:n], tile_at(Y[:, :, 0:n], i * 4 + b), ACT.Square)\
                           .then_inc(ysq_ready, 1)
                    act_hi(act, st, i, b)
            act_rounds(act, st, body)

        def dve_y(dve, st, num, first, last, n):
            ysq, s, xb = num
            with dve.Fori(0, st.n) as i:
                for b in range(4):
                    dve.drain()
                    evac_wait(dve, st, i, b)
                    y = Y[:, bass.ds(i * 4 + b, 1), :].rearrange("p a n -> p (a n)")
                    for gi, c0, nn in st.groups:
                        if first:
                            op = dve.tensor_copy(y[:, c0:c0 + nn], psl[:, b % 2, gi, 0:nn])
                        else:
                            op = dve.tensor_tensor(y[:, c0:c0 + nn], psl[:, b % 2, gi, 0:nn], y[:, c0:c0 + nn], ALU.add)
                    op.then_inc(evac_done, 1)
                    if last:
                        dve.wait_ge(ysq_ready, i * 4 + (ysq + b + 1))
                        dve.tensor_tensor(ACC[:, 0:n], ACC[:, 0:n], TMP[:, 0:n], ALU.add).then_inc(acc_ready, 1)

        def dve_zero_acc(dve, n):
            dve.drain()
            dve.memset(ACC[:, 0:n], 0.0)

        def dve_residual(dve, num, groups, which, done=x_ready):
            ysq, s, xb = num
            n = sum(g[2] for g in groups)
            dve.wait_ge(rstd_ready, s + 1)
            for k in range(KT):
                dve.tensor_tensor(Y[:, k, 0:n], Y[:, k, 0:n], RB[:, 0:n], ALU.mult)
                dve.drain()
                for v, (gi, c0, nn) in enumerate(groups):
                    op = dve.scalar_tensor_tensor(out=X[:, k, c0:c0 + nn], in0=Y[:, k, c0:c0 + nn],
                                                  scalar=COEF[:, v, 2 * which + 1, k:k + 1], in1=X[:, k, c0:c0 + nn],
                                                  op0=ALU.mult, op1=ALU.add)
                op.then_inc(done, 1)

        def act_up(act, st, sp, G, n):
            def body(i):
                for b in range(4):
                    act_split(act, i * 4 + (sp + b), WK[:, b % 2, 0:n], tile_at(G[:, 0, :, 0:n], i * 4 + b))
                    act_hi(act, st, i, b)
            act_rounds(act, st, body)

        def dve_up(dve, st, sp, G, n):
            with dve.Fori(0, st.n) as i:
                for b in range(4):
                    dve.drain()
                    evac_wait(dve, st, i, b)
                    z = WK[:, b % 2, 0:n]
                    for gi, c0, nn in st.groups:
                        op = dve.tensor_scalar(z[:, c0:c0 + nn], psl[:, b % 2, gi, 0:nn], 0.0, None, ALU.max)
                    op.then_inc(evac_done, 1)
                    dve.drain()
                    dve.tensor_tensor(z, z, z, ALU.mult).then_inc(split_ready, 1)
                    dve_split(dve, i * 4 + (sp + b), z, tile_at(G[:, 0, :, 0:n], i * 4 + b),
                              tile_at(G[:, 1, :, 0:n], i * 4 + b))

        def mlp(l, G, groups, num):
            n = sum(g[2] for g in groups)

            def pe_part(pe):
                for c in range(4):
                    pe_dense(pe, S[f"mlp{l}_up{c}"], HA, N["n1" if l == 0 else "n3"][2])
                    pe_dense(pe, S[f"mlp{l}_down{c}"], G, N[f"mlp{l}_{c}"])

            def act_part(act):
                for c in range(4):
                    act_up(act, S[f"mlp{l}_up{c}"], N[f"mlp{l}_{c}"], G, n)
                    act_ysq(act, S[f"mlp{l}_down{c}"], num, c == 3, n)

            def dve_part(dve):
                for c in range(4):
                    dve_up(dve, S[f"mlp{l}_up{c}"], N[f"mlp{l}_{c}"], G, n)
                    if c == 3:
                        dve_zero_acc(dve, n)
                    dve_y(dve, S[f"mlp{l}_down{c}"], num, c == 0, c == 3, n)
            return pe_part, act_part, dve_part

        pe_mlp0, act_mlp0, dve_mlp0 = mlp(0, GA, GXC, N["r1"])
        pe_mlp1, act_mlp1, dve_mlp1 = mlp(1, G1, GX, N["r3"])

        def pe_mod(pe, l, st, lo, hi):
            with pe.Fori(lo, hi) as i:
                def unit_rows(r, b):
                    pe.wait_ge(loaded[b], plan.loaded(st, i * 2 + r, b))
                    for k in range(KT):
                        mm = pe.matmul(psl[0:2, r, 1, b * P:b * P + P], SV[:, k, :], WR[:, b, k, :],
                                       start=(k == 0), stop=(k == KT - 1))
                    mm.then_inc(mod_used, 1)

                def turn(r):
                    pe.wait_ge(mod_taken, i * 2 + (12 * l + r + 3))
                    for b in range(4):
                        tr = pe.matmul(psa[:, 2, bass.ds(i * 16 + (8 * r + 2 * b), 2)], MR[:, r, b * P:b * P + P],
                                       ident[0:2, 0:2], start=True, stop=True)
                    tr.then_inc(mod_turned, 1)

                for r in range(2):
                    pe.wait_ge(mod_taken, i * 2 + (12 * l + r + 1))
                    for b in range(4):
                        unit_rows(r, b)
                        if r == 1 and b == 1:
                            turn(0)
                turn(1)

        def act_mod(act, l, st, lo, hi):
            with act.Fori(lo, hi) as i:
                for r in range(2):
                    act.wait_ge(mod_used, i * 8 + (st.m0 + 4 * r + 4))
                    act.activation(MR[:, r, :], psl[0:2, r, 1, :], ACT.Copy).then_inc(mod_taken, 1)

        def dve_mod(dve, l, st):
            dve.drain()
            dve.wait_ge(mod_turned, 12 * (l + 1))
            for v in range(2):
                dve.tensor_tensor(MOD[:, v, :], psa[:, 2, v:96:2], VT[:, 1, 48 * l:48 * l + 48], ALU.add)
            dve.drain()
            nw = 32 * l
            for v in range(2):
                for w in range(2):
                    dve.scalar_tensor_tensor(out=COEF[:, v, 2 * w, :], in0=MOD[:, v, 24 * w + 8:24 * w + 16], scalar=1.0,
                                             in1=VT[:, 0, nw + 16 * w:nw + 16 * w + 8], op0=ALU.add, op1=ALU.mult)
                    dve.tensor_tensor(COEF[:, v, 2 * w + 1, :], MOD[:, v, 24 * w + 16:24 * w + 24],
                                      VT[:, 0, nw + 16 * w + 8:nw + 16 * w + 16], ALU.mult)
            dve.drain()

        TB, RBB, ACS, ACR, MNB, ZB = (WB[:, j, :] for j in range(6))

        def act_lnsq(act, st, num, last):
            ysq, s, mn, sp = num

            def body(i):
                for b in range(4):
                    if last:
                        act.wait_ge(evac_done, h_of(st, i, b) + 1)
                        act.wait_ge(acc_ready, 8 * s + i * 4 + b)
                        act.activation(TB, tile_at(X[:, :, 0:TX], i * 4 + b), ACT.Square).then_inc(ysq_ready, 1)
                    act_hi(act, st, i, b)
            act_rounds(act, st, body)

        def dve_lnx(dve, st, num, first, last):
            ysq, s, mn, sp = num
            if last:
                dve.drain()
                dve.memset(ACS, 0.0)
                dve.memset(ACR, 0.0)
            with dve.Fori(0, st.n) as i:
                for b in range(4):
                    dve.drain()
                    evac_wait(dve, st, i, b)
                    x = X[:, bass.ds(i * 4 + b, 1), 0:TX].rearrange("p a n -> p (a n)")
                    if first:
                        dve.scalar_tensor_tensor(out=x, in0=x, scalar=ALPHA, in1=psl[:, b % 2, 0, :],
                                                 op0=ALU.mult, op1=ALU.add).then_inc(evac_done, 1)
                    else:
                        dve.tensor_tensor(x, psl[:, b % 2, 0, :], x, ALU.add).then_inc(evac_done, 1)
                    if last:
                        dve.drain()
                        dve.tensor_tensor(ACR, ACR, x, ALU.add)
                        dve.wait_ge(ysq_ready, i * 4 + (ysq + b + 1))
                        dve.tensor_tensor(ACS, ACS, TB, ALU.add).then_inc(acc_ready, 1)

        def pe_ln(pe, num):
            pe.wait_ge(acc_ready, 8 * (num[1] + 1))
            pe.matmul(psa[:, 0, :], ones[:], ACR, start=True, stop=True)
            pe.matmul(psa[:, 1, :], ones[:], ACS, start=True, stop=True).then_inc(stat_ready, 1)

        def act_ln(act, num, l, j, between=None):
            ysq, s, mn, sp = num
            act.wait_ge(stat_ready, s + 1)
            act.activation(MNB, psa[:, 0, :], ACT.Copy, scale=1.0 / D)
            act.activation(TB, psa[:, 0, :], ACT.Square, scale=1.0 / D).then_inc(mean_ready, 1)
            act.wait_ge(var_ready, mn + 1)
            act.activation(RBB, RBB, ACT.Ln, bias=LN_EPS)
            act.drain()
            act.activation(RBB, RBB, ACT.Exp, scale=-0.5).then_inc(rstd_ready, 1)
            for k in range(KT):
                g0 = l * 24 + j * 8 + k
                if sp is not None:
                    act.wait_ge(split_ready, sp + k + 1)
                else:
                    act.wait_ge(end_norm, k + 1)
                op = act.activation(X_(k, TX), X_(k, TX), ACT.Identity, scale=VT[:, 2, g0:g0 + 1],
                                    bias=VT[:, 2, 48 + g0:49 + g0])
                if sp is None:
                    op.then_inc(x_ready, 1)
                else:
                    act.drain()
                    act.activation(HB[:, 0, k, :], X_(k, TX), ACT.Copy).then_inc(split_hi, 1)
                if between is not None:
                    between(act, k)

        def dve_ln(dve, num, between=None):
            ysq, s, mn, sp = num
            dve.wait_ge(mean_ready, mn + 1)
            dve.scalar_tensor_tensor(out=RBB, in0=psa[:, 1, :], scalar=1.0 / D, in1=TB, op0=ALU.mult, op1=ALU.subtract)\
               .then_inc(var_ready, 1)
            dve.wait_ge(rstd_ready, s + 1)
            for k in range(KT + 1):
                if k < KT:
                    x = X_(k, TX)
                    dve.tensor_tensor(x, x, MNB, ALU.subtract)
                    dve.drain()
                    dve.tensor_tensor(x, x, RBB, ALU.mult).then_inc(split_ready if sp is not None else end_norm, 1)
                if k > 0 and sp is not None:
                    dve_split(dve, sp + k - 1, X_(k - 1, TX), HB[:, 0, k - 1, :], HB[:, 1, k - 1, :])
                    if between is not None:
                        between(dve, k)

        def ffn_parts(l):
            g_ready = sem(f"gate_conv{l}")
            gelu_ready = sem(f"gelu{l}")
            num = N[f"ln{l}2"]

            def pe_part(pe):
                for c in range(3):
                    pe_dense(pe, S[f"ffn{l}_in{c}"], HB, N[f"ln{l}1"][3])
                    pe_dense(pe, S[f"ffn{l}_out{c}"], GB, N[f"ffn{l}_{c}"])

            def act_part(act):
                for c in range(3):
                    st = S[f"ffn{l}_in{c}"]

                    def body(i):
                        for t in range(2):
                            tile = i * 2 + t
                            act.wait_ge(g_ready, i * 2 + (8 * c + t + 1))
                            act.activation(WB[:, 1 + t, :], WB[:, 1 + t, :], ACT.Gelu).then_inc(gelu_ready, 1)
                            act_hi(act, st, i, 2 * t)
                            act_split(act, i * 2 + (N[f"ffn{l}_{c}"] + t), WB[:, 3 + t, :], tile_at(GB[:, 0, :, :], tile))
                            act_hi(act, st, i, 2 * t + 1)
                    act_rounds(act, st, body)
                    act_lnsq(act, S[f"ffn{l}_out{c}"], num, c == 2)

            def dve_part(dve):
                for c in range(3):
                    st = S[f"ffn{l}_in{c}"]
                    with dve.Fori(0, st.n) as i:
                        for t in range(2):
                            def wcol(j):
                                return col(VT[:, 3 + l, :], i * 2 + (j * FT2 + 8 * c + t))
                            g, y, z = WB[:, 0, :], WB[:, 1 + t, :], WB[:, 3 + t, :]
                            dve.drain()
                            evac_wait(dve, st, i, 2 * t)
                            dve.tensor_copy(g, psl[:, 0, 0, :]).then_inc(evac_done, 1)
                            dve.drain()
                            dve.tensor_scalar(y, g, wcol(1), wcol(3), ALU.mult, ALU.add)
                            dve.drain()
                            dve.scalar_tensor_tensor(out=y[:, 1:TX], in0=g[:, 0:TX - 1], scalar=wcol(0), in1=y[:, 1:TX],
                                                     op0=ALU.mult, op1=ALU.add)
                            dve.drain()
                            dve.scalar_tensor_tensor(out=y[:, 0:TX - 1], in0=g[:, 1:TX], scalar=wcol(2),
                                                     in1=y[:, 0:TX - 1], op0=ALU.mult, op1=ALU.add).then_inc(g_ready, 1)
                            evac_wait(dve, st, i, 2 * t + 1)
                            dve.wait_ge(gelu_ready, i * 2 + (8 * c + t + 1))
                            dve.tensor_tensor(z, psl[:, 1, 0, :], y, ALU.mult).then_inc(evac_done, 1)
                            dve.drain().then_inc(split_ready, 1)
                            dve_split(dve, i * 2 + (N[f"ffn{l}_{c}"] + t), z, tile_at(GB[:, 0, :, :], i * 2 + t),
                                      tile_at(GB[:, 1, :, :], i * 2 + t))
                    dve_lnx(dve, S[f"ffn{l}_out{c}"], num, c == 0, c == 2)
                    if l == 0 and c == 0:
                        dve_dil_tables(dve)
            return pe_part, act_part, dve_part

        ffn = [ffn_parts(0), ffn_parts(1)]

        def act_conv(act):
            st, sp = S["conv"], N["conv"]

            def body(i):
                act_hi(act, st, i, 0)
                act_hi(act, st, i, 1)
                act_hi(act, st, i, 2)
                act_hi(act, st, i, 3)
                act_split(act, i + sp, Y[:, 3, :], tile_at(GA[:, 0, :, :], i))
            act_rounds(act, st, body)

        def dve_conv(dve):
            st, sp = S["conv"], N["conv"]
            Bt, Ct, U, Z = (Y[:, j, :] for j in range(4))
            with dve.Fori(0, st.n) as i:
                def wcol(j):
                    return col(VT[:, 0, :], i + (64 + 8 * j))
                for b, dst in ((0, Bt), (1, Ct)):
                    dve.drain()
                    evac_wait(dve, st, i, b)
                    for gi, c0, nn in GXC:
                        op = dve.tensor_copy(dst[:, c0:c0 + nn], psl[:, b % 2, gi, 0:nn])
                    op.then_inc(evac_done, 1)
                dve.drain()
                evac_wait(dve, st, i, 2)
                for gi, c0, nn in GXC:
                    op = dve.tensor_tensor(U[:, c0:c0 + nn], psl[:, 0, gi, 0:nn], Ct[:, c0:c0 + nn], ALU.mult)
                op.then_inc(evac_done, 2)
                dve.drain()
                dve.tensor_scalar(Z, U, wcol(1), None, ALU.mult)
                dve.drain()
                Zr = Z[:, 0:TX].rearrange("p (r w) -> p r w", w=GRID_W)
                Ur = U[:, 0:TX].rearrange("p (r w) -> p r w", w=GRID_W)
                for (dz, du, j) in ((slice(1, GRID_W), slice(0, GRID_W - 1), 0), (slice(0, GRID_W - 1), slice(1, GRID_W), 2)):
                    dve.scalar_tensor_tensor(out=Zr[:, :, dz], in0=Ur[:, :, du], scalar=wcol(j), in1=Zr[:, :, dz],
                                             op0=ALU.mult, op1=ALU.add)
                    dve.drain()
                for (dz, du, j) in ((slice(TX + 1, TA), slice(TX, TA - 1), 0), (slice(TX, TA - 1), slice(TX + 1, TA), 2)):
                    dve.scalar_tensor_tensor(out=Z[:, dz], in0=U[:, du], scalar=wcol(j), in1=Z[:, dz],
                                             op0=ALU.mult, op1=ALU.add)
                    dve.drain()
                dve.tensor_tensor(Z, Z, Bt, ALU.mult).then_inc(split_ready, 1)
                dve_split(dve, i + sp, Z, tile_at(GA[:, 0, :, :], i), tile_at(GA[:, 1, :, :], i))

        gate_mm = sem("gate_mm")
        gate_f = sem("gate_f")
        gate_ln = sem("gate_ln")
        gate_m = sem("gate_m")
        gate_e = sem("gate_e")
        gate_t = sem("gate_t")
        gate_c = sem("gate_c")

        def pe_gates(pe):
            pe.wait_ge(wif_in, 64)
            pe.wait_ge(split_ready, N["n2"][2] + KT)
            for gi, c0, n in GXC:
                for k in range(KT):
                    mm = pe.matmul(psa[:, 2 + gi, 0:n], WIF[:, k, :], Y[:, k, c0:c0 + n], start=(k == 0), stop=(k == KT - 1))
            mm.then_inc(gate_mm, 1)

        def pe_gate_columns(pe):
            pe.wait_ge(gate_f, 2)
            for r in range(2):
                for st in range(6):
                    tr = pe.transpose(psa[:, 0, (r * 6 + st) * 8:(r * 6 + st) * 8 + 8], IG[:, r, st * P:st * P + P],
                                      ident[0:8, 0:8])
            tr.then_inc(gate_t, 1)

        def act_gate_logs(act):
            act.wait_ge(gate_f, 1)
            for fn, sc, bi in ((ACT.Abs, 1.0, 0.0), (ACT.Exp, -1.0, 0.0), (ACT.Ln, 1.0, 1.0)):
                for r in range(2):
                    op = act.activation(LF[:, 2 + r, :], LF[:, (0 if fn == ACT.Abs else 2) + r, :], fn, bias=bi, scale=sc)
                if fn != ACT.Ln:
                    act.drain()
            op.then_inc(gate_ln, 1)

        def act_gate_exps(act):
            act.wait_ge(gate_m, 1)
            for r in range(2):
                op = act.activation(BR[:, r, 0:TX], LF[:, 2 + r, 0:TX], ACT.Exp, scale=-1.0)
            op.then_inc(gate_e, 1)

        def dve_gates(dve):
            dve.drain()
            dve.wait_ge(gate_mm, 1)
            rows = [IG[:, 0, :], IG[:, 1, :], LF[:, 0, :], LF[:, 1, :]]
            for q in range(4):
                dve.tensor_copy(rows[q][:, 0:TX], psa[32 * q:32 * q + 8, 2, :])
                dve.tensor_copy(rows[q][:, TX:TA], psa[32 * q:32 * q + 8, 3, 0:TC])
            dve.memset(LF[:, 4, :], 0.0)
            dve.drain()
            for q in (0, 1, 2, 3):
                op = dve.tensor_scalar(rows[q], rows[q], SM[0:8, q:q + 1], None, ALU.add)
            op.then_inc(gate_f, 1)

        def dve_gate_scans(dve):
            dve.wait_ge(gate_ln, 1)
            zero = LF[:, 4, :]
            for r in range(2):
                dve.scalar_tensor_tensor(out=LF[:, r, :], in0=LF[:, r, :], scalar=0.0, in1=LF[:, 2 + r, :],
                                         op0=ALU.min, op1=ALU.subtract)
            dve.drain()

            def view(t, r, lo, hi):
                return t[:, lo:hi] if r == 0 else t[:, lo:hi][:, ::-1]

            def last(t, r):
                return t[:, TA - 1:TA] if r == 0 else t[:, TX:TX + 1]

            for r in range(2):
                b = BR[:, r, :]
                dve.tensor_tensor_scan(view(b, r, TX, TA), zero[:, 0:TC], view(LF[:, r, :], r, TX, TA), 0.0, ALU.add, ALU.add)
                dve.drain()
                dve.tensor_tensor_scan(view(b, r, 0, TX), zero[:, 0:TX], view(LF[:, r, :], r, 0, TX), last(b, r),
                                       ALU.add, ALU.add)
            dve.drain()
            op = dve.tensor_tensor(IG[:, :, :], IG[:, :, :], BR[:, :, :], ALU.subtract)
            op.then_inc(gate_f, 1)
            dve.drain()
            for r in range(2):
                g, t = IG[:, r, :], LF[:, 5, :]
                dve.tensor_tensor_scan(view(t, r, TX, TA), zero[:, 0:TC], view(g, r, TX, TA), 0.0, ALU.add, ALU.max)
                dve.drain()
                dve.tensor_tensor_scan(view(MROW[:, r, :], r, 0, TX), zero[:, 0:TX], view(g, r, 0, TX), last(t, r),
                                       ALU.add, ALU.max)
                dve.drain()
                op = dve.tensor_tensor(LF[:, 2 + r, 0:TX], BR[:, r, 0:TX], MROW[:, r, :], ALU.add)
                dve.drain()
            dve.drain().then_inc(gate_m, 1)

        def dve_gate_columns(dve):
            dve.wait_ge(gate_t, 1)
            dve.tensor_copy(X[:, 6, TX:TX + 96], psa[:, 0, 0:96]).then_inc(gate_c, 1)
            dve.wait_ge(gate_e, 1)

        ml_vt = sem("ml_v_transposed")
        ml_vk = sem("ml_v_ready")
        ml_sig = sem("ml_gate_exp")
        ml_rows = sem("ml_rows")
        ml_mb = sem("ml_rows_spread")
        ml_me = sem("ml_mneg_ready")
        ml_s = sem("ml_scores")
        ml_e = sem("ml_weights")
        ml_p = sem("ml_weighted")
        ml_pv = sem("ml_summed")
        ml_h = sem("ml_h_ready")
        ml_hq = sem("ml_h_squared")
        ml_hs = sem("ml_h_ssq")
        ml_hr = sem("ml_h_rstd")
        SEQ = [4, 5, 0, 1, 2, 3]

        def span(st, r):
            if st >= 4:
                return 0, TX
            return (P * st, TX) if r == 0 else (0, P * (st + 1))

        def vtok(a_, st):
            c = a_ * 6 + st
            return X[:, c // 2, TX + (c % 2) * P:TX + (c % 2) * P + P]

        def ml_rounds(eng, pair):
            with eng.Fori(0, HEADS // 2 - 2) as i:
                pair(i, i + 1)
            pair(HEADS // 2 - 2, HEADS // 2 - 1)
            pair(HEADS // 2 - 1, None)

        numden = [(psa[:, 2, :], psa[:, 3, :]), (psl[:, 1, 0, :], psl[:, 1, 1, :])]

        def weights(n, r):
            return ME[:, r, :] if n % 2 == 0 else ME2[r][:, :]

        def pe_mlstm(pe):
            st_, sp = S["mlstm"], N["mlstm"]

            def unit_of(n, b, kwait=None):
                pe_unit(pe, st_, n, b, HA, kwait, slots=1)

            def values(n, a_, b):
                pe.wait_ge(evac_done, h_of(st_, n, b) + st_.inc[b])
                for st in range(6):
                    tr = pe.transpose(psl[:, 0, st // 4, (st % 4) * P:(st % 4) * P + P], MV[:, st * P:st * P + P], ident[:])
                tr.then_inc(ml_vt, 1)
                pe.wait_ge(ml_vk, n * 2 + (a_ + 1))

            def first_units(n, kwait=None):
                unit_of(n, 0, kwait)
                values(n, 0, 0)
                unit_of(n, 1)

            unit_of(0, 0, N["n2"][2])
            pe_gates(pe)
            values(0, 0, 0)
            for b in (1, 2):
                unit_of(0, b)
            values(0, 1, 2)
            for b in (3, 4, 5):
                unit_of(0, b)
            pe_gate_columns(pe)
            pe.wait_ge(gate_c, 1)

            def head(i, a_, nxt):
                lo = 64 * a_
                if a_ == 0:
                    pe.wait_ge(evac_done, i * 8 + (st_.h0 + 8))

                def spread(r2):
                    pe.wait_ge(ml_rows, i * 4 + (2 * a_ + 1 + r2))
                    for r in range(2):
                        mm = pe.matmul(psa[:, r, :], ones[0:8, :], RH[:, r, :], start=True, stop=True)
                    mm.then_inc(ml_mb, 1)

                def scores(n):
                    if n >= 2:
                        pe.wait_ge(ml_p, i * 24 + (12 * a_ + 2 * (n - 1)))
                    pe.matmul(psa[:, n % 2, :], MK[lo:lo + 64, SEQ[n] * P:SEQ[n] * P + P], MQ[lo:lo + 64, :],
                              start=True, stop=True).then_inc(ml_s, 1)

                spread(0)
                pe.wait_ge(ml_me, i * 4 + (2 * a_ + 1))
                scores(0)
                for n in range(6):
                    if n < 5:
                        scores(n + 1)
                    for r in range(2):
                        t0, t1 = span(SEQ[n], r)
                        pe.wait_ge(ml_p, i * 24 + (12 * a_ + 2 * n + r + 1))
                        pe.matmul(numden[r][0][:, t0:t1], vtok(a_, SEQ[n]), weights(n, r)[:, t0:t1], start=(n == 0),
                                  stop=(n == 5), skip_group_check=True)
                        mm = pe.matmul(numden[r][1][:, t0:t1], ones[:], weights(n, r)[:, t0:t1], start=(n == 0),
                                       stop=(n == 5), skip_group_check=True)
                    mm.then_inc(ml_pv, 1)
                spread(1)
                if nxt is not None:
                    if a_ == 0:
                        first_units(nxt)
                    else:
                        values(nxt, 1, 2)
                        unit_of(nxt, 3)
                        unit_of(nxt, 4)
                pe.wait_ge(ml_hq, i * 2 + (a_ + 1))
                pe.matmul(psa[:, 0, :], ones[:], ME[:, 0, :], start=True, stop=True).then_inc(ml_hs, 1)
                if nxt is not None:
                    unit_of(nxt, 2 if a_ == 0 else 5)

            def pair(i, nxt):
                head(i, 0, nxt)
                head(i, 1, nxt)

            ml_rounds(pe, pair)

        def act_mlstm(act):
            st_, sp = S["mlstm"], N["mlstm"]
            act_hi(act, st_, 0, 0)
            act_gate_logs(act)
            for b in range(1, 6):
                act_hi(act, st_, 0, b)
            act_gate_exps(act)
            for b in (6, 7):
                act_hi(act, st_, 0, b)

            def head(i, a_, nxt):
                def hi_of(*bs):
                    for b in bs:
                        if nxt is not None:
                            act_hi(act, st_, nxt, b)

                if a_ == 0:
                    act.wait_ge(evac_done, i * 8 + (st_.h0 + 8))
                act.activation(MO[:, a_, :], MO[:, a_, :], ACT.Exp, scale=-1.0).then_inc(ml_sig, 1)
                for n in range(6):
                    st = SEQ[n]
                    if n in (0, 2):
                        act.wait_ge(ml_me, i * 4 + (2 * a_ + 1 + n // 2))
                    act.wait_ge(ml_pv, i * 12 + (6 * a_ + n + 1))
                    for r in range(2):
                        g = GCOL[:, r, st, bass.ds(i * 2 + a_, 1)]
                        if st >= 4:
                            op = act.activation(weights(n, r), MN[:, r, :], ACT.Exp, bias=g)
                        else:
                            d0 = st * P
                            t0, t1 = (d0 + P, TX) if r == 0 else (0, d0)
                            if t1 > t0:
                                act.activation(weights(n, r)[:, t0:t1], MN[:, r, t0:t1], ACT.Exp, bias=g)
                            op = act.activation(weights(n, r)[:, d0:d0 + P], MM[:, r, d0:d0 + P], ACT.Exp, bias=g)
                        op.then_inc(ml_e, 1)
                hi_of(*((0, 1) if a_ == 0 else (3, 4)))
                act.wait_ge(ml_h, i * 2 + (a_ + 1))
                act.activation(ME[:, 0, :], HS[:, :], ACT.Square).then_inc(ml_hq, 1)
                act.wait_ge(ml_hs, i * 2 + (a_ + 1))
                act.activation(MM[:, 0, :], psa[:, 0, :], ACT.Ln, bias=EPS, scale=1.0 / P)
                act.drain()
                act.activation(MM[:, 0, :], MM[:, 0, :], ACT.Exp, scale=-0.5).then_inc(ml_hr, 1)
                act_split(act, i * 2 + (sp + a_), MT[:, :], tile_at(G1[:, 0, :, :], i * 2 + a_))
                hi_of(*((2,) if a_ == 0 else (5, 6, 7)))

            def pair(i, nxt):
                head(i, 0, nxt)
                head(i, 1, nxt)

            ml_rounds(act, pair)

        def dve_mlstm(dve):
            st_, sp = S["mlstm"], N["mlstm"]
            dst = [MV, MV, MO[:, 0, :], MQ, MK, MO[:, 1, :]]

            def take_unit(n, b):
                dve.drain()
                evac_wait(dve, st_, n, b)
                d = dst[b]
                if b == 3:
                    op = dve.tensor_scalar(d[:, 0:TX], psl[:, 0, 0, :], 64 ** -0.5, None, ALU.mult)
                else:
                    op = dve.tensor_copy(d[:, 0:TX], psl[:, 0, 0, :])
                if b in (0, 1, 4):
                    op = dve.tensor_copy(d[:, TX:TA], psl[:, 0, 1, 0:TC])
                op.then_inc(evac_done, st_.inc[b])

            def take_values(n, a_):
                dve.drain()
                dve.wait_ge(ml_vt, n * 2 + (a_ + 1))
                dve.tensor_copy(X[:, 3 * a_:3 * a_ + 3, TX:TA],
                                psl[:, 0, :, :].rearrange("p a n -> p (a n)")[:, 0:768].rearrange("p (a n) -> p a n", n=2 * P))\
                   .then_inc(ml_vk, 1)

            take_unit(0, 0)
            take_values(0, 0)
            dve_gates(dve)
            take_unit(0, 1)
            dve_gate_scans(dve)
            take_unit(0, 2)
            take_values(0, 1)
            for b in (3, 4, 5):
                take_unit(0, b)
            dve_gate_columns(dve)

            def head(i, a_, nxt):
                onehot = ident[0:8, bass.ds(i * 2 + a_, 1)]
                dve.tensor_scalar(RH[:, :, :], MROW[:, :, :], onehot, None, ALU.mult).then_inc(ml_rows, 1)
                dve.wait_ge(ml_mb, i * 4 + (2 * a_ + 1))
                dve.tensor_scalar(MN[:, :, :], psa[:, 0:2, :], -1.0, None, ALU.mult).then_inc(ml_me, 1)
                dve.drain()
                for r in range(2):
                    op = dve.tensor_tensor(MM[:, r, :].rearrange("p (a n) -> p a n", a=4),
                                           MN[:, r, :].rearrange("p (a n) -> p a n", a=4),
                                           MASK[:, r:r + 1, :].to_broadcast([P, 4, P]), ALU.add)
                op.then_inc(ml_me, 1)
                for n in range(6):
                    dve.wait_ge(ml_s, i * 12 + (6 * a_ + n + 1))
                    for r in range(2):
                        t0, t1 = span(SEQ[n], r)
                        dve.wait_ge(ml_e, i * 24 + (12 * a_ + 2 * n + r + 1))
                        e = weights(n, r)[:, t0:t1]
                        dve.tensor_tensor(e, psa[:, n % 2, t0:t1], e, ALU.mult)\
                           .then_inc(ml_p, 1)
                dve.tensor_scalar(RH[:, :, :], BR[:, :, 0:TX], onehot, None, ALU.mult).then_inc(ml_rows, 1)
                if a_ == 1 and nxt is not None:
                    take_values(nxt, 1)
                dve.wait_ge(ml_mb, i * 4 + (2 * a_ + 2))
                dve.wait_ge(ml_pv, i * 12 + (6 * a_ + 8))
                for r in range(2):
                    num, den = numden[r]
                    if r == 1:
                        dve.drain()
                    dve.tensor_copy(RD[:, :], den)
                    dve.drain()
                    dve.scalar_tensor_tensor(out=RD[:, :], in0=RD[:, :], scalar=-1.0, in1=RD[:, :], op0=ALU.mult,
                                             op1=ALU.max)
                    dve.drain()
                    dve.tensor_tensor(RD[:, :], RD[:, :], psa[:, r, :], ALU.max)
                    dve.drain()
                    dve.reciprocal(RD[:, :], RD[:, :])
                    dve.drain()
                    if r == 0:
                        dve.tensor_tensor(HS[:, :], num, RD[:, :], ALU.mult)
                        if nxt is not None:
                            take_unit(nxt, 0 if a_ == 0 else 3)
                            if a_ == 0:
                                take_values(nxt, 0)
                    else:
                        dve.tensor_tensor(MT[:, :], num, RD[:, :], ALU.mult)
                        dve.drain()
                        dve.tensor_tensor(HS[:, :], HS[:, :], MT[:, :], ALU.add).then_inc(ml_h, 1)
                dve.wait_ge(ml_sig, i * 2 + (a_ + 1))
                dve.tensor_scalar(MO[:, a_, :], MO[:, a_, :], 1.0, None, ALU.add)
                dve.drain()
                dve.reciprocal(MO[:, a_, :], MO[:, a_, :])
                if nxt is not None:
                    take_unit(nxt, 1 if a_ == 0 else 4)
                dve.drain()
                dve.wait_ge(ml_hr, i * 2 + (a_ + 1))
                dve.tensor_tensor(MT[:, :], HS[:, :], MM[:, 0, :], ALU.mult)
                dve.drain()
                dve.scalar_tensor_tensor(out=MT[:, :], in0=MT[:, :], scalar=col(VT[:, 0, :], i * 2 + (88 + a_)),
                                         in1=MO[:, a_, :], op0=ALU.mult, op1=ALU.mult).then_inc(split_ready, 1)
                if nxt is not None:
                    take_unit(nxt, 2 if a_ == 0 else 5)
                dve_split(dve, i * 2 + (sp + a_), MT[:, :], tile_at(G1[:, 0, :, :], i * 2 + a_),
                          tile_at(G1[:, 1, :, :], i * 2 + a_))

            def pair(i, nxt):
                head(i, 0, nxt)
                head(i, 1, nxt)

            ml_rounds(dve, pair)

        mem_tr = sem("mem_transposed")
        mem_f = sem("mem_f_ready")

        def pe_mem(pe):
            pe.wait_ge(mem_in, 16)
            for k in range(KT):
                for t in range(2):
                    o = (k * 2 + t) * P
                    tr = pe.transpose(psa[:, o // 512, o % 512:o % 512 + P], MEMT[:, t, k * P:k * P + P], ident[:])
            tr.then_inc(mem_tr, 1)

        def dve_mem(dve):
            dve.drain()
            dve.wait_ge(mem_tr, 1)
            dve.tensor_copy(MEMF[:, :, :].rearrange("p k n -> p (k n)"), psa[:, :, :].rearrange("p a n -> p (a n)"))
            dve.drain()
            for k in range(KT):
                dve.drain().then_inc(split_ready, 1)
                dve_split(dve, N["mem"] + k, MEMF[:, k, :], MEMH[:, 0, k, :], MEMH[:, 1, k, :])

        def act_mem(act):
            for k in range(KT):
                act_split(act, N["mem"] + k, MEMF[:, k, :], MEMH[:, 0, k, :])

        lam_b = sem("lam_products")
        lam_s = sem("lam_sums")
        lam_e = sem("lam_exp")
        dist_i = sem("dist_iota")
        df_vt = sem("df_v_transposed")
        df_vk = sem("df_v_ready")
        df_s = sem("df_scores")
        df_u = sem("df_scores_used")
        df_m = sem("df_max")
        df_e = sem("df_exp")
        df_a = sem("df_attn")
        df_t = sem("df_attn_transposed")
        df_c = sem("df_attn_copied")
        df_p = sem("df_out")
        df_q = sem("df_squared")
        df_z = sem("df_ssq")
        df_r = sem("df_rstd")

        def pe_lam(pe):
            pe.wait_ge(lam_b, 1)
            pe.matmul(psl[:, 1, 0, 0:2], ones[0:64, :], SM[0:64, 28:30], start=True, stop=True).then_inc(lam_s, 1)

        def act_lam(act):
            act.wait_ge(lam_s, 1)
            act.activation(SM[:, 8:10], psl[:, 1, 0, 0:2], ACT.Exp).then_inc(lam_e, 1)

        def dve_lam(dve):
            dve.wait_ge(lam_e, 1)
            dve.tensor_tensor(SM[:, 10:11], SM[:, 9:10], SM[:, 8:9], ALU.subtract)
            dve.drain()
            dve.tensor_scalar(SM[:, 10:11], SM[:, 10:11], -LAMBDA_INIT, None, ALU.add)
            dve.tensor_scalar(SM[:, 11:12], VT[:, 0, 112:113], 1.0 - LAMBDA_INIT, None, ALU.mult)
            dve.wait_ge(dist_i, 1)
            dve.tensor_copy(DIST[:, :].rearrange("p (a n) -> p a n", a=4), DISTI)
            dve.drain()
            dve.scalar_tensor_tensor(out=DIST[:, :], in0=DIST[:, :], scalar=-1.0, in1=DIST[:, :], op0=ALU.mult, op1=ALU.max)
            dve.drain()

        def diff_after(i, r):
            if r == 0:
                return i, 1
            if isinstance(i, int) and i == HEADS // 2 - 1:
                return None
            return i + 1, 0

        def diff_rounds(eng, step):
            with eng.Fori(0, HEADS // 2 - 1) as i:
                for r in range(2):
                    step(i, r)
            for r in range(2):
                step(HEADS // 2 - 1, r)

        def pe_diff(pe):
            st_, sp = S["diff"], N["mix0"]

            def unit_of(at, j):
                if at is not None:
                    pe_unit(pe, st_, at[0], 4 * at[1] + j, HB)

            for j in range(3):
                pe_unit(pe, st_, 0, j, HB, N["xb"] if j == 0 else None)
            pe_mem(pe)
            pe.wait_ge(split_ready, N["mem"] + 8)

            def step(i, r):
                nxt = diff_after(i, r)
                pe.wait_ge(evac_done, i * 8 + (st_.h0 + 4 * r + 4))

                def scores(t):
                    if t >= 2:
                        pe.wait_ge(df_u, i * 16 + (8 * r + 2 * (t - 1)))
                    for c in range(2):
                        pe.matmul(psa[:, 2 * (t % 2) + c, :], AQ[64 * c:64 * c + 64, r, t * P:t * P + P],
                                  AK[64 * c:64 * c + 64, r, :], start=True, stop=True).then_inc(df_s, 1)

                def turn(t):
                    pe.wait_ge(df_a, i * 8 + (4 * r + t + 1))
                    if t >= 1:
                        pe.wait_ge(df_c, i * 8 + (4 * r + t))
                    for kt in range(4):
                        tr = pe.transpose(psl[:, 1, 1, kt * P:kt * P + P], DS[:, t % 2, 0, kt * P:kt * P + P], ident[:])
                    tr.then_inc(df_t, 1)

                scores(0)
                scores(1)
                unit_of(nxt, 0)
                pe.wait_ge(split_ready, i * 2 + (sp + r))
                for t in range(4):
                    tr = pe.transpose(psl[:, 0, 1, t * P:t * P + P], AV[:, t * P:t * P + P], ident[:])
                tr.then_inc(df_vt, 1)
                turn(0)
                scores(2)
                unit_of(nxt, 1)
                turn(1)
                scores(3)
                turn(2)
                unit_of(nxt, 2)
                turn(3)
                pe.wait_ge(df_vk, i * 2 + (r + 1))
                pe.wait_ge(df_c, i * 8 + (4 * r + 4))
                for kt in range(4):
                    mm = pe.matmul(psl[:, 0, 1, :], VTK[:, kt, :], AT[:, kt, :], start=(kt == 0), stop=(kt == 3))
                mm.then_inc(df_p, 1)
                pe.wait_ge(df_q, i * 2 + (r + 1))
                pe.matmul(psl[:, 1, 1, :], ones[:], TB, start=True, stop=True).then_inc(df_z, 1)

            diff_rounds(pe, step)

        def act_diff(act):
            st_, sp = S["diff"], N["mix0"]

            def hi_of(at, j):
                if at is not None:
                    act_hi(act, st_, at[0], 4 * at[1] + j)

            for j in range(4):
                hi_of((0, 0), j)
            act_mem(act)

            def step(i, r):
                nxt = diff_after(i, r)
                def expo(t):
                    act.wait_ge(df_m, i * 8 + (4 * r + t + 1))
                    for c in range(2):
                        act.activation(DS[:, t % 2, c, :], DS[:, t % 2, c, :], ACT.Exp, bias=DST[:, t, 1, c:c + 1],
                                       accum_out=DST[:, t, 2, c:c + 1]).then_inc(df_e, 1)

                def copy(t):
                    act.wait_ge(df_t, i * 8 + (4 * r + t + 1))
                    act.activation(AT[:, :, t * P:t * P + P], psl[:, 1, 1, :].rearrange("p (a n) -> p a n", a=4), ACT.Copy)\
                       .then_inc(df_c, 1)

                expo(0)
                expo(1)
                hi_of(nxt, 0)
                act.wait_ge(df_vt, i * 2 + (r + 1))
                act.activation(VTK[:, :, :].rearrange("p a n -> p (a n)"), psl[:, 0, 1, :], ACT.Copy).then_inc(df_vk, 1)
                copy(0)
                expo(2)
                hi_of(nxt, 1)
                copy(1)
                expo(3)
                copy(2)
                hi_of(nxt, 2)
                copy(3)
                act.wait_ge(df_p, i * 2 + (r + 1))
                act.activation(TB, psl[:, 0, 1, :], ACT.Square).then_inc(df_q, 1)
                act.wait_ge(df_z, i * 2 + (r + 1))
                act.activation(RBB, psl[:, 1, 1, :], ACT.Ln, bias=LN_EPS, scale=1.0 / P)
                act.drain()
                act.activation(RBB, RBB, ACT.Exp, scale=-0.5).then_inc(df_r, 1)
                hi_of(nxt, 3)
                act_split(act, i * 2 + (sp + r), ZB, tile_at(GB[:, 0, :, :], i * 2 + r))

            diff_rounds(act, step)

        def dve_diff(dve):
            st_, sp = S["diff"], N["mix0"]

            def take_unit(at, j):
                if at is None:
                    return
                i, r = at
                dve.drain()
                evac_wait(dve, st_, i, 4 * r + j)
                if j == 0:
                    op = dve.tensor_scalar(AQ[:, r, :], psl[:, 0, 0, :], 64 ** -0.5, None, ALU.mult)
                else:
                    op = dve.tensor_copy(AK[:, r, :] if j == 1 else AV[:, :], psl[:, j % 2, 0, :])
                op.then_inc(evac_done, st_.inc[4 * r + j])

            for j in range(3):
                take_unit((0, 0), j)
            dve_mem(dve)
            dve_lam(dve)

            def step(i, r):
                nxt = diff_after(i, r)
                head = i * 2 + r
                dve.tensor_scalar(SB[:, :], DIST[:, :], col(SLOPE[:, :], head), None, ALU.mult)

                def bias_max(t):
                    if t >= 2:
                        dve.wait_ge(df_t, i * 8 + (4 * r + t - 1))
                    off = 384 - t * P
                    dve.wait_ge(df_s, i * 16 + (8 * r + 2 * t + 2))
                    dve.tensor_copy(DST[:, t, 3, :], SM[:, 12:14])
                    dve.drain()
                    for c in range(2):
                        dve.tensor_tensor_reduce(DS[:, t % 2, c, :], psa[:, 2 * (t % 2) + c, :], SB[:, off:off + TX], 1.0,
                                                 -3e38, ALU.add, ALU.max, DST[:, t, 0, c:c + 1]).then_inc(df_u, 1)
                    dve.drain()
                    dve.tensor_scalar(DST[:, t, 1, :], DST[:, t, 0, :], -1.0, None, ALU.mult).then_inc(df_m, 1)

                def combine(t):
                    dve.wait_ge(df_e, i * 16 + (8 * r + 2 * t + 2))
                    dve.reciprocal(DST[:, t, 3, :], DST[:, t, 2, :])
                    dve.drain()
                    dve.tensor_scalar(DST[:, t, 3, 1:2], DST[:, t, 3, 1:2], SM[:, 10:11], None, ALU.mult)
                    dve.tensor_scalar(DS[:, t % 2, 0, :], DS[:, t % 2, 0, :], DST[:, t, 3, 0:1], None, ALU.mult)
                    dve.drain()
                    dve.scalar_tensor_tensor(out=DS[:, t % 2, 0, :], in0=DS[:, t % 2, 1, :], scalar=DST[:, t, 3, 1:2],
                                             in1=DS[:, t % 2, 0, :], op0=ALU.mult, op1=ALU.add).then_inc(df_a, 1)

                bias_max(0)
                bias_max(1)
                combine(0)
                combine(1)
                take_unit(nxt, 0)
                bias_max(2)
                combine(2)
                take_unit(nxt, 1)
                bias_max(3)
                combine(3)
                take_unit(nxt, 2)
                dve.wait_ge(df_r, i * 2 + (r + 1))
                dve.tensor_tensor(ZB, psl[:, 0, 1, :], RBB, ALU.mult)
                dve.drain()
                dve.tensor_scalar(ZB, ZB, SM[:, 11:12], None, ALU.mult).then_inc(split_ready, 1)
                dve_split(dve, i * 2 + (sp + r), ZB, tile_at(GB[:, 0, :, :], i * 2 + r),
                          tile_at(GB[:, 1, :, :], i * 2 + r))

            diff_rounds(dve, step)

        def xatt_parts(l):
            vt, vk, xs, xm, xe, xa, xt, xc, xp, xz = (sem(f"xa{l}_{n}") for n in
                ("v_transposed", "v_ready", "scores", "max", "exp", "probs", "probs_transposed", "probs_copied",
                 "out", "out_taken"))
            st_, sp = S[f"xatt{l}"], N[f"xatt{l}"]
            XS = DS[:, 0, :, :].rearrange("p a n -> p (a n)").rearrange("p (t m) -> p t m", t=4)
            STT = DST[:, :, :, :].rearrange("p a b c -> p (a b c)")
            V2 = AV[:, :].rearrange("p (e m) -> p e m", e=2)
            VK = VTK[:, :, :].rearrange("p a n -> p (a n)").rearrange("p (m n) -> p m n", m=2)

            def pe_part(pe):
                with pe.Fori(0, st_.n) as i:
                    for b in range(6):
                        if b < 4:
                            pe_unit(pe, st_, i, b, MEMH, N["mem"] if b == 0 else None)
                        else:
                            pe_unit(pe, st_, i, b, HB, N[f"ln{l}0"][3] if b == 4 else None)
                    pe.wait_ge(split_done, i * 2 + sp)
                    pe.wait_ge(evac_done, i * 8 + (st_.h0 + 8))
                    for m in range(2):
                        for e in range(2):
                            tr = pe.transpose(psl[:, 0, 1, (m * 2 + e) * P:(m * 2 + e) * P + P],
                                              AV[:, e * TM + m * P:e * TM + m * P + P], ident[:])
                    tr.then_inc(vt, 1)
                    for t in range(4):
                        for e in range(2):
                            mm = pe.matmul(psa[:, t, 0:TM], AQ[:, e, t * P:t * P + P], AK[:, e, 0:TM], start=(e == 0),
                                           stop=(e == 1))
                        mm.then_inc(xs, 1)
                    pe.wait_ge(vk, i + 1)
                    for t in range(4):
                        pe.wait_ge(xa, i * 4 + (t + 1))
                        if t >= 2:
                            pe.wait_ge(xc, i * 4 + (t - 1))
                        for m in range(2):
                            tr = pe.transpose(psl[:, t % 2, 1, m * P:m * P + P], XS[:, t, m * P:m * P + P], ident[:])
                        tr.then_inc(xt, 1)
                    pe.wait_ge(xc, i * 4 + 4)
                    for e in range(2):
                        for m in range(2):
                            mm = pe.matmul(psa[:, e, :], VK[:, m, e * P:e * P + P], AT[:, m, :], start=(m == 0), stop=(m == 1))
                        mm.then_inc(xp, 1)

            def act_early(act, k):
                if k == 2:
                    act_hi(act, st_, 0, 0)

            def act_part(act):
                def body(i):
                    for b in range(8):
                        if b > 0 or not (isinstance(i, int) and i == 0):
                            act_hi(act, st_, i, b)
                    act.wait_ge(vt, i + 1)
                    act.activation(VTK[:, :, :].rearrange("p a n -> p (a n)"), psl[:, 0, 1, :], ACT.Copy).then_inc(vk, 1)
                    for t in range(4):
                        act.wait_ge(xm, i * 4 + (t + 1))
                        act.activation(XS[:, t, :], psa[:, t, 0:TM], ACT.Exp, bias=STT[:, 4 + t:5 + t],
                                       accum_out=STT[:, 8 + t:9 + t]).then_inc(xe, 1)
                    for t in range(4):
                        act.wait_ge(xt, i * 4 + (t + 1))
                        act.activation(AT[:, 0:2, t * P:t * P + P],
                                       psl[:, t % 2, 1, 0:2 * P]
                                       .rearrange("p (a n) -> p a n", a=2), ACT.Copy).then_inc(xc, 1)
                    for e in range(2):
                        act_split(act, i * 2 + (sp + e), WB[:, e, :], tile_at(GB[:, 0, :, :], i * 2 + e))
                body(0)
                with act.Fori(1, st_.n - 1) as i:
                    body(i)
                body(st_.n - 1)

            def take_unit(dve, i, b):
                dve.drain()
                evac_wait(dve, st_, i, b)
                if b < 2:
                    op = dve.tensor_copy(AK[:, b, 0:TM], psl[:, b % 2, 0, 0:TM])
                elif b < 4:
                    op = dve.tensor_copy(V2[:, b - 2, :], psl[:, b % 2, 0, 0:TM])
                else:
                    op = dve.tensor_scalar(AQ[:, b - 4, :], psl[:, b % 2, 0, :], 256 ** -0.5, None, ALU.mult)
                op.then_inc(evac_done, st_.inc[b])

            def dve_early(dve, k):
                if k in (2, 4, 6, 8):
                    take_unit(dve, 0, k // 2 - 1)

            def dve_part(dve):
                def body(i):
                    for b in range(4 if isinstance(i, int) else 0, 6):
                        take_unit(dve, i, b)
                    for t in range(4):
                        dve.wait_ge(xs, i * 4 + (t + 1))
                        dve.tensor_reduce(STT[:, t:t + 1], psa[:, t, 0:TM], AXX, ALU.max)
                        dve.drain()
                        dve.tensor_scalar(STT[:, 4 + t:5 + t], STT[:, t:t + 1], -1.0, None, ALU.mult).then_inc(xm, 1)
                    for t in range(4):
                        dve.wait_ge(xe, i * 4 + (t + 1))
                        dve.reciprocal(STT[:, 12 + t:13 + t], STT[:, 8 + t:9 + t])
                        dve.drain()
                        dve.tensor_scalar(XS[:, t, :], XS[:, t, :], STT[:, 12 + t:13 + t], None, ALU.mult).then_inc(xa, 1)
                    for e in range(2):
                        dve.wait_ge(xp, i * 2 + (e + 1))
                        dve.tensor_copy(WB[:, e, :], psa[:, e, :]).then_inc(split_ready, 1)
                    for e in range(2):
                        dve_split(dve, i * 2 + (sp + e), WB[:, e, :], tile_at(GB[:, 0, :, :], i * 2 + e),
                                  tile_at(GB[:, 1, :, :], i * 2 + e))
                body(0)
                with dve.Fori(1, st_.n) as i:
                    body(i)
            return pe_part, act_part, dve_part, act_early, dve_early

        xatt = [xatt_parts(0), xatt_parts(1)]

        dl_i = sem("dl_iota")
        dl_mf = sem("dl_mask_float")
        dl_mk = sem("dl_mask")
        dl_vt = sem("dl_v_transposed")
        dl_vk = sem("dl_v_ready")
        dl_s = sem("dl_scores")
        dl_m = sem("dl_max")
        dl_e = sem("dl_exp")
        dl_t = sem("dl_p_transposed")
        dl_c = sem("dl_p_copied")
        dl_o = sem("dl_out")
        dl_q = sem("dl_out_taken")
        dl_x = sem("dl_rows_transposed")
        dl_y = sem("dl_rows_taken")
        dl_w1 = sem("dl_row_diff")
        dl_w2 = sem("dl_row_exp")
        dl_rw = sem("dl_rows_ready")
        dl_b = sem("dl_rows_spread")
        DIL = [1, 4, 16]
        LW = [2 * P, P, P]
        LOFF = [0, 384, 512]
        WIN = [0, 64, 192, 256]

        def perm(ap, g):
            if g == 0:
                return ap
            return ap.rearrange("p (u r) -> p r u", r=DIL[g])

        def ordered(ap, g):
            if g == 0:
                return ap
            return ap.rearrange("p (r u) -> p r u", r=DIL[g])

        def vkeys(g, t, ch):
            c = 2 * t + ch if g == 0 else t
            return X[:, c // 2, TX + (c % 2) * P:TX + (c % 2) * P + P]

        def table(g, t):
            if g == 0:
                delta = t * P - WIN[t]
                return LSB[:, P - delta:P - delta + 2 * P]
            return LSB[:, LOFF[g]:LOFF[g] + P]

        def dil_bank(i, g):
            if i % 2 == 0:
                return psa[:, g, :]
            return psa[:, 3, :] if g == 0 else psl[:, g - 1, 1, :]

        def dil_after(i, g):
            if g < 2:
                return i, g + 1
            if isinstance(i, int) and i == HEADS - 1:
                return None
            return i + 1, 0

        def dil_rounds(eng, step):
            with eng.Fori(0, HEADS - 1) as i:
                for g in range(3):
                    step(i, g)
            for g in range(3):
                step(HEADS - 1, g)

        def pe_dil(pe):
            st_ = S["dil"]

            def unit_of(at, j):
                if at is not None:
                    pe_unit(pe, st_, at[0], 4 * at[1] + j, HB)

            for j in range(3):
                pe_unit(pe, st_, 0, j, HB, N["ln02"][3] if j == 0 else None)

            def step(i, g):
                nxt = dil_after(i, g)
                Q = LQK[g]
                w, nt = LW[g], (8 if g == 0 else 4)
                pe.wait_ge(evac_done, i * 12 + (st_.h0 + 4 * g + 4))
                def scores(a_):
                    lo = 64 * a_
                    for t in range(4):
                        k0 = WIN[t] if g == 0 else t * P
                        mm = pe.matmul(psa[:, (t * w) // 512, (t * w) % 512:(t * w) % 512 + w],
                                       Q[lo:lo + 64, 0, t * P:t * P + P], Q[lo:lo + 64, 1, k0:k0 + w],
                                       start=True, stop=True)
                    mm.then_inc(dl_s, 1)

                def turn(a_):
                    n6 = 2 * g + a_
                    pe.wait_ge(dl_e, i * 6 + (n6 + 1))
                    for c in range(nt):
                        tr = pe.transpose(psa[:, 2 + c // 4, (c % 4) * P:(c % 4) * P + P], LP[:, c * P:c * P + P], ident[:])
                    tr.then_inc(dl_t, 1)

                def values(a_):
                    lo, n6 = 64 * a_, 2 * g + a_
                    if a_ == 0:
                        pe.wait_ge(dl_vk, i * 3 + (g + 1))
                    pe.wait_ge(dl_c, i * 6 + (n6 + 1))
                    for t in range(4):
                        for ch in range(2 if g == 0 else 1):
                            c = 2 * t + ch if g == 0 else t
                            mm = pe.matmul(psl[lo:lo + 64, 0, 1, t * P:t * P + P], vkeys(g, t, ch)[:, lo:lo + 64],
                                           LPT[:, c, :], start=(ch == 0), stop=(ch == (1 if g == 0 else 0)),
                                           skip_group_check=True)
                    mm.then_inc(dl_o, 1)

                scores(0)
                pe.wait_ge(dl_q, i * 3 + (g + 1))
                for c in range(nt):
                    t0 = WIN[c // 2] + (c % 2) * P if g == 0 else c * P
                    tr = pe.transpose(psl[:, c // 4, 1, (c % 4) * P:(c % 4) * P + P], LV[:, t0:t0 + P], ident[:])
                tr.then_inc(dl_vt, 1)
                unit_of(nxt, 0)
                turn(0)
                scores(1)
                unit_of(nxt, 1)
                values(0)
                turn(1)
                unit_of(nxt, 2)
                values(1)

            dil_rounds(pe, step)
            pe.wait_ge(dl_q, 3 * HEADS + 1)
            for q in range(2):
                for g in range(3):
                    if q == 1:
                        pe.wait_ge(dl_y, 1)
                    for t in range(4):
                        tr = pe.transpose(psa[0:16, g, t * P:t * P + P], LMS[:, q, g, t, :], ident[:])
                tr.then_inc(dl_x, 1)
            pe.wait_ge(dl_mk, 2)
            for i in range(HEADS):
                if i == 0:
                    pe.wait_ge(dl_rw, 1)
                elif i > 1:
                    pe.wait_ge(split_ready, N["mix1"] + i - 1)
                for g in range(3):
                    mm = pe.matmul(dil_bank(i, g), LSEL[:, i, :], LROW[:, g, :], start=True, stop=True)
                mm.then_inc(dl_b, 1)

        def act_dil(act):
            st_ = S["dil"]

            def hi_of(at, j):
                if at is not None:
                    act_hi(act, st_, at[0], 4 * at[1] + j)

            for j in range(4):
                hi_of((0, 0), j)

            def step(i, g):
                nxt = dil_after(i, g)
                w, nt = LW[g], (8 if g == 0 else 4)
                act.wait_ge(dl_vt, i * 3 + (g + 1))
                for h in range(nt // 4):
                    op = act.activation(X[:, 2 * h:2 * h + 2, TX:TA],
                                        psl[:, h, 1, :].rearrange("p (a n) -> p a n", a=2), ACT.Copy)
                op.then_inc(dl_vk, 1)
                hi_of(nxt, 0)
                for a_ in range(2):
                    n6 = 2 * g + a_
                    act.wait_ge(dl_m, i * 6 + (n6 + 1))
                    for t in range(4):
                        op = act.activation(LP[:, t * w:t * w + w], LP[:, t * w:t * w + w], ACT.Exp,
                                            bias=SM[:, 16 + t:17 + t], accum_out=LMS[:, 1, g, t, bass.ds(i * 2 + a_, 1)])
                    op.then_inc(dl_e, 1)
                    if a_ == 1:
                        hi_of(nxt, 2)
                    act.wait_ge(dl_t, i * 6 + (n6 + 1))
                    act.activation(LPT[:, 0:nt, :].rearrange("p a n -> p (a n)"),
                                   psa[:, 2:2 + nt // 4, :].rearrange("p a n -> p (a n)"), ACT.Copy).then_inc(dl_c, 1)
                    hi_of(nxt, 1 + 2 * a_)

            dil_rounds(act, step)
            act.wait_ge(dl_w1, 1)
            act.activation(LROW[:, 0:3, :], LROW[:, 0:3, :], ACT.Exp).then_inc(dl_w2, 1)
            for i in range(KT):
                act_split(act, N["mix1"] + i, LP[:, (i % 2) * TX:(i % 2) * TX + TX], HB[:, 0, i, :])

        def dve_dil_tables(dve):
            dve.wait_ge(dl_i, 1)
            dve.tensor_copy(LB[:, :], LBI[:, :])
            dve.drain()
            dve.scalar_tensor_tensor(out=LB[:, :], in0=LB[:, :], scalar=-1.0, in1=LB[:, :], op0=ALU.mult, op1=ALU.max)
            dve.drain()
            dve.drain().then_inc(dl_mf, 1)

        def dve_dil(dve):
            st_ = S["dil"]
            dve.wait_ge(dl_mk, 1)
            def take_unit(at, j):
                if at is None:
                    return
                i, g = at
                dve.drain()
                evac_wait(dve, st_, i, 4 * g + j)
                src, dst = perm(psl[:, j % 2, 0, :], g), ordered(LV[:, :] if j == 2 else LQK[g][:, j, :], g)
                if j == 0:
                    op = dve.tensor_scalar(dst, src, 64 ** -0.5, None, ALU.mult)
                else:
                    op = dve.tensor_copy(dst, src)
                op.then_inc(evac_done, st_.inc[4 * g + j])

            for j in range(3):
                take_unit((0, 0), j)

            def step(i, g):
                nxt = dil_after(i, g)
                w = LW[g]
                o, n = (0, 384) if g == 0 else (LOFF[g], P)
                for a_ in range(2):
                    n6 = 2 * g + a_
                    head = bass.ds(i * 2 + a_, 1)
                    dve.drain()
                    dve.tensor_scalar(LSB[:, o:o + n], LB[:, o:o + n], LSL[:, head], None, ALU.mult)
                    dve.drain()
                    dve.wait_ge(dl_s, i * 6 + (n6 + 1))
                    for t in range(4):
                        dve.tensor_tensor(LP[:, t * w:t * w + w], psa[:, (t * w) // 512, (t * w) % 512:(t * w) % 512 + w],
                                          table(g, t), ALU.add)
                    dve.drain()
                    dve.tensor_reduce(SM[:, 20:24], LP[:, 0:4 * w].rearrange("p (t w) -> p t w", t=4), AXX, ALU.max)
                    dve.drain()
                    dve.tensor_copy(LMS[:, 0, g, :, head].rearrange("p t a -> p (t a)"), SM[:, 20:24])
                    dve.tensor_scalar(SM[:, 16:20], SM[:, 20:24], -1.0, None, ALU.mult).then_inc(dl_m, 1)
                    take_unit(nxt, a_)
                take_unit(nxt, 2)
                dve.wait_ge(dl_o, i * 6 + (2 * g + 2))
                og = tile_at(OG[:, :, g, :], i) if g < 2 else tile_at(OG2[:, :, :], i)
                dve.tensor_copy(perm(og, g) if g else og, ordered(psl[:, 0, 1, :], g) if g else psl[:, 0, 1, :])\
                   .then_inc(dl_q, 1)

            dil_rounds(dve, step)
            for q in range(2):
                dve.drain()
                dve.wait_ge(dl_x, q + 1)
                for g in range(3):
                    dst, src = LROW[:, 3 * q + g, :], psa[0:16, g, :]
                    op = dve.tensor_copy(perm(dst, g) if g else dst, ordered(src, g) if g else src)
                op.then_inc(dl_y, 1)
            dve.drain()
            dve.tensor_tensor(LR2[:, :], LROW[:, 0, :], LROW[:, 1, :], ALU.max)
            dve.drain()
            dve.tensor_tensor(LR2[:, :], LR2[:, :], LROW[:, 2, :], ALU.max)
            dve.drain()
            for g in range(3):
                dve.tensor_tensor(LROW[:, g, :], LROW[:, g, :], LR2[:, :], ALU.subtract)
            dve.drain().then_inc(dl_w1, 1)
            dve.wait_ge(dl_w2, 1)
            for g in range(3):
                dve.tensor_tensor(LROW[:, 3 + g, :], LROW[:, 3 + g, :], LROW[:, g, :], ALU.mult)
            dve.drain()
            dve.tensor_tensor(LR2[:, :], LROW[:, 3, :], LROW[:, 4, :], ALU.add)
            dve.drain()
            dve.tensor_tensor(LR2[:, :], LR2[:, :], LROW[:, 5, :], ALU.add)
            dve.drain()
            dve.reciprocal(LR2[:, :], LR2[:, :])
            dve.drain()
            for g in range(3):
                dve.tensor_tensor(LROW[:, g, :], LROW[:, g, :], LR2[:, :], ALU.mult)
            dve.drain().then_inc(dl_rw, 1)
            for i in range(HEADS + 1):
                if i < HEADS:
                    parts = [OG[:, i, 0, :], OG[:, i, 1, :], OG2[:, i, :]]
                    A = LP[:, (i % 2) * TX:(i % 2) * TX + TX]
                    dve.wait_ge(dl_b, i + 1)
                    for g, part in enumerate(parts):
                        dve.tensor_tensor(part, part, dil_bank(i, g), ALU.mult)
                    dve.drain()
                    dve.tensor_tensor(A, parts[0], parts[1], ALU.add)
                    dve.drain()
                    dve.tensor_tensor(A, A, parts[2], ALU.add).then_inc(split_ready, 1)
                if i > 0:
                    o = ((i - 1) % 2) * TX
                    dve_split(dve, N["mix1"] + i - 1, LP[:, o:o + TX], HB[:, 0, i - 1, :], HB[:, 1, i - 1, :])

        block = ctx.enter_context(nc.Block())

        @block.sync
        def _(sp):
            sp.dma_start(XTOK[:, 0:4, :], a["x"][0].rearrange("(t p) d -> p t d", p=P)).then_inc(x_in, 16)
            sp.dma_start(XTOK[:, 4:6, :], a["ctx"][0].rearrange("(t p) d -> p t d", p=P)).then_inc(x_in, 16)
            before = None
            for st in plan.stages:
                if before is not None and st.raw:
                    sp.wait_ge(lo_ready, st.h0)
                if before is not None and before.raw:
                    sp.wait_ge(mod_used, before.m1)
                if st.name == "diff":
                    sp.wait_ge(split_done, N["mlstm"] + 8)
                    sp.dma_start(MEMT[:, :, :], a["mem_2"][0].rearrange("(t p) d -> p t d", p=P)).then_inc(mem_in, 16)
                with sp.Fori(0, st.n) as i:
                    for b, u in enumerate(st.body):
                        if u is None:
                            continue
                        if st.raw:
                            sp.wait_ge(mod_used, i * 4 + (st.m0 + b - 3))
                        else:
                            sp.wait_ge(lo_ready, i * st.B + (st.h0 + b - 3))
                        sp.dma_start(WR[:, b % RING, 0:st.kt, :], u(i)).then_inc(loaded[b % RING], 16)
                before = st
            sp.wait_ge(x_tr, 2)
            sp.dma_start(out[0].rearrange("(t p) d -> p t d", p=P), OTOK[:, :, :]).then_inc(out_sem, 16)
            sp.wait_ge(out_sem, 16)

        @block.gpsimd
        def _(pool):
            pool.sem_inc(lo_ready, RING)
            pool.memset(ident[:], 0.0)
            pool.memset(MASK[:, :, :], 0.0)
            pool.memset(ones[:], 1.0).then_inc(const_step, 1)
            pool.wait_ge(const_step, 1)
            pool.affine_select(out=ident[:], in_=ident[:], compare_op=ALU.not_equal, fill=1.0, base=0,
                               pattern=[[-1, P]], channel_multiplier=1).then_inc(const_step, 1)
            pool.affine_select(out=MASK[:, 0, :], in_=MASK[:, 0, :], compare_op=ALU.is_ge, fill=-BIG, base=0,
                               pattern=[[1, P]], channel_multiplier=-1).then_inc(const_step, 1)
            pool.affine_select(out=MASK[:, 1, :], in_=MASK[:, 1, :], compare_op=ALU.is_ge, fill=-BIG, base=0,
                               pattern=[[-1, P]], channel_multiplier=1).then_inc(const_step, 1)
            for h in range(HEADS):
                pool.memset(SLOPE[:, h:h + 1], -2.0 ** -(h + 1))
            for h in range(2 * HEADS):
                pool.memset(LSL[:, h:h + 1], -2.0 ** (-(h + 1) / 2))
            pool.memset(SM[:, 12:16], 0.0).then_inc(const_step, 1)
            pool.wait_ge(const_step, 5)
            pool.sem_inc(const_ready, 1)
            before = None
            for st in plan.stages:
                if st.raw:
                    before = st
                    continue
                if before is not None and before.raw:
                    pool.wait_ge(mod_used, before.m1)
                if st.name == "mlp1_up0":
                    pool.wait_ge(split_done, N["mlstm"] + 8)
                    pool.iota(DISTI, [[-224, 4], [-1, 224]], base=384, channel_multiplier=1).then_inc(dist_i, 1)
                if st.name == "ffn0_in1":
                    pool.wait_ge(split_done, N["ln01"][3] + 8)
                    pool.iota(LBI[:, 0:384], [[-1, 384]], base=P, channel_multiplier=1)
                    pool.iota(LBI[:, 384:512], [[-4, P]], base=0, channel_multiplier=4)
                    pool.iota(LBI[:, 512:640], [[-16, P]], base=0, channel_multiplier=16).then_inc(dl_i, 1)
                if st.name == "ffn0_out1":
                    pool.wait_ge(dl_mf, 1)
                    sel = dict(compare_op=ALU.is_ge, fill=BIG)
                    for k_, (o, n_, b0) in enumerate(((0, 384, P), (384, P, 0))):
                        t_ = LB[:, o:o + n_]
                        pool.affine_select(out=t_, in_=t_, base=64 + b0, pattern=[[-1, n_]], channel_multiplier=1, **sel)\
                            .then_inc(dl_i, 1)
                        pool.wait_ge(dl_i, 2 + 2 * k_)
                        pool.affine_select(out=t_, in_=t_, base=64 - b0, pattern=[[1, n_]], channel_multiplier=-1, **sel)\
                            .then_inc(dl_i, 1)
                        pool.wait_ge(dl_i, 3 + 2 * k_)
                    t_ = LB[:, 512:640].rearrange("p (b u) -> p b u", b=4)
                    pool.affine_select(out=t_, in_=t_, base=0, pattern=[[-32, 4], [0, 32]], channel_multiplier=1, **sel)\
                        .then_inc(dl_i, 1)
                    pool.wait_ge(dl_i, 6)
                    pool.affine_select(out=t_, in_=t_, base=31, pattern=[[32, 4], [0, 32]], channel_multiplier=-1, **sel)\
                        .then_inc(dl_mk, 1)
                if st.name == "dil_out":
                    pool.wait_ge(dl_q, 3 * HEADS + 1)
                    pool.memset(LSEL[:, :, :], 0.0).then_inc(dl_i, 1)
                    pool.wait_ge(dl_i, 7)
                    pool.affine_select(out=LSEL[:, :, :].rearrange("p i (a n) -> p i a n", a=2),
                                       in_=LSEL[:, :, :].rearrange("p i (a n) -> p i a n", a=2),
                                       compare_op=ALU.not_equal, fill=1.0, base=0,
                                       pattern=[[-2, HEADS], [-1, 2], [0, 64]], channel_multiplier=1).then_inc(dl_mk, 1)
                with pool.Fori(0, st.n) as i:
                    for b in sorted(st.inc):
                        pool.wait_ge(hi_ready, h_of(st, i, b) + 1)
                        pool.wait_ge(unit_done, h_of(st, i, b) - 3)
                        pool.tensor_tensor(WS[:, 1, b % RING, 0:st.kt, :], WR[:, b % RING, 0:st.kt, :],
                                           WS[:, 0, b % RING, 0:st.kt, :].bitcast(F32), ALU.subtract)\
                            .then_inc(lo_ready, st.inc[b])
                before = st

        @block.scalar
        def _(act):
            act.sem_inc(hi_ready, RING)
            rows = [(0, 0, a["norm_w"].rearrange("l n (k p) -> (l n k) p", p=P)),
                    (0, 64, a["conv_w"].rearrange("l j (k p) -> (l j k) p", p=P)),
                    (0, 88, a["ml_norm_w"].rearrange("l (k p) -> (l k) p", p=P)),
                    (0, 96, a["c"].rearrange("l (k p) -> (l k) p", p=P)),
                    (0, 104, a["c_ctx"].rearrange("(k p) -> k p", p=P)),
                    (0, 112, a["diff_subln_2"]),
                    (1, 0, a["mod_b"].rearrange("l (k p) -> (l k) p", p=P)),
                    (2, 0, a["ln_g_2"].rearrange("l n (k p) -> (l n k) p", p=P)),
                    (2, 48, a["ln_b_2"].rearrange("l n (k p) -> (l n k) p", p=P))]
            for l in range(2):
                rows.append((3 + l, 0, a["ffn_conv_w_2"][l].rearrange("j (k p) -> (j k) p", p=P)))
                rows.append((3 + l, 66, a["ffn_conv_b_2"][l].rearrange("(k p) -> k p", p=P)))
            rows.append((5, 0, a["diff_lambda_2"][0]))
            for blk, r0, src in rows:
                act.dma_start(VR[r0:r0 + src.shape[0], blk, 0:src.shape[1]], src).then_inc(small_in, 16)
            for kind in range(2):
                for r in range(2):
                    act.dma_start(SM[0:8, 2 * kind + r:2 * kind + r + 1],
                                  a["ml_b_if"][0][r:r + 1, 8 * kind:8 * kind + 8].rearrange("r h -> h r"))\
                       .then_inc(small_in, 16)
            act.wait_ge(v_ready, 1)
            act.activation(SV[:, :, :], VT[:, 0, 96:112].rearrange("p (v k) -> p k v", v=2), ACT.Exp, scale=-1.0)\
               .then_inc(sv_exp, 1)
            act_lam(act)
            def act_mod0():
                act_mod(act, 0, S["mod0"], 1, 6)
                act_first(act, S["conv"])

            def act_mod1():
                act_mod(act, 1, S["mod1"], 4, 6)
                act_first(act, S["mlstm"])

            act_mod(act, 0, S["mod0"], 0, 1)
            act_prenorm(act, N["n0"], GXC, N["x0"], True, 0, act_mod0)
            act_conv(act)
            act_ysq(act, S["conv_out"], N["r0"], True, TA)
            act_stat(act, N["r0"][1], GXC, EPS)
            act_prenorm(act, N["n1"], GXC, N["r0"][2], False, 1)
            act_mlp0(act)
            act_stat(act, N["r1"][1], GXC, EPS)
            act.wait_ge(wif_zero, 1)
            for r in range(2):
                for kind in range(2):
                    q = 2 * kind + r
                    act.dma_start(WIF[:, :, 32 * q:32 * q + 8],
                                  a["ml_w_if"][0, r].rearrange("(k p) g -> p k g", p=P)[:, :, 8 * kind:8 * kind + 8])\
                       .then_inc(wif_in, 16)
            act_mod(act, 1, S["mod1"], 0, 4)
            act_prenorm(act, N["n2"], GXC, N["r1"][2], False, None, act_mod1)
            act_mlstm(act)
            act_ysq(act, S["mlstm_out"], N["r2"], True, TX)
            act_stat(act, N["r2"][1], GX, EPS)
            act_prenorm(act, N["n3"], GX, N["r2"][2], False, 1)
            act_mlp1(act)
            act_stat(act, N["r3"][1], GX, EPS)
            for k in range(KT):
                act_split(act, N["xb"] + k, X_(k, TX), HB[:, 0, k, :])
            act_diff(act)
            for l in range(2):
                if l == 1:
                    act_dil(act)
                act_lnsq(act, S["diff_out" if l == 0 else "dil_out"], N[f"ln{l}0"], True)
                act_ln(act, N[f"ln{l}0"], l, 0, xatt[l][3])
                xatt[l][1](act)
                act_lnsq(act, S[f"xatt{l}_out"], N[f"ln{l}1"], True)
                act_ln(act, N[f"ln{l}1"], l, 1)
                ffn[l][1](act)
                act_ln(act, N[f"ln{l}2"], l, 2)
            act.wait_ge(x_tr, 1)
            for t in range(2):
                act.activation(OTOK[:, t, :], psa[:, 2 * t:2 * t + 2, :].rearrange("p a n -> p (a n)"), ACT.Copy)
            for t in range(2):
                op = act.activation(OTOK[:, 2 + t, :], psl[:, t, :, :].rearrange("p a n -> p (a n)"), ACT.Copy)
            act.drain().then_inc(x_tr, 1)

        @block.tensor
        def _(pe):
            pe.sem_inc(unit_done, RING)
            pe.sem_inc(mod_used, RING)
            pe.sem_inc(mod_taken, 2)
            pe.sem_inc(ml_pv, 2)
            pe.wait_ge(const_ready, 1)
            pe.wait_ge(small_in, 16 * 18)
            for blk, n in enumerate((113, 96, 96, 88, 88)):
                tr = pe.transpose(psl[:, blk // 4, 0, (blk % 4) * P:(blk % 4) * P + n], VR[0:n, blk, :], ident[0:n, 0:n])
            tr = pe.transpose(psl[0:64, 1, 0, P:P + 4], VR[0:4, 5, 0:64], ident[0:4, 0:4])
            tr.then_inc(v_tr, 1)
            pe.wait_ge(x_in, 32)
            for k in range(KT):
                if k >= 2:
                    pe.wait_ge(x_ready, k - 1)
                for t in range(6):
                    tr = pe.transpose(psa[:, 2 * (k % 2) + t // 4, (t % 4) * P:(t % 4) * P + P], XTOK[:, t, k * P:k * P + P],
                                      ident[:])
                tr.then_inc(x_tr_k, 1)
            pe_lam(pe)
            pe.wait_ge(sv_ready, 1)
            pe.wait_ge(x_ready, KT)
            pe_mod(pe, 0, S["mod0"], 0, 1)
            pe_stat_squares(pe, N["n0"], GXC)
            pe_mod(pe, 0, S["mod0"], 1, 6)
            pe_dense(pe, S["conv"], HA, N["n0"][2])
            pe_dense(pe, S["conv_out"], GA, N["conv"])
            pe_stat(pe, N["r0"][1], GXC, ACC)
            pe_stat_squares(pe, N["n1"], GXC)
            pe_mlp0(pe)
            pe_stat(pe, N["r1"][1], GXC, ACC)
            pe.wait_ge(rstd_ready, N["r1"][1] + 1)
            pe_mod(pe, 1, S["mod1"], 0, 4)
            pe_stat_squares(pe, N["n2"], GXC)
            pe_mod(pe, 1, S["mod1"], 4, 6)
            pe_mlstm(pe)
            pe_dense(pe, S["mlstm_out"], G1, N["mlstm"])
            pe_stat(pe, N["r2"][1], GX, ACC)
            pe_stat_squares(pe, N["n3"], GX)
            pe_mlp1(pe)
            pe_stat(pe, N["r3"][1], GX, ACC)
            pe_diff(pe)
            for l in range(2):
                if l == 1:
                    pe_dil(pe)
                pe_dense(pe, S["diff_out" if l == 0 else "dil_out"], GB if l == 0 else HB, N[f"mix{l}"])
                pe_ln(pe, N[f"ln{l}0"])
                xatt[l][0](pe)
                pe_dense(pe, S[f"xatt{l}_out"], GB, N[f"xatt{l}"])
                pe_ln(pe, N[f"ln{l}1"])
                ffn[l][0](pe)
                pe_ln(pe, N[f"ln{l}2"])
            pe.wait_ge(x_ready, N["x_end"] + 8)
            for t in range(4):
                for k in range(KT):
                    dst = psa[:, 2 * t + k // 4, :] if t < 2 else psl[:, t - 2, k // 4, :]
                    tr = pe.transpose(dst[:, (k % 4) * P:(k % 4) * P + P], X[:, k, t * P:t * P + P], ident[:])
            tr.then_inc(x_tr, 1)

        @block.vector
        def _(dve):
            dve.sem_inc(evac_done, RING)
            dve.sem_inc(dl_q, 1)
            dve.wait_ge(v_tr, 1)
            for blk, n in enumerate((113, 96, 96, 88, 88)):
                op = dve.tensor_copy(VT[:, blk, 0:n], psl[:, blk // 4, 0, (blk % 4) * P:(blk % 4) * P + n])
            op.then_inc(v_ready, 1)
            dve.tensor_copy(SM[0:64, 24:28], psl[0:64, 1, 0, P:P + 4])
            dve.drain()
            dve.tensor_tensor(SM[0:64, 28:30], SM[0:64, 24:28:2], SM[0:64, 25:28:2], ALU.mult).then_inc(lam_b, 1)
            for k in range(KT):
                dve.wait_ge(x_tr_k, k + 1)
                dve.tensor_copy(X[:, k, 0:TX], psa[:, 2 * (k % 2), :])
                dve.tensor_copy(X[:, k, TX:TA], psa[:, 2 * (k % 2) + 1, 0:TC]).then_inc(x_ready, 1)
            dve.wait_ge(sv_exp, 1)
            dve.tensor_scalar(SV[:, :, :], SV[:, :, :], 1.0, None, ALU.add)
            dve.drain()
            dve.reciprocal(SV[:, :, :], SV[:, :, :])
            dve.drain()
            dve.tensor_tensor(SV[:, :, :], SV[:, :, :], VT[:, 0, 96:112].rearrange("p (v k) -> p k v", v=2), ALU.mult)\
               .then_inc(sv_ready, 1)
            dve_prenorm(dve, N["n0"], GXC, 0, lambda: dve_mod(dve, 0, S["mod0"]))
            dve_conv(dve)
            dve_zero_acc(dve, TA)
            dve_y(dve, S["conv_out"], N["r0"], True, True, TA)
            dve_residual(dve, N["r0"], GXC, 0)
            dve_prenorm(dve, N["n1"], GXC, 1)
            dve_mlp0(dve)
            dve_residual(dve, N["r1"], GXC, 1)
            dve.memset(WIF[:, :, :], 0.0).then_inc(wif_zero, 1)
            dve_prenorm(dve, N["n2"], GXC, 0, lambda: dve_mod(dve, 1, S["mod1"]), whole=True)
            dve_mlstm(dve)
            dve_zero_acc(dve, TX)
            dve_y(dve, S["mlstm_out"], N["r2"], True, True, TX)
            dve_residual(dve, N["r2"], GX, 0)
            dve_prenorm(dve, N["n3"], GX, 1)
            dve_mlp1(dve)
            dve_residual(dve, N["r3"], GX, 1, split_ready)
            for k in range(KT):
                dve_split(dve, N["xb"] + k, X_(k, TX), HB[:, 0, k, :], HB[:, 1, k, :])
            dve_diff(dve)
            for l in range(2):
                if l == 1:
                    dve_dil(dve)
                dve_lnx(dve, S["diff_out" if l == 0 else "dil_out"], N[f"ln{l}0"], True, True)
                dve_ln(dve, N[f"ln{l}0"], xatt[l][4])
                xatt[l][2](dve)
                dve_lnx(dve, S[f"xatt{l}_out"], N[f"ln{l}1"], True, True)
                dve_ln(dve, N[f"ln{l}1"])
                ffn[l][2](dve)
                dve_ln(dve, N[f"ln{l}2"])


_INS = ["x", "c", "ctx", "c_ctx", "norm_w", "mod_w", "mod_b", "mlp_w1", "mlp_w2", "conv_w_in", "conv_w", "conv_w_out",
        "ml_w_qkvo", "ml_w_if", "ml_b_if", "ml_norm_w", "ml_w_out", "mem_2", "diff_w_qkv_2", "diff_lambda_2",
        "diff_subln_2", "diff_w_o_2", "dil_w_qkv_2", "dil_w_o_2", "xatt_w_q_2", "xatt_w_kv_2", "xatt_w_o_2",
        "ffn_w_in_2", "ffn_conv_w_2", "ffn_conv_b_2", "ffn_w_out_2", "ln_g_2", "ln_b_2"]


def kernel(**inputs):
    import numpy as _np
    import concourse.bacc as _bacc
    from concourse import mybir as _mybir
    from concourse.bass_utils import run_bass_kernel_spmd as _run

    nc = _bacc.Bacc("TRN2", target_bir_lowering=False, num_devices=1)
    arrays, aps = {}, {}
    for name in _INS:
        arr = _np.ascontiguousarray(inputs[name])
        arrays[f"in_{name}_dram"] = arr
        aps[name] = nc.dram_tensor(f"in_{name}_dram", arr.shape, _mybir.dt.from_np(arr.dtype), kind="ExternalInput").ap()
    out = nc.dram_tensor("out_0_dram", (1, TX, D), F32, kind="ExternalOutput").ap()
    build(nc, aps, out)
    r = _run(nc, [arrays], core_ids=[0])
    return r.results[0]["out_0_dram"]
```
